# Optimizing a Trainium2 kernel written in Bass

```python
import math
import jax, jax.numpy as jnp
from jax import lax
import numpy as np

D_MODEL = 2048
BATCH = 1
SEQ = 256
DEPTH = 1

CHUNK = 64
MIX_WIDTH = D_MODEL
RWKV_WIDTH = MIX_WIDTH // 2
RWKV_HEAD = 64
RWKV_HEADS = RWKV_WIDTH // RWKV_HEAD
DECAY_LORA = max(32, int(round(1.8 * RWKV_WIDTH ** 0.5 / 32)) * 32)
ICL_LORA = max(32, int(round(1.8 * RWKV_WIDTH ** 0.5 / 32)) * 32)
GATE_LORA = max(32, int(round(0.6 * RWKV_WIDTH ** 0.8 / 32)) * 32)
DECAY_SCALE = math.exp(-0.5)
GN_EPS = 64e-5
SWA_WIDTH = MIX_WIDTH - RWKV_WIDTH
SWA_HEAD = 64
SWA_Q_HEADS = SWA_WIDTH // SWA_HEAD
SWA_KV_HEADS = 4
SWA_GROUP = SWA_Q_HEADS // SWA_KV_HEADS
WINDOW = 128
WINDOW_CHUNKS = WINDOW // CHUNK
ROPE_THETA = 500000.0
ROT_DIM = SWA_HEAD // 4
NEG_INF = -1e30
MEM_LEN = 256
X_HEADS = 4
X_HEAD = D_MODEL // X_HEADS
D_FF = int(round(8 * D_MODEL / 3 / 256)) * 256
CONV_WIDTH = 3
RMS_EPS = 1e-6
N_RWKV_IN = 3 * RWKV_WIDTH + DECAY_LORA + ICL_LORA + GATE_LORA
N_SWA_IN = (SWA_Q_HEADS + 2 * SWA_KV_HEADS) * SWA_HEAD
N_IN = N_RWKV_IN + N_SWA_IN

kernel_name = 'hybrid_rwkv7_swa_sink_stream_block'

def rms_norm(x, gain):
    xf = x.astype(jnp.float32)
    y = xf * lax.rsqrt(jnp.mean(xf * xf, axis=-1, keepdims=True) + RMS_EPS)
    return (y * gain.astype(jnp.float32)).astype(x.dtype)

def rope_tables(positions):
    inv_freq = ROPE_THETA ** (-jnp.arange(0, ROT_DIM, 2, dtype=jnp.float32) / ROT_DIM)
    ang = positions.astype(jnp.float32)[..., None] * inv_freq
    return jnp.cos(ang)[:, :, None, :], jnp.sin(ang)[:, :, None, :]

def partial_rope(t, cos, sin):
    half = ROT_DIM // 2
    tf = t.astype(jnp.float32)
    t1, t2, rest = tf[..., :half], tf[..., half:ROT_DIM], tf[..., ROT_DIM:]
    out = jnp.concatenate([t1 * cos - t2 * sin, t2 * cos + t1 * sin, rest], axis=-1)
    return out.astype(t.dtype)

def token_shift(z):
    return jnp.pad(z, ((0, 0), (1, 0), (0, 0)))[:, :-1]

def rwkv7_time_mix(z, mu, w0, w_lora_up, a0, a_lora_up, g_lora_up, k_k, k_a, r_k, ln_w, ln_b):
    B, T, _ = z.shape
    dt = z.dtype
    z = (z + (token_shift(z) - z) * mu).astype(jnp.float32)
    C = RWKV_WIDTH
    r, k, v = z[..., :C], z[..., C:2 * C], z[..., 2 * C:3 * C]
    o = 3 * C
    wd = z[..., o:o + DECAY_LORA]
    o += DECAY_LORA
    ad = z[..., o:o + ICL_LORA]
    o += ICL_LORA
    gd = z[..., o:o + GATE_LORA]
    log_decay = -DECAY_SCALE * jax.nn.sigmoid(w0 + jnp.tanh(wd) @ w_lora_up)
    a = jax.nn.sigmoid(a0 + ad @ a_lora_up)
    g = jax.nn.sigmoid(gd) @ g_lora_up

    def heads(t):
        return t.reshape(B, T, RWKV_HEADS, RWKV_HEAD)

    kk = heads(k * k_k)
    kk = kk / jnp.maximum(jnp.sqrt(jnp.sum(kk * kk, axis=-1, keepdims=True)), 1e-12)
    k = heads(k * (1.0 + (a - 1.0) * k_a))
    r, v, a, decay = heads(r), heads(v), heads(a), heads(jnp.exp(log_decay))

    def step(state, inp):
        r_t, dec_t, k_t, v_t, kk_t, a_t = inp
        sa = jnp.einsum('bhvk,bhk->bhv', state, kk_t)
        state = (state * dec_t[:, :, None, :]
                 - sa[..., None] * (kk_t * a_t)[:, :, None, :]
                 + v_t[..., None] * k_t[:, :, None, :])
        return state, jnp.einsum('bhvk,bhk->bhv', state, r_t)

    xs = tuple(jnp.moveaxis(t, 1, 0) for t in (r, decay, k, v, kk, a))
    s0 = jnp.zeros((B, RWKV_HEADS, RWKV_HEAD, RWKV_HEAD), jnp.float32)
    _, y = lax.scan(step, s0, xs)
    y = jnp.moveaxis(y, 0, 1)
    mean = jnp.mean(y, axis=-1, keepdims=True)
    var = jnp.mean(jnp.square(y - mean), axis=-1, keepdims=True)
    y = ((y - mean) * lax.rsqrt(var + GN_EPS)).reshape(B, T, C) * ln_w + ln_b
    bonus = jnp.sum(r * k * r_k, axis=-1, keepdims=True) * v
    y = (y + bonus.reshape(B, T, C)) * g
    return y.astype(dt)

def band(t, n_chunks):
    parts = [jnp.pad(t, ((0, 0), (j, 0), (0, 0), (0, 0), (0, 0)))[:, :n_chunks]
             for j in range(WINDOW_CHUNKS - 1, -1, -1)]
    return jnp.concatenate(parts, axis=2)

def swa_sink_attention(z, cos, sin, sinks):
    B, T, _ = z.shape
    nq = SWA_Q_HEADS * SWA_HEAD
    nkv = SWA_KV_HEADS * SWA_HEAD
    q = partial_rope(z[..., :nq].reshape(B, T, SWA_Q_HEADS, SWA_HEAD), cos, sin)
    k = partial_rope(z[..., nq:nq + nkv].reshape(B, T, SWA_KV_HEADS, SWA_HEAD), cos, sin)
    v = z[..., nq + nkv:].reshape(B, T, SWA_KV_HEADS, SWA_HEAD)
    nC = T // CHUNK
    qb = q.reshape(B, nC, CHUNK, SWA_KV_HEADS, SWA_GROUP, SWA_HEAD)
    kb = band(k.reshape(B, nC, CHUNK, SWA_KV_HEADS, SWA_HEAD), nC)
    vb = band(v.reshape(B, nC, CHUNK, SWA_KV_HEADS, SWA_HEAD), nC)
    s = jnp.einsum('bcqhgd,bckhd->bhgcqk', qb, kb).astype(jnp.float32) / math.sqrt(SWA_HEAD)
    back = (WINDOW_CHUNKS - 1) - jnp.arange(WINDOW_CHUNKS * CHUNK) // CHUNK
    valid = jnp.arange(nC)[:, None] >= back[None, :]
    s = jnp.where(valid[:, None, :], s, NEG_INF)
    sink = sinks.astype(jnp.float32).reshape(SWA_KV_HEADS, SWA_GROUP)[None, :, :, None, None, None]
    sink = jnp.broadcast_to(sink, s.shape[:-1] + (1,))
    p = jax.nn.softmax(jnp.concatenate([s, sink], axis=-1), axis=-1)[..., :-1]
    o = jnp.einsum('bhgcqk,bckhd->bcqhgd', p.astype(vb.dtype), vb)
    return o.reshape(B, T, SWA_WIDTH)

def memory_cross_attention(h, mem_n, wq, wk, wv, wo):
    B, T, _ = h.shape
    q = (h @ wq).reshape(B, T, X_HEADS, X_HEAD)
    k = (mem_n @ wk).reshape(B, -1, X_HEADS, X_HEAD)
    v = (mem_n @ wv).reshape(B, -1, X_HEADS, X_HEAD)
    s = jnp.einsum('bthd,bmhd->bhtm', q, k).astype(jnp.float32) / math.sqrt(X_HEAD)
    p = jax.nn.softmax(s, axis=-1).astype(v.dtype)
    o = jnp.einsum('bhtm,bmhd->bthd', p, v).reshape(B, T, D_MODEL)
    return o @ wo

def conv_glu(h, w_up, conv_w, conv_b, w_down):
    T = h.shape[1]
    u = h @ w_up
    gate, val = u[..., :D_FF], u[..., D_FF:]
    gp = jnp.pad(gate, ((0, 0), (CONV_WIDTH - 1, 0), (0, 0)))
    conv = conv_b
    for i in range(CONV_WIDTH):
        conv = conv + gp[:, i:i + T] * conv_w[i]
    return (jax.nn.gelu(conv, approximate=False) * val) @ w_down

def setup_inputs(seed: int = 0) -> dict:
    key = jax.random.key(seed)
    ks = jax.random.split(key, 32)
    L, D = DEPTH, D_MODEL

    def nrm(k, shape, scale):
        return scale * jax.random.normal(k, shape, jnp.float32)

    def gain(k, n):
        return 1.0 + nrm(k, (L, n), 0.02)

    offsets = jax.random.randint(ks[2], (BATCH, 1), 0, 1024, dtype=jnp.int32) * CHUNK
    positions = (offsets + jnp.arange(SEQ, dtype=jnp.int32)[None, :]).astype(jnp.int32)
    return {
        'x': nrm(ks[0], (BATCH, SEQ, D), 1.0),
        'mem': nrm(ks[1], (BATCH, MEM_LEN, D), 1.0),
        'positions': positions,
        'norm_mix_pre': gain(ks[3], D),
        'norm_mix_post': gain(ks[4], D),
        'w_in': nrm(ks[5], (L, D, N_IN), D ** -0.5),
        'shift_mu': jax.random.uniform(ks[6], (L, N_RWKV_IN), jnp.float32),
        'w0': nrm(ks[7], (L, RWKV_WIDTH), 1.0),
        'w_lora_up': nrm(ks[8], (L, DECAY_LORA, RWKV_WIDTH), 0.5 * DECAY_LORA ** -0.5),
        'a0': nrm(ks[9], (L, RWKV_WIDTH), 0.5),
        'a_lora_up': nrm(ks[10], (L, ICL_LORA, RWKV_WIDTH), 0.5 * ICL_LORA ** -0.5),
        'g_lora_up': nrm(ks[11], (L, GATE_LORA, RWKV_WIDTH), GATE_LORA ** -0.5),
        'k_k': 0.85 + nrm(ks[12], (L, RWKV_WIDTH), 0.05),
        'k_a': 1.0 + nrm(ks[13], (L, RWKV_WIDTH), 0.05),
        'r_k': nrm(ks[14], (L, RWKV_HEADS, RWKV_HEAD), 0.1),
        'ln_x_w': gain(ks[15], RWKV_WIDTH),
        'ln_x_b': nrm(ks[16], (L, RWKV_WIDTH), 0.02),
        'attn_sinks': nrm(ks[17], (L, SWA_Q_HEADS), 0.5),
        'w_out': nrm(ks[18], (L, MIX_WIDTH, D), MIX_WIDTH ** -0.5),
        'norm_cross_pre': gain(ks[19], D),
        'norm_cross_post': gain(ks[20], D),
        'mem_norm': 1.0 + nrm(ks[21], (D,), 0.02),
        'wq_x': nrm(ks[22], (L, D, D), D ** -0.5),
        'wk_x': nrm(ks[23], (L, D, D), D ** -0.5),
        'wv_x': nrm(ks[24], (L, D, D), D ** -0.5),
        'wo_x': nrm(ks[25], (L, D, D), D ** -0.5),
        'norm_ffn_pre': gain(ks[26], D),
        'norm_ffn_post': gain(ks[27], D),
        'w_up': nrm(ks[28], (L, D, 2 * D_FF), D ** -0.5),
        'conv_w': nrm(ks[29], (L, CONV_WIDTH, D_FF), CONV_WIDTH ** -0.5),
        'conv_b': nrm(ks[30], (L, D_FF), 0.02),
        'w_down': nrm(ks[31], (L, D_FF, D), D_FF ** -0.5),
    }

def reference(x, mem, positions, norm_mix_pre, norm_mix_post, w_in, shift_mu, w0, w_lora_up,
              a0, a_lora_up, g_lora_up, k_k, k_a, r_k, ln_x_w, ln_x_b, attn_sinks, w_out,
              norm_cross_pre, norm_cross_post, mem_norm, wq_x, wk_x, wv_x, wo_x,
              norm_ffn_pre, norm_ffn_post, w_up, conv_w, conv_b, w_down):
    cos, sin = rope_tables(positions)
    mem_n = rms_norm(mem, mem_norm)
    for l in range(DEPTH):
        h = rms_norm(x, norm_mix_pre[l])
        z = h @ w_in[l]
        y_a = rwkv7_time_mix(z[..., :N_RWKV_IN], shift_mu[l], w0[l], w_lora_up[l], a0[l],
                             a_lora_up[l], g_lora_up[l], k_k[l], k_a[l], r_k[l],
                             ln_x_w[l], ln_x_b[l])
        y_b = swa_sink_attention(z[..., N_RWKV_IN:], cos, sin, attn_sinks[l])
        y = jnp.concatenate([y_a, y_b], axis=-1) @ w_out[l]
        x = x + rms_norm(y, norm_mix_post[l])
        h = rms_norm(x, norm_cross_pre[l])
        y = memory_cross_attention(h, mem_n, wq_x[l], wk_x[l], wv_x[l], wo_x[l])
        x = x + rms_norm(y, norm_cross_post[l])
        h = rms_norm(x, norm_ffn_pre[l])
        y = conv_glu(h, w_up[l], conv_w[l], conv_b[l], w_down[l])
        x = x + rms_norm(y, norm_ffn_post[l])
    return x


_drawn_inputs = setup_inputs


def setup_inputs(seed=0):
    import zlib

    import numpy as np

    out = dict(_drawn_inputs(seed))
    spreads = {}
    factors = {'norm_mix_post': 3.6,
     'k_k': 5.788,
     'ln_x_w': 3.786,
     'ln_x_b': 3.915,
     'attn_sinks': 8.0,
     'norm_cross_pre': 4.529,
     'norm_cross_post': 13.538,
     'mem_norm': 2.901,
     'norm_ffn_pre': 11.917,
     'norm_ffn_post': 22.801,
     'conv_b': 15.786}
    for name, (base, spread) in spreads.items():
        noise = np.random.default_rng([zlib.crc32(name.encode()), seed]).standard_normal(out[name].shape)
        drawn = base * np.exp(spread * noise) if base else spread * noise
        out[name] = __import__('jax').numpy.asarray(drawn.astype(out[name].dtype))
    for name, factor in factors.items():
        out[name] = (out[name] * factor).astype(out[name].dtype)
    return out
```

```python
import math
import concourse.bass as bass
from concourse import mybir
from contextlib import ExitStack

F32, F32R, I32 = mybir.dt.float32, mybir.dt.float32r, mybir.dt.int32
ALU, ACT, AX = mybir.AluOpType, mybir.ActivationFunctionType, mybir.AxisListType

D, SEQ, MEM, P = 2048, 256, 256, 128
KT = D // P
TT = SEQ // P
CH = 64
NCH = SEQ // CH
RW, HD = 1024, 64
NLORA_W, NLORA_A, NLORA_G = 64, 64, 160
N_RWKV = 3 * RW + NLORA_W + NLORA_A + NLORA_G
N_IN = N_RWKV + 24 * HD
DFF = 5376
FT_FF = DFF // P
XHEADS, XHD = 4, 512
DECAY_SCALE = math.exp(-0.5)
GN_EPS, RMS_EPS = 64e-5, 1e-6
NEG_INF = -1e30
ROT = 16
INV_FREQ = [500000.0 ** (-i / ROT) for i in range(0, ROT, 2)]

B_SWA, B_LORA, B_RKV, B_WK, B_WV, B_OUT, B_WQ, B_WO, B_UP, B_DOWN = 0, 3, 4, 10, 14, 18, 22, 26, 30, 51
N_UP, N_DOWN = 21, 4
HU = 8
Q_DOWN = B_DOWN * HU
HD_DOWN = FT_FF // 2
SLOTS, SLOTS_D, RAW_D = 4, 3, 7
COLS, ROWS = "cols", "rows"


def kind_of(g):
    return COLS if B_LORA <= g < B_WV or B_WQ <= g < B_WO or B_UP <= g < B_DOWN else ROWS


FIRST_OF_FILL = {B_SWA: 0, B_WK: 1, B_OUT: 2, B_WQ: 3, B_WO: 4, B_UP: 5}

LEVELS = (2, 4, 8, 16, 32)


def swa_jobs():
    yield ("swa_kT",)
    for g in range(4):
        yield ("swa_qT", g)
        for j in range(TT):
            for what in ("swa_scores", "swa_pT", "swa_out"):
                yield (what, g, j)


def rwkv_jobs():
    for G in range(4):
        yield ("lora_wa", G)
        yield ("lora_g", G)
        yield ("kk_norm", G)
        yield ("v_rows", G)
        yield ("bk_rows", G)
        yield ("scores", G, 0)
        yield ("scores", G, 1)
        yield ("lower", G)
        for b in LEVELS:
            yield ("inv_p", G, b)
            yield ("inv_x", G, b)
            if b != LEVELS[-1]:
                yield ("inv_t", G, b)
        for c in range(NCH):
            yield ("scan_x", G, c)
            yield ("scan_u", G, c)
            yield ("scan_ys", G, c)
        yield ("gn_mean", G)
        yield ("gn_var", G)


def cross_jobs(h):
    yield ("x_scores", h)
    yield ("x_pT", h)
    yield ("x_out", h)


def spread(jobs, hus):
    jobs, hus = list(jobs), list(hus)
    out, done = [], 0
    for i, job in enumerate(jobs):
        out.append(job)
        upto = (i + 1) * len(hus) // len(jobs)
        out += hus[done:upto]
        done = upto
    return out + hus[done:]


def half_units(g0, g1):
    return [("hu", g, k) for g in range(g0, g1) for k in range(HU)]


def schedule():
    mix = [("params",)] + [("fill", 0, i) for i in range(4)]
    mix += half_units(B_SWA, B_SWA + 1) + [("mem_norm",)]
    mix += half_units(B_SWA + 1, B_LORA)
    mix += spread(swa_jobs(), half_units(B_LORA, B_WK))
    mix += [("fill", 1, i) for i in range(4)]
    mix += spread(rwkv_jobs(), half_units(B_WK, B_OUT))
    mix += [("fill_T", 2, i) for i in range(4)]
    cross = [("fill", 3, i) for i in range(4)] + half_units(B_WQ, B_WQ + 1)
    for h in range(XHEADS):
        jobs = list(cross_jobs(h))
        if h < XHEADS - 1:
            cross += spread(jobs, half_units(B_WQ + h + 1, B_WQ + h + 2))
        else:
            cross += jobs
    cross += [("fill_T", 4, i) for i in range(4)]
    ffn = [("fill", 5, i) for i in range(4)]
    n, out = 0, []
    for part in (mix, cross, ffn):
        steps = []
        for s in part:
            if s[0] in ("hu", "mem_norm", "fill_T"):
                steps.append((None,) + s)
            else:
                steps.append((n,) + s)
                n += 1
        out.append(steps)
    return out


def build(nc, a, out):
    mix_steps, cross_steps, ffn_steps = schedule()
    ctx = ExitStack()
    with ctx:
        base = 16640

        def sb(name, shape, dt, at):
            return nc.alloc_sbuf_tensor_at(name, [P] + list(shape), dt, offset=base + at)

        raw = sb("raw", [4, 4, 512], F32, 0)
        raw_d = sb("raw_d", [RAW_D, 2, 512], F32, 0)
        w_hi = sb("w_hi", [SLOTS, 2, 512], F32R, 32768)
        w_lo = sb("w_lo", [SLOTS, 2, 512], F32R, 49152)
        x_hi = sb("x_hi", [KT, SEQ], F32R, 65536)
        x_lo = sb("x_lo", [KT, SEQ], F32R, 81920)
        at = [98304]

        def const(name, shape, dt=F32):
            n = 4
            for s in shape:
                n *= s
            t = sb(name, shape, dt, at[0])
            at[0] += (n + 31) // 32 * 32
            return t

        colA, colB, colC = const("colA", [P]), const("colB", [P]), const("colC", [P])
        ident, hones = const("ident", [P]), const("hones", [P])
        mask_sc, mask_low = const("mask_sc", [2, CH]), const("mask_low", [CH])
        lvl_x, lvl_t = const("lvl_x", [6, CH]), const("lvl_t", [5, CH])
        eye = const("eye", [CH])
        reset = const("reset", [SEQ])
        trig = const("trig", [2, TT, 8])
        sink = const("sink", [16])
        ssq = const("ssq", [TT, 4])
        stat = const("stat", [8, TT])
        soft = const("soft", [6, 4])
        assert at[0] <= 106496, at
        R = 106496

        y_T = sb("y_T", [KT, SEQ], F32, R)
        rkv = sb("rkv", [24, SEQ], F32, R + 16384)
        junk = sb("junk", [D], F32, R + 16384)
        lora = sb("lora", [3, SEQ], F32, R + 40960)
        lora_w = sb("lora_w", [3, 2 * P], F32, R + 44032)
        stage = sb("stage", [2, 4, SEQ + 1], F32, R + 47104)
        fill_tmp = sb("fill_tmp", [2, 4, SEQ], F32, R + 47104)
        pack = sb("pack", [3, P], F32, R + 47104)
        pos_i = sb("pos_i", [P], I32, R + 47104 + 1536)
        ang = sb("ang", [6, TT, 8], F32, R + 47104 + 2048)
        S = R + 55360
        rows0 = sb("rows0", [TT, D], F32, S)
        zq = sb("zq", [TT, 24, HD], F32, S + 16384)
        q_T = sb("q_T", [2, 2, SEQ], F32, S + 28672)
        k_T = sb("k_T", [4, SEQ], F32, S + 32768)
        v_win = sb("v_win", [NCH, 4, HD], F32, S + 36864)
        prob = sb("prob", [2, 4, P], F32, S + 40960)
        rope = sb("rope", [4, 20, 8], F32, S + 40960)
        prob_T = sb("prob_T", [2, 4, P], F32, S + 45056)
        k_dup = sb("k_dup", [TT, 4, 2, HD], F32, S + 45056)
        kr = sb("kr", [2, NCH, 2, CH], F32, S)
        bk = sb("bk", [2, NCH, 2, CH], F32, S + 4096)
        bk_rows = sb("bk_rows", [2, NCH, P], F32, S + 8192)
        uv = sb("uv", [NCH, 4, HD], F32, S + 12288)
        mx = sb("mx", [2, 2, 2, 2, 2 * CH], F32, S + 16384)
        low = sb("low", [2, 2, 2, CH], F32, S + 24576)
        inv_t = sb("inv_t", [2, 2, 2, CH], F32, S + 26624)
        inv_x = sb("inv_x", [2, 2, 2, CH], F32, S + 28672)
        inv_p = sb("inv_p", [2, 2, 2, CH], F32, S + 30720)
        state = sb("state", [2, HD], F32, S + 32768)
        xs = sb("xs", [4, HD], F32, S + 33280)
        sl = [sb(f"sl{i}", [2, SEQ], F32, S + 34304 + 2048 * i) for i in range(8)]
        y_rows = sb("y_rows", [TT, D], F32, R + 16384)
        x_res = sb("x_res", [TT, D], F32, R + 32768)
        kx = sb("kx", [KT, MEM], F32, R + 49152)
        vx = sb("vx", [TT, 4, 512], F32, R + 65536)
        g_post = sb("g_post", [D], F32, R + 81920)
        xp = sb("xp", [2, TT, MEM], F32, R + 90112)
        xp_T = sb("xp_T", [2, TT, SEQ], F32, R + 94208)
        xfill = sb("xfill", [2, 4, SEQ], F32, R)
        act_hi = sb("act_hi", [FT_FF, SEQ], F32R, R)
        act_lo = sb("act_lo", [FT_FF, SEQ], F32R, R + 43008)
        F = R + 86016
        gate = sb("gate", [2, 2, SEQ + 2], F32, F)
        conv = sb("conv", [2, 2, SEQ], F32, F + 4128)
        gelu = sb("gelu", [2, 2, SEQ], F32, F + 8224)
        act32 = sb("act32", [2, 2, SEQ], F32, F + 12320)
        ffill = sb("ffill", [2, 4, SEQ], F32, F)
        y_fin = sb("y_fin", [TT, D], F32, 65536)
        x_fin = sb("x_fin", [TT, D], F32, 81920)
        g_fin = sb("g_fin", [D], F32, F)

        acc = [ctx.enter_context(nc.psum_tensor(f"acc{i}", [P, 1024], F32)) for i in range(2)]
        js = [ctx.enter_context(nc.psum_tensor(f"job{i}", [P, 1024], F32)) for i in range(2)]
        kx_d = nc.dram_tensor("kx_scratch", (4, P, 1024), F32, kind="Internal").ap()
        vx_d = nc.dram_tensor("vx_scratch", (4, P, 1024), F32, kind="Internal").ap()

        sems = {}

        def S_(name):
            if name not in sems:
                sems[name] = ctx.enter_context(nc.semaphore(name))
            return sems[name]

        raw_loaded = [S_(f"raw_loaded{j}") for j in range(4)]
        rawd_loaded = [S_(f"rawd_loaded{j}") for j in range(RAW_D)]
        hi_ready, lo_ready, used = S_("hi_ready"), S_("lo_ready"), S_("used")
        evac_done = S_("evac_done")
        job_full, job_free = [S_("job_full0"), S_("job_full1")], [S_("job_free0"), S_("job_free1")]
        xh_ready, xl_ready = S_("xh_ready"), S_("xl_ready")
        kv_stored = [S_("kv_stored0"), S_("kv_stored1")]
        JOB = {tuple(s): n for steps in (mix_steps, cross_steps, ffn_steps) for n, *s in steps if n is not None}
        FREE_AT = {0: 0, 1: B_WK, 2: B_OUT, 3: B_WQ, 4: B_WO, 5: B_UP}

        def fill_buf(f, i):
            return (fill_tmp if f < 2 else xfill if f == 3 else ffill)[:, i % 2]

        def produced(eng, *step):
            n = JOB[step]
            eng.wait_ge(job_full[n % 2], n // 2 + 1)

        def consumed(eng, *step):
            n = JOB[step]
            eng.wait_ge(job_free[n % 2], n // 2 + 1)

        G_COL = {0: 0, 1: 16, 3: 32, 5: 48}
        C_W0, C_A0, C_KK, C_KA, C_RK, C_LNW, C_LNB = (64 + 8 * i for i in range(7))
        CB_MU, CB_CB, CB_POS = 0, 27, 96
        block = ctx.enter_context(nc.Block())

        def job_wait_full(eng, n):
            eng.wait_ge(job_full[n % 2], n // 2 + 1)
            return js[n % 2]

        def half(c):
            return slice(64, 128) if c % 2 == 0 else slice(0, 64)

        def b_part(c):
            return 1 if c % 2 == 0 else 0

        @block.sync
        def _(sp):
            xv = a["x"].rearrange("b (t p) d -> p (b t) d", p=P)
            for j in range(TT):
                sp.dma_start(rows0[:, j], xv[:, j]).then_inc(S_("x_loaded"), 16)

            w_in = a["w_in"]
            src = {}
            for i in range(3):
                src[B_SWA + i] = (w_in, N_RWKV + 512 * i, 512)
            src[B_LORA] = (w_in, 3 * RW, NLORA_W + NLORA_A + NLORA_G)
            for i in range(6):
                src[B_RKV + i] = (w_in, 512 * i, 512)
            for i in range(4):
                src[B_WK + i] = (a["wk_x"], 512 * i, 512)
                src[B_WV + i] = (a["wv_x"], 512 * i, 512)
                src[B_WQ + i] = (a["wq_x"], 512 * i, 512)

            def load(g, j, w, c0, n):
                if not (isinstance(g, int) and g == 0):
                    sp.wait_ge(lo_ready, g * HU + (2 * j + 2 - HU))
                sp.dma_start(raw[:, j, :, 0:n],
                             w[0, j * 512:(j + 1) * 512, bass.ds(c0, n)].rearrange("(k p) n -> p k n", p=P)
                             ).then_inc(raw_loaded[j], 16)

            for g in range(B_OUT):
                for j in range(4):
                    load(g, j, *src[g])
            for g0, w in ((B_OUT, a["w_out"]), (B_WQ, a["wq_x"]), (B_WO, a["wo_x"])):
                with sp.Fori(0, 4) as b:
                    for j in range(4):
                        load(b + g0, j, w, b * 512, 512)
            with sp.Fori(0, N_UP) as b:
                for j in range(4):
                    sp.wait_ge(lo_ready, (b + B_UP) * HU + (2 * j + 2 - HU))
                    for part in range(2):
                        sp.dma_start(raw[:, j, :, part * 256:part * 256 + 256],
                                     a["w_up"][0, j * 512:(j + 1) * 512, bass.ds(b * 256 + part * DFF, 256)]
                                     .rearrange("(k p) n -> p k n", p=P)).then_inc(raw_loaded[j], 16)

            def load_down(b, k, first):
                if first:
                    sp.wait_ge(lo_ready, Q_DOWN)
                else:
                    sp.wait_ge(lo_ready, b * HD_DOWN + (Q_DOWN + k - RAW_D + 1))
                sp.dma_start(raw_d[:, k % RAW_D],
                             a["w_down"][0, k * 256:(k + 1) * 256, bass.ds(b * 512, 512)]
                             .rearrange("(k p) n -> p k n", p=P)).then_inc(rawd_loaded[k % RAW_D], 16)

            for k in range(HD_DOWN):
                load_down(0, k, k < RAW_D)
            with sp.Fori(1, N_DOWN) as b:
                for k in range(HD_DOWN):
                    load_down(b, k, False)
            ov = out.rearrange("b (t p) d -> p (b t) d", p=P)
            for j in range(TT):
                sp.wait_ge(S_("result"), j + 1)
                sp.dma_start(ov[:, j], x_fin[:, j]).then_inc(S_("result_stored"), 16)
            sp.wait_ge(S_("result_stored"), 16 * TT)

        @block.gpsimd
        def _(pool):
            nc.gpsimd.memset(pack[:], 0.0).then_inc(S_("pack_zero"), 1)
            pool.wait_ge(S_("pack_zero"), 1)

            def vec(name, rows, t, row):
                pool.dma_start(pack[row:row + rows, t, :],
                               a[name].rearrange("l (f p) -> (l f) p", p=P)).then_inc(S_("pack_loaded"), 16)

            n = 0
            for f, name in ((0, "norm_mix_pre"), (3, "norm_cross_pre"), (5, "norm_ffn_pre")):
                vec(name, 16, 0, G_COL[f])
                n += 1
            pool.dma_start(pack[16:32, 0, :], a["mem_norm"].rearrange("(f p) -> f p", p=P)).then_inc(S_("pack_loaded"), 16)
            for name, c in (("w0", C_W0), ("a0", C_A0), ("k_k", C_KK), ("k_a", C_KA), ("ln_x_w", C_LNW), ("ln_x_b", C_LNB)):
                vec(name, 8, 0, c)
                n += 1
            pool.dma_start(pack[C_RK:C_RK + 8, 0, :], a["r_k"].rearrange("l (f h) d -> (l f) (h d)", h=2)).then_inc(S_("pack_loaded"), 16)
            pool.dma_start(pack[0:26, 1, :], a["shift_mu"][:, 0:26 * P].rearrange("l (f p) -> (l f) p", p=P)).then_inc(S_("pack_loaded"), 16)
            pool.dma_start(pack[26:27, 1, 0:32], a["shift_mu"][:, 26 * P:26 * P + 32]).then_inc(S_("pack_loaded"), 16)
            vec("conv_b", FT_FF, 1, CB_CB)
            pool.dma_start(pack[0:3 * FT_FF, 2, :], a["conv_w"].rearrange("l w (f p) -> (l w f) p", p=P)).then_inc(S_("pack_loaded"), 16)
            pool.dma_start(pos_i[96:98, :], a["positions"].rearrange("b (t p) -> (b t) p", p=P)).then_inc(S_("pos_loaded"), 16)
            pool.dma_start(sink[:], a["attn_sinks"].partition_broadcast(P).rearrange("q l n -> q (l n)")).then_inc(S_("sink_loaded"), 16)
            n += 6
            assert n * 16 == 15 * 16
            marks = S_("mask_step")
            cnt = [0]

            def mark(ins):
                cnt[0] += 1
                ins.then_inc(marks, 1)
                pool.wait_ge(marks, cnt[0])

            def pick(ap, pattern, op, base_, cm, fill):
                mark(nc.gpsimd.affine_select(out=ap, in_=ap, compare_op=op, fill=fill, base=base_,
                                             pattern=pattern, channel_multiplier=cm))

            mark(nc.gpsimd.memset(ident[:], 0.0))
            pick(ident[:], [[-1, P]], ALU.not_equal, 0, 1, 1.0)
            S_("masks")
            nc.gpsimd.memset(hones[:], 0.0).then_inc(S_("ident_ready"), 1)
            mark(nc.gpsimd.memset(mask_sc[:], 1.0))
            mark(nc.gpsimd.memset(mask_low[:], -1.0))
            mark(nc.gpsimd.memset(lvl_x[:], 0.0))
            mark(nc.gpsimd.memset(lvl_t[:], 0.0))
            mark(nc.gpsimd.memset(eye[:], 0.0))
            for hh in range(2):
                h = slice(64 * hh, 64 * hh + 64)
                mark(nc.gpsimd.memset(hones[h, 64 * hh:64 * hh + 64], 1.0))
                pick(eye[h], [[-1, CH]], ALU.not_equal, 0, 1, 1.0)
                pick(mask_sc[h, 0], [[1, CH]], ALU.is_gt, 0, -1, 0.0)
                pick(mask_sc[h, 1], [[1, CH]], ALU.is_ge, 0, -1, 0.0)
                pick(mask_low[h], [[-1, CH]], ALU.is_gt, 0, 1, 0.0)
                for i in range(6):
                    b = 1 << i
                    n2 = CH // (2 * b)
                    v = lvl_x[h, i].rearrange("p (n h b) -> p n h b", h=2, b=b)[:, :, 1]
                    sgn = -1.0 if i == 0 else 1.0
                    mark(nc.gpsimd.memset(v, sgn))
                    pick(v, [[-2 * b, n2], [0, b]], ALU.is_ge, 0, 1, 0.0)
                    pick(v, [[2 * b, n2], [0, b]], ALU.is_ge, b - 1, -1, 0.0)
                    if i < 5:
                        v = lvl_t[h, i].rearrange("p (n h b) -> p n h b", h=2, b=b)[:, :, 0]
                        mark(nc.gpsimd.memset(v, 1.0))
                        pick(v, [[-2 * b, n2], [0, b]], ALU.is_ge, -b, 1, 0.0)
                        pick(v, [[2 * b, n2], [0, b]], ALU.is_ge, 2 * b - 1, -1, 0.0)
            mark(nc.gpsimd.memset(reset[:], 1.0))
            nc.gpsimd.memset(reset[:].rearrange("p (c t) -> p c t", t=CH)[:, :, 0:1], 0.0).then_inc(S_("masks"), 1)

            pool.wait_ge(job_full[0], 3)
            pool.wait_ge(job_full[1], 2)
            mv = a["mem"].rearrange("b (t p) d -> p (b t) d", p=P)
            for j in range(TT):
                pool.dma_start(rows0[:, j], mv[:, j]).then_inc(S_("mem_loaded"), 16)
            for G in range(4):
                if G:
                    produced(pool, "lora_g", G - 1)
                c = slice(256 * G, 256 * G + 256)
                pool.dma_start(lora_w[0:64, 0], a["w_lora_up"][0, :, c]).then_inc(S_("lora_loaded"), 16)
                pool.dma_start(lora_w[64:128, 0], a["a_lora_up"][0, :, c]).then_inc(S_("lora_loaded"), 16)
                pool.dma_start(lora_w[:, 1], a["g_lora_up"][0, 0:128, c]).then_inc(S_("lora_loaded"), 16)
                pool.dma_start(lora_w[0:32, 2], a["g_lora_up"][0, 128:160, c]).then_inc(S_("lora_loaded"), 16)
            pool.wait_ge(S_("yt_ready"), 4)
            for i in range(2):
                pool.wait_ge(kv_stored[i], 16 * 4)
            xv = a["x"].rearrange("b (t p) d -> p (b t) d", p=P)
            pool.dma_start(x_res[:], xv).then_inc(S_("xres_loaded"), 16)
            pool.dma_start(g_post[:], a["norm_mix_post"][0].partition_broadcast(P)).then_inc(S_("gpost_loaded"), 16)
            for b in range(4):
                pool.dma_start(kx[:, 4 * b:4 * b + 4, :], kx_d[b].rearrange("p (f m) -> p f m", f=4)).then_inc(S_("kv_loaded"), 16)
                pool.dma_start(vx[:, :, b, :], vx_d[b].rearrange("p (t n) -> p t n", t=2)).then_inc(S_("kv_loaded"), 16)
            pool.wait_ge(S_("xres_ready"), TT)
            pool.dma_start(g_post[:], a["norm_cross_post"][0].partition_broadcast(P)).then_inc(S_("gpost_loaded"), 16)
            pool.wait_ge(S_("xres_ready"), 2 * TT)
            pool.dma_start(out.rearrange("b (t p) d -> p (b t) d", p=P), x_res[:]).then_inc(S_("x2_stored"), 16)
            pool.wait_ge(S_("x2_stored"), 16)
            pool.wait_ge(used, Q_DOWN)
            pool.dma_start(x_fin[:], out.rearrange("b (t p) d -> p (b t) d", p=P)).then_inc(S_("x2_loaded"), 16)
            pool.wait_ge(S_("actl_ready"), N_UP)
            pool.dma_start(g_fin[:], a["norm_ffn_post"][0].partition_broadcast(P)).then_inc(S_("gpost_loaded"), 16)

        @block.scalar
        def _(act):
            A = nc.scalar.activation

            def w_high(q, g, k, n=512, up=False):
                j = k // 2
                if up:
                    act.wait_ge(raw_loaded[j], g * 32 + (32 - 16 * B_UP))
                else:
                    act.wait_ge(raw_loaded[j], g * 16 + 16)
                if not (isinstance(q, int) and q < SLOTS):
                    act.wait_ge(used, q + (1 - SLOTS))
                A(w_hi[:, k % SLOTS, :, 0:n], raw[:, j, 2 * (k % 2):2 * (k % 2) + 2, 0:n], ACT.Copy).then_inc(hi_ready, 1)

            def w_high_down(b, m):
                act.wait_ge(rawd_loaded[m % RAW_D], b * 48 + 16 * (m // RAW_D + 1))
                act.wait_ge(used, b * HD_DOWN + (Q_DOWN - 2 + m))
                A(w_hi[:, m % SLOTS_D], raw_d[:, m % RAW_D], ACT.Copy).then_inc(hi_ready, 1)

            def width(g):
                return 288 if g == B_LORA else 512

            def lead(g, k):
                g2, k2 = (g, k + 3) if k + 3 < HU else (g + 1, k + 3 - HU)
                w_high(g2 * HU + k2, g2, k2, width(g2), g2 >= B_UP)

            def rows_out(dst, b, sq):
                par = acc[sq]
                for j in range(TT):
                    A(dst[:, j, bass.ds(b * 512, 512)], par[:, j * 512:j * 512 + 512], ACT.Copy)
                    last = A(par[:, j * 512:j * 512 + 512], par[:, j * 512:j * 512 + 512], ACT.Square,
                             accum_out=ssq[:, j, bass.ds(b, 1)])
                last.then_inc(evac_done, 1)

            def evac(g):
                p = acc[g % 2]
                act.wait_ge(used, HU * (g + 1))
                if g < B_SWA + 2:
                    A(zq[:, :, 8 * g:8 * g + 8, :].rearrange("p t h d -> p t (h d)"),
                      p[:].rearrange("p (t n) -> p t n", t=TT), ACT.Copy).then_inc(evac_done, 1)
                elif g == B_SWA + 2:
                    pv = p[:].rearrange("p (t n) -> p t n", t=TT)
                    A(zq[:, :, 16:20, :].rearrange("p t h d -> p t (h d)"), pv[:, :, 0:256], ACT.Copy)
                    act.wait_ge(S_("vwin_zero"), 1)
                    for c, rows, t in ((1, slice(0, 128), 0), (3, slice(0, 128), 1), (0, slice(0, 64), 0),
                                       (2, slice(0, 64), 1), (2, slice(64, 128), 0)):
                        last = A(v_win[rows, c].rearrange("p g d -> p (g d)"), pv[rows, t, 256:512], ACT.Copy)
                    last.then_inc(evac_done, 1)
                elif g < B_WK:
                    if g == B_LORA:
                        act.wait_ge(S_("stage_zero"), 1)
                    if g >= B_LORA + 2:
                        act.wait_ge(S_("shifted"), g - B_LORA - 1)
                    A(stage[:, g % 2, 0:nf(g), 1:SEQ + 1],
                      p[:, 0:nf(g) * SEQ].rearrange("p (f t) -> p f t", t=SEQ), ACT.Copy).then_inc(evac_done, 1)
                elif g < B_OUT:
                    i = g - B_WK
                    if i >= 2:
                        act.wait_ge(kv_stored[i % 2], 16 * (i // 2))
                    st = fill_tmp[:, g % 2]
                    A(st.rearrange("p f t -> p (f t)"), p[:], ACT.Copy).then_inc(evac_done, 1)
                    act.wait_ge(evac_done, g + 1)
                    act.dma_start(kx_d[i] if i < 4 else vx_d[i - 4],
                                  st.rearrange("p f t -> p (f t)")).then_inc(kv_stored[i % 2], 16)
                elif B_WQ <= g < B_WO:
                    i = g - B_WQ
                    A(y_T[:, 4 * i:4 * i + 4].rearrange("p f t -> p (f t)"), p[:], ACT.Copy).then_inc(evac_done, 1)

            def nf(g):
                return 3 if g == B_LORA else 4

            def stat_sqrt(i, sem):
                act.wait_ge(S_(sem + "_ms"), 1)
                A(stat[:, i], stat[:, i], ACT.Sqrt).then_inc(S_(sem + "_rt"), 1)

            for j in range(TT):
                act.wait_ge(S_("x_loaded"), 16 * TT)
                A(junk[:], rows0[:, j], ACT.Square, accum_out=ssq[:, j, 0:1]).then_inc(S_("x_ssq"), 1)
                act.wait_ge(S_("x_ssq"), j + 1)
            stat_sqrt(0, "x")
            for k in range(3):
                w_high(k, 0, k)

            def fill_high(f, i, src):
                if i == 0 and f:
                    act.wait_ge(used, HU * FREE_AT[f])
                consumed(act, "fill", f, i)
                A(x_hi[:, 4 * i:4 * i + 4].rearrange("p f t -> p (f t)"), src.rearrange("p f t -> p (f t)"), ACT.Copy).then_inc(xh_ready, 1)

            def swa(n, s):
                if s[0] == "swa_scores":
                    p = job_wait_full(act, n)
                    g, j = s[1:]
                    m = 2 * g + j
                    if g:
                        produced(act, "swa_pT", g - 1, j)
                    else:
                        consumed(act, "swa_kT")
                    A(prob[:, j].rearrange("p (h f) k -> p h (f k)", h=2),
                      p[:].rearrange("p (h n) -> p h n", h=2)[:, :, 0:256], ACT.Copy, scale=HD ** -0.5).then_inc(job_free[n % 2], 1)
                    act.wait_ge(S_("s_shift"), m + 1)
                    A(prob[:, j], prob[:, j], ACT.Exp).then_inc(S_("s_exp"), 1)
                    A(soft[:, 2], soft[:, 1], ACT.Exp).then_inc(S_("s_exp"), 1)
                elif s[0] == "swa_pT":
                    p = job_wait_full(act, n)
                    g, j = s[1:]
                    if g:
                        produced(act, "swa_out", g - 1, j)
                    A(prob_T[:, j].rearrange("p h t -> p (h t)"), p[:, 0:512], ACT.Copy).then_inc(job_free[n % 2], 1)

            def rwkv(n, s):
                what, G = s[0], s[1]
                if what == "lora_wa":
                    p = job_wait_full(act, n)
                    if G:
                        act.wait_ge(S_("yt_ready"), G)
                    for f in range(2):
                        A(sl[0][:, f], p[:, f * 256:f * 256 + 256], ACT.Sigmoid, bias=colA[:, C_W0 + 2 * G + f:C_W0 + 2 * G + f + 1])
                        last = A(sl[2][:, f], p[:, 512 + f * 256:768 + f * 256], ACT.Sigmoid, bias=colA[:, C_A0 + 2 * G + f:C_A0 + 2 * G + f + 1])
                    last.then_inc(job_free[n % 2], 1)
                elif what == "lora_g":
                    p = job_wait_full(act, n)
                    A(sl[3][:].rearrange("p f t -> p (f t)"), p[:, 0:512], ACT.Copy).then_inc(job_free[n % 2], 1)
                elif what == "kk_norm":
                    consumed(act, *s)
                    A(sl[6][:], sl[6][:], ACT.Sqrt).then_inc(S_("kk_rt"), 1)
                    act.wait_ge(S_("cum_ready"), G + 1)
                    A(sl[0][:], sl[0][:], ACT.Exp).then_inc(S_("exp_ready"), 1)
                    A(sl[5][:], sl[1][:], ACT.Exp, scale=-1.0).then_inc(S_("exp_ready"), 1)
                    act.wait_ge(S_("exp_ready"), 3 * G + 2)
                    A(sl[1][:], sl[1][:], ACT.Exp).then_inc(S_("exp_ready"), 1)
                elif what == "bk_rows":
                    p = job_wait_full(act, n)
                    A(bk_rows[:].rearrange("p f c n -> p (f c n)"), p[:], ACT.Copy).then_inc(job_free[n % 2], 1)
                elif what == "inv_p":
                    p = job_wait_full(act, n)
                    for i in range(2):
                        h = slice(64 * i, 64 * i + 64)
                        last = A(inv_p[h].rearrange("p a b c d -> p (a b c d)"), p[h, 512 * i:512 * i + 512], ACT.Copy)
                    last.then_inc(job_free[n % 2], 1)
                elif what == "scan_x":
                    p = job_wait_full(act, n)
                    h = half(s[2])
                    A(xs[h].rearrange("p (f i) d -> p i f d", i=2),
                      p[h].rearrange("p (i n) -> p i n", i=2)[:, :, 0:P].rearrange("p i (f d) -> p i f d", f=2),
                      ACT.Copy, scale=-1.0).then_inc(job_free[n % 2], 1)
                elif what == "scan_u":
                    p = job_wait_full(act, n)
                    h = half(s[2])
                    A(uv[h, s[2]].rearrange("p i d -> p (i d)"), p[h, 0:256], ACT.Copy).then_inc(job_free[n % 2], 1)
                elif what == "gn_var":
                    consumed(act, *s)
                    A(sl[2][:], sl[2][:], ACT.Sqrt).then_inc(S_("gn_rt"), 1)

            def cross(n, s):
                h = s[1]
                if s[0] == "x_scores":
                    act.wait_ge(S_("x_max"), h + 1)
                    if h >= 2:
                        produced(act, "x_pT", h - 2)
                    p = js[n % 2]
                    for j in range(TT):
                        last = A(xp[:, h % 2, j], p[:, j * 256:j * 256 + 256], ACT.Exp, bias=stat[:, 6, j:j + 1],
                                 scale=XHD ** -0.5, accum_out=stat[:, 7, j:j + 1])
                    last.then_inc(job_free[n % 2], 1)
                elif s[0] == "x_pT":
                    p = job_wait_full(act, n)
                    if h >= 2:
                        produced(act, "x_out", h - 2)
                    A(xp_T[:, h % 2].rearrange("p m t -> p (m t)"), p[:, 0:512], ACT.Copy).then_inc(job_free[n % 2], 1)
                elif s[0] == "x_out":
                    p = job_wait_full(act, n)
                    A(y_T[:, 4 * h:4 * h + 4].rearrange("p f t -> p (f t)"), p[:], ACT.Copy).then_inc(job_free[n % 2], 1)

            def walk(steps):
                for n, *s in steps:
                    if s[0] == "hu":
                        g, k = s[1:]
                        lead(g, k)
                        if k == HU - 1:
                            evac(g)
                            if g == B_LORA:
                                act.wait_ge(S_("shifted"), 1)
                                A(lora[0:64, 0], lora[0:64, 0], ACT.Tanh).then_inc(S_("lora_act"), 1)
                                A(lora[:, 1], lora[:, 1], ACT.Sigmoid).then_inc(S_("lora_act"), 1)
                                A(lora[0:32, 2], lora[0:32, 2], ACT.Sigmoid).then_inc(S_("lora_act"), 1)
                    elif s[0] == "mem_norm":
                        for j in range(TT):
                            act.wait_ge(S_("mem_loaded"), 16 * TT)
                            A(junk[:], rows0[:, j], ACT.Square, accum_out=ssq[:, j, 1:2]).then_inc(S_("mem_ssq"), 1)
                            act.wait_ge(S_("mem_ssq"), j + 1)
                        stat_sqrt(1, "mem")
                        act.wait_ge(S_("ang_ready"), 1)
                        A(trig[:].rearrange("p a t i -> p (a t i)"), ang[:, 1:3].rearrange("p a t i -> p (a t i)"), ACT.Sin).then_inc(S_("trig_ready"), 1)
                    elif s[0] == "fill":
                        f, i = s[1:]
                        fill_high(f, i, fill_buf(f, i))
                    elif s[0] == "fill_T":
                        f, i = s[1:]
                        if i == 0:
                            act.wait_ge(used, HU * FREE_AT[f])
                            if f == 2:
                                act.wait_ge(S_("yt_ready"), 4)
                            else:
                                consumed(act, "x_out", XHEADS - 1)
                        A(x_hi[:, 4 * i:4 * i + 4].rearrange("p f t -> p (f t)"),
                          y_T[:, 4 * i:4 * i + 4].rearrange("p f t -> p (f t)"), ACT.Copy).then_inc(xh_ready, 1)
                    elif s[0].startswith("swa"):
                        swa(n, s)
                    elif s[0].startswith("x_"):
                        cross(n, s)
                    elif s[0] != "params":
                        rwkv(n, s)

            def residual(i):
                stat_sqrt(2 + i, f"post{i}")
                if i < 2:
                    for j in range(TT):
                        act.wait_ge(S_("xres_ready"), TT * i + j + 1)
                        A(y_rows[:, j], x_res[:, j], ACT.Square, accum_out=ssq[:, j, 0:1]).then_inc(S_(f"pre{i}_ssq"), 1)
                    stat_sqrt(5, f"pre{i}")

            def loop_rows(g0):
                with act.Fori(0, 2) as b2:
                    for r in range(2):
                        for k in range(HU):
                            g2, k2 = (r, k + 3) if k + 3 < HU else (r + 1, k + 3 - HU)
                            if not (r == 1 and k + 3 >= HU):
                                w_high(b2 * (2 * HU) + ((g0 + g2) * HU + k2), b2 * 2 + (g0 + g2), k2)
                            elif g0 == B_OUT:
                                w_high(b2 * (2 * HU) + ((g0 + g2) * HU + k2), b2 * 2 + (g0 + g2), k2)
                            else:
                                act.wait_ge(raw_loaded[k2 // 2], b2 * (16 * 3) + 16 * (B_WO + 3))
                                act.wait_ge(used, b2 * (2 * HU) + ((g0 + g2) * HU + k2 + 1 - SLOTS))
                                A(w_hi[:, k2 % SLOTS], raw[:, k2 // 2, 2 * (k2 % 2):2 * (k2 % 2) + 2], ACT.Copy).then_inc(hi_ready, 1)
                        act.wait_ge(used, b2 * (2 * HU) + (g0 + r + 1) * HU)
                        rows_out(y_rows, b2 * 2 + r, (g0 + r) % 2)

            walk(mix_steps)
            loop_rows(B_OUT)
            residual(0)
            walk(cross_steps)
            loop_rows(B_WO)
            residual(1)
            walk(ffn_steps)

            def up_step(i, r, last, first):
                for k in range(HU):
                    if not (last and k + 3 >= HU):
                        g2, k2 = (0, k + 3) if k + 3 < HU else (1, k + 3 - HU)
                        w_high(i * HU + ((B_UP + g2) * HU + k2), i + (B_UP + g2), k2, 512, True)
                    if not first and k == 2:
                        act.wait_ge(S_("conv_ready"), i)
                        A(gelu[:, 1 - r], conv[:, 1 - r], ACT.Gelu).then_inc(S_("gelu_ready"), 1)
                    if not first and k == 5:
                        act.wait_ge(evac_done, i + B_UP)
                        A(act_hi[:, bass.ds(i * 2 - 2, 2)], act32[:, 1 - r], ACT.Copy).then_inc(S_("acth_ready"), 1)
                act.wait_ge(used, i * HU + (B_UP + 1) * HU)
                A(gate[:, r, :, 2:SEQ + 2], acc[(B_UP + r) % 2][:, 0:512].rearrange("p (f t) -> p f t", f=2), ACT.Copy).then_inc(S_("gate_ready"), 1)

            act.wait_ge(S_("gate_zero"), 1)
            act.wait_ge(S_("x2_stored"), 16)
            up_step(0, 0, False, True)
            up_step(1, 1, False, False)
            with act.Fori(1, (N_UP - 1) // 2) as i2:
                up_step(i2 * 2, 0, False, False)
                up_step(i2 * 2 + 1, 1, False, False)
            up_step(N_UP - 1, 0, True, False)
            act.wait_ge(S_("conv_ready"), N_UP)
            A(gelu[:, 0], conv[:, 0], ACT.Gelu).then_inc(S_("gelu_ready"), 1)
            act.wait_ge(evac_done, B_DOWN)
            A(act_hi[:, FT_FF - 2:FT_FF], act32[:, 0], ACT.Copy).then_inc(S_("acth_ready"), 1)

            with act.Fori(0, N_DOWN // 2) as b2:
                w_high_down(b2 * 2, 0)
                w_high_down(b2 * 2, 1)
                for r in range(2):
                    for m in range(2, HD_DOWN):
                        w_high_down(b2 * 2 + r, m)
                    if r == 0:
                        w_high_down(b2 * 2 + 1, 0)
                        w_high_down(b2 * 2 + 1, 1)
                    act.wait_ge(used, b2 * (2 * HD_DOWN) + (Q_DOWN + (r + 1) * HD_DOWN))
                    rows_out(y_fin, b2 * 2 + r, (B_DOWN + r) % 2)
            residual(2)

        @block.vector
        def _(dve):
            V = nc.vector
            chain, counts = [0], {}

            def link(ins):
                chain[0] += 1
                ins.then_inc(S_("dve_chain"), 1)
                dve.wait_ge(S_("dve_chain"), chain[0])

            def give(ins, name):
                counts[name] = counts.get(name, 0) + 1
                ins.then_inc(S_(name), 1)
                dve.wait_ge(S_(name), counts[name])

            def free_job(ins, n):
                ins.then_inc(job_free[n % 2], 1)
                dve.wait_ge(job_free[n % 2], n // 2 + 1)

            def w_low(q, k, n=512):
                dve.wait_ge(hi_ready, q + 1)
                V.tensor_tensor(w_lo[:, k % SLOTS, :, 0:n], raw[:, k // 2, 2 * (k % 2):2 * (k % 2) + 2, 0:n],
                                w_hi[:, k % SLOTS, :, 0:n].bitcast(F32), ALU.subtract).then_inc(lo_ready, 1)

            def w_low_down(b, m):
                dve.wait_ge(hi_ready, b * HD_DOWN + (Q_DOWN + m + 1))
                V.tensor_tensor(w_lo[:, m % SLOTS_D], raw_d[:, m % RAW_D],
                                w_hi[:, m % SLOTS_D].bitcast(F32), ALU.subtract).then_inc(lo_ready, 1)

            def bc(t, shape):
                return t.broadcast_to(shape)

            def mean_square(i, k, name):
                give(V.tensor_scalar(stat[:, i], ssq[:, :, k], 1.0 / D, RMS_EPS, ALU.mult, ALU.add), name + "_ms")
                dve.wait_ge(S_(name + "_rt"), 1)
                link(V.reciprocal(stat[:, i], stat[:, i]))

            def fill(n, f, i):
                p = job_wait_full(dve, n)
                if i >= 2:
                    dve.wait_ge(xh_ready, 4 * f + i - 1)
                gain = colA[:, G_COL[f] + 4 * i:G_COL[f] + 4 * i + 4].unsqueeze(2)
                free_job(V.tensor_tensor(fill_buf(f, i), p[:].rearrange("p (f t) -> p f t", f=4),
                                         bc(gain, [P, 4, SEQ]), ALU.mult), n)
                low_fill(f, i, fill_buf(f, i))

            def low_fill(f, i, src):
                dve.wait_ge(xh_ready, 4 * f + i + 1)
                V.tensor_tensor(x_lo[:, 4 * i:4 * i + 4], src, x_hi[:, 4 * i:4 * i + 4].bitcast(F32),
                                ALU.subtract).then_inc(xl_ready, 1)

            def angles():
                c1, rest = 6.28125, 2 * math.pi - 6.28125
                c2 = math.floor(rest * 2.0 ** 17) / 2.0 ** 17
                c3 = math.floor((rest - c2) * 2.0 ** 26) / 2.0 ** 26
                c4 = rest - c2 - c3
                for i in range(8):
                    last = V.memset(ang[:, 5, 0, i:i + 1], INV_FREQ[i])
                link(last)
                for t in range(TT):
                    last = V.tensor_scalar(ang[:, 0, t], ang[:, 5, 0], colB[:, CB_POS + t:CB_POS + t + 1], None, ALU.mult)
                link(last)
                for m, turn, off in ((1, 0.25, math.pi / 2), (2, 0.0, 0.0)):
                    r, q = ang[:, m], ang[:, 2 + m]
                    link(V.tensor_scalar(q, ang[:, 0], 1 / (2 * math.pi), turn, ALU.mult, ALU.add))
                    link(V.tensor_scalar(q, q, 12582912.0, 12582912.0, ALU.add, ALU.subtract))
                    link(V.scalar_tensor_tensor(r, q, -c1, ang[:, 0], ALU.mult, ALU.add))
                    for c in (c2, c3, c4):
                        link(V.scalar_tensor_tensor(r, q, -c, r, ALU.mult, ALU.add))
                    link(V.tensor_scalar(r, r, off, 3.1415925, ALU.add, ALU.min))
                    ins = V.tensor_scalar(r, r, -3.1415925, None, ALU.max)
                    if m == 1:
                        link(ins)
                give(ins, "ang_ready")

            def rope_q_k():
                dve.wait_ge(evac_done, B_LORA)
                dve.wait_ge(S_("trig_ready"), 1)
                for j in range(TT):
                    t1, t2 = zq[:, j, 0:20, 0:8], zq[:, j, 0:20, 8:16]
                    cos, sin = (bc(trig[:, m, j].unsqueeze(1), [P, 20, 8]) for m in range(2))
                    for i, (x, y) in enumerate(((t1, cos), (t2, sin), (t2, cos), (t1, sin))):
                        last = V.tensor_tensor(rope[:, i], x, y, ALU.mult)
                    link(last)
                    V.tensor_tensor(t1, rope[:, 0], rope[:, 1], ALU.subtract)
                    link(V.tensor_tensor(t2, rope[:, 2], rope[:, 3], ALU.add))
                for j in range(TT):
                    last = V.tensor_copy(k_dup[:, j], bc(zq[:, j, 16:20].unsqueeze(2), [P, 4, 2, HD]))
                give(last, "kdup_ready")

            def swa(n, s):
                if s[0] == "swa_kT":
                    rope_q_k()
                    p = job_wait_full(dve, n)
                    free_job(V.tensor_copy(k_T[:].rearrange("p g t -> p (g t)"), p[:]), n)
                elif s[0] == "swa_qT":
                    p = job_wait_full(dve, n)
                    free_job(V.tensor_copy(q_T[:, s[1] % 2].rearrange("p f t -> p (f t)"), p[:, 0:512]), n)
                elif s[0] == "swa_scores":
                    g, j = s[1:]
                    consumed(dve, *s)
                    pr = prob[:, j]
                    if j == 0:
                        link(V.memset(prob[0:64, 0, :, 64:128], NEG_INF))
                    sk = sink[:, 4 * g:4 * g + 4].rearrange("p (f h) -> p h f", h=2)
                    s4 = [soft[:, i] for i in range(5)]
                    link(V.tensor_reduce(s4[0], pr, AX.X, ALU.max))
                    link(V.tensor_tensor(s4[0].rearrange("p (h f) -> p h f", h=2), s4[0].rearrange("p (h f) -> p h f", h=2), sk, ALU.max))
                    V.tensor_tensor(s4[1].rearrange("p (h f) -> p h f", h=2), sk, s4[0].rearrange("p (h f) -> p h f", h=2), ALU.subtract)
                    give(V.tensor_tensor(pr, pr, bc(s4[0].unsqueeze(2), [P, 4, P]), ALU.subtract), "s_shift")
                    dve.wait_ge(S_("s_exp"), 2 * (2 * g + j) + 2)
                    link(V.tensor_reduce(s4[3], pr, AX.X, ALU.add))
                    link(V.tensor_tensor(s4[3], s4[3], s4[2], ALU.add))
                    link(V.reciprocal(s4[3], s4[3]))
                    give(V.tensor_tensor(pr, pr, bc(s4[3].unsqueeze(2), [P, 4, P]), ALU.mult), "s_norm")
                elif s[0] == "swa_out":
                    g, j = s[1:]
                    p = job_wait_full(dve, n)
                    free_job(V.tensor_copy(y_T[:, 8 + 2 * g:10 + 2 * g, j * P:j * P + P],
                                           p[:, 0:256].rearrange("p (f t) -> p f t", f=2)), n)

            def shift(g):
                nf = 3 if g == B_LORA else 4
                f0 = 24 if g == B_LORA else 4 * (g - B_RKV)
                dst = lora[:] if g == B_LORA else rkv[:, f0:f0 + 4]
                dve.wait_ge(evac_done, g + 1)
                now, before = stage[:, g % 2, 0:nf, 1:SEQ + 1], stage[:, g % 2, 0:nf, 0:SEQ]
                link(V.tensor_tensor(dst, before, now, ALU.subtract))
                mu = bc(colB[:, CB_MU + f0:CB_MU + f0 + nf].unsqueeze(2), [P, nf, SEQ])
                link(V.tensor_tensor(dst, dst, mu, ALU.mult))
                give(V.tensor_tensor(dst, dst, now, ALU.add), "shifted")

            def heads(t):
                return t.rearrange("p f (c t) -> p f c t", c=NCH)

            def flat(t):
                return t.rearrange("p f t -> p (f t)")

            def rwkv(n, s):
                what, G = s[0], s[1]
                r, k, v = (rkv[:, 8 * i + 2 * G:8 * i + 2 * G + 2] for i in range(3))
                col = lambda c, f: colA[:, c + 2 * G + f:c + 2 * G + f + 1]
                if what == "lora_wa":
                    for f in range(2):
                        last = V.tensor_scalar(sl[4][:, f], k[:, f], col(C_KK, f), None, ALU.mult)
                    link(last)
                    give(V.tensor_tensor(sl[6][:], sl[4][:], sl[4][:], ALU.mult), "kk_sq")
                    V.memset(uv[64:128, 0:NCH:2], 0.0)
                    give(V.memset(uv[0:64, 1:NCH:2], 0.0), "uv_zero")
                elif what == "kk_norm":
                    p = job_wait_full(dve, n)
                    free_job(V.tensor_scalar(flat(sl[6][:]), p[:, 0:512], 1e-24, None, ALU.max), n)
                    consumed(dve, "lora_wa", G)
                    link(V.tensor_scalar(sl[0][:], sl[0][:], -DECAY_SCALE, None, ALU.mult))
                    for f in range(2):
                        last = V.tensor_tensor_scan(sl[1][:, f], reset[:], sl[0][:, f], 0.0, ALU.mult, ALU.add)
                    link(last)
                    give(V.tensor_tensor(sl[0][:], sl[1][:], sl[0][:], ALU.subtract), "cum_ready")
                    for f in range(2):
                        last = V.tensor_scalar(sl[7][:, f], sl[2][:, f], -1.0, col(C_KA, f), ALU.add, ALU.mult)
                    link(last)
                    link(V.scalar_tensor_tensor(sl[7][:], sl[7][:], 1.0, k, ALU.add, ALU.mult))
                    dve.wait_ge(S_("kk_rt"), G + 1)
                    link(V.reciprocal(sl[6][:], sl[6][:]))
                    link(V.tensor_tensor(sl[4][:], sl[4][:], sl[6][:], ALU.mult))
                    for f in range(2):
                        last = V.scalar_tensor_tensor(sl[6][:, f], r[:, f], col(C_RK, f), sl[7][:, f], ALU.mult, ALU.mult)
                    give(last, "bonus_ready")
                    dve.wait_ge(S_("exp_ready"), 3 * G + 3)
                    V.tensor_tensor(kr[:, :, :, 0], heads(sl[4][:]), heads(sl[0][:]), ALU.mult)
                    V.tensor_tensor(kr[:, :, :, 1], heads(r), heads(sl[1][:]), ALU.mult)
                    link(V.tensor_tensor(sl[2][:], sl[2][:], sl[4][:], ALU.mult))
                    for c in range(2):
                        cs = slice(c, NCH, 2)
                        V.tensor_tensor(bk[:, :, cs, b_part(c)], heads(sl[2][:])[:, :, cs], heads(sl[5][:])[:, :, cs], ALU.mult)
                        last = V.tensor_tensor(bk[:, :, cs, 1 - b_part(c)], heads(sl[7][:])[:, :, cs], heads(sl[5][:])[:, :, cs], ALU.mult)
                    give(last, "kr_ready")
                elif what == "v_rows":
                    p = job_wait_full(dve, n)
                    pv = p[:, 0:512].rearrange("p (t n) -> p t n", t=TT)
                    V.tensor_copy(uv[0:64, 0:NCH:2].rearrange("p c i d -> p c (i d)"), pv[0:64])
                    free_job(V.tensor_copy(uv[64:128, 1:NCH:2].rearrange("p c i d -> p c (i d)"), pv[64:128]), n)
                elif what == "scores":
                    p = job_wait_full(dve, n)
                    mask = bc(mask_sc[:].rearrange("p m t -> p (m t)").unsqueeze(1), [P, 8, P])
                    free_job(V.tensor_tensor(mx[:, s[2]].rearrange("p h f c n -> p (h f c) n"),
                                             p[:].rearrange("p (i n) -> p i n", i=8), mask, ALU.mult), n)
                elif what == "lower":
                    p = job_wait_full(dve, n)
                    mask = bc(mask_low[:].unsqueeze(1).unsqueeze(1), [P, 2, 2, CH])
                    for hh in range(2):
                        last = V.tensor_tensor(low[:, :, hh], p[:, 512 * hh:512 * hh + 256].rearrange("p (c f s) -> p c f s", c=2, f=2), mask, ALU.mult)
                    free_job(last, n)
                    for c in range(2):
                        h = half(c)
                        V.tensor_tensor(inv_x[h].rearrange("p a b c d -> p (a b c) d"),
                                        mx[h].rearrange("p a b f c n -> p (a b f) c n")[:, :, c, 0:CH],
                                        bc(lvl_x[h, 0].unsqueeze(1), [64, 8, CH]), ALU.mult)
                    link(V.tensor_tensor(inv_t[:].rearrange("p a b c d -> p (a b c) d"), low[:].rearrange("p a b c d -> p (a b c) d"),
                                         bc(lvl_t[:, 0].unsqueeze(1), [P, 8, CH]), ALU.mult))
                    e8 = bc(eye[:].unsqueeze(1), [P, 8, CH])
                    for t in (inv_x, inv_t):
                        tv = t[:].rearrange("p a b c d -> p (a b c) d")
                        last = V.tensor_tensor(tv, tv, e8, ALU.add)
                    give(last, "inv_ready")
                elif what in ("inv_x", "inv_t"):
                    p = job_wait_full(dve, n)
                    i = s[2].bit_length() - 1
                    dst, m = (inv_x, lvl_x) if what == "inv_x" else (inv_t, lvl_t)
                    for q in range(2):
                        h = slice(64 * q, 64 * q + 64)
                        last = V.copy_predicated(dst[h].rearrange("p a b c d -> p (a b c) d"),
                                                 bc(m[h, i].bitcast(I32).unsqueeze(1), [64, 8, CH]),
                                                 p[h, 512 * q:512 * q + 512].rearrange("p (i n) -> p i n", i=8))
                    free_job(last, n)
                elif what == "scan_ys":
                    p = job_wait_full(dve, n)
                    c = s[2]
                    if c < NCH - 1:
                        ps = p[:, 512:640].rearrange("p (f d) -> p f d", f=2)
                        decay = bc(heads(sl[1][:])[:, :, c, CH - 1:CH], [P, 2, HD])
                        if c:
                            link(V.tensor_tensor(state[:], ps, state[:], ALU.add))
                            give(V.tensor_tensor(state[:], state[:], decay, ALU.mult), "state_ready")
                        else:
                            give(V.tensor_tensor(state[:], ps, decay, ALU.mult), "state_ready")
                    free_job(V.tensor_copy(sl[7][:, :, CH * c:CH * c + CH], p[:, 0:128].rearrange("p (f t) -> p f t", f=2)), n)
                elif what == "gn_mean":
                    p = job_wait_full(dve, n)
                    V.scalar_tensor_tensor(flat(sl[7][:]), p[:, 0:512], -1.0 / HD, flat(sl[7][:]), ALU.mult, ALU.add)
                    free_job(V.tensor_tensor(flat(sl[4][:]), p[:, 512:1024], flat(v), ALU.mult), n)
                    give(V.tensor_tensor(sl[5][:], sl[7][:], sl[7][:], ALU.mult), "gn_sq")
                elif what == "gn_var":
                    p = job_wait_full(dve, n)
                    free_job(V.tensor_scalar(flat(sl[2][:]), p[:, 0:512], 1.0 / HD, GN_EPS, ALU.mult, ALU.add), n)
                    dve.wait_ge(S_("gn_rt"), G + 1)
                    link(V.reciprocal(sl[2][:], sl[2][:]))
                    link(V.tensor_tensor(sl[7][:], sl[7][:], sl[2][:], ALU.mult))
                    for f in range(2):
                        last = V.tensor_scalar(sl[7][:, f], sl[7][:, f], col(C_LNW, f), col(C_LNB, f), ALU.mult, ALU.add)
                    link(last)
                    link(V.tensor_tensor(sl[7][:], sl[7][:], sl[4][:], ALU.add))
                    consumed(dve, "lora_g", G)
                    give(V.tensor_tensor(y_T[:, 2 * G:2 * G + 2], sl[7][:], sl[3][:], ALU.mult), "yt_ready")

            def cross(n, s):
                h = s[1]
                if s[0] == "x_scores":
                    p = job_wait_full(dve, n)
                    link(V.tensor_reduce(stat[:, 5], p[:, 0:512].rearrange("p (t m) -> p t m", t=TT), AX.X, ALU.max))
                    give(V.tensor_scalar(stat[:, 6], stat[:, 5], -XHD ** -0.5, None, ALU.mult), "x_max")
                    consumed(dve, *s)
                    link(V.reciprocal(stat[:, 7], stat[:, 7]))
                    for j in range(TT):
                        last = V.tensor_scalar(xp[:, h % 2, j], xp[:, h % 2, j], stat[:, 7, j:j + 1], None, ALU.mult)
                    give(last, "x_norm")

            def lead(g, k):
                g2, k2 = (g, k + 3) if k + 3 < HU else (g + 1, k + 3 - HU)
                w_low(g2 * HU + k2, k2, 288 if g2 == B_LORA else 512)

            def walk(steps):
                for n, *s in steps:
                    if s[0] == "params":
                        p = job_wait_full(dve, n)
                        for i, t in enumerate((colA, colB, colC)):
                            last = V.tensor_copy(t[:], p[:, P * i:P * i + P])
                        free_job(last, n)
                    elif s[0] == "hu":
                        g, k = s[1:]
                        lead(g, k)
                        if k == HU - 1 and B_LORA <= g < B_WK:
                            shift(g)
                    elif s[0] == "mem_norm":
                        dve.wait_ge(S_("mem_ssq"), TT)
                        mean_square(1, 1, "mem")
                        for j in range(TT):
                            give(V.tensor_scalar(rows0[:, j], rows0[:, j], stat[:, 1, j:j + 1], None, ALU.mult), "mem_rows")
                        dve.wait_ge(xh_ready, 4)
                        V.memset(v_win[64:128, 0], 0.0).then_inc(S_("vwin_zero"), 1)
                        angles()
                        dve.wait_ge(S_("trig_ready"), 1)
                        V.memset(stage[:, :, :, 0:1], 0.0).then_inc(S_("stage_zero"), 1)
                    elif s[0] == "fill":
                        fill(n, *s[1:])
                    elif s[0] == "fill_T":
                        f, i = s[1:]
                        low_fill(f, i, y_T[:, 4 * i:4 * i + 4])
                    elif s[0].startswith("swa"):
                        swa(n, s)
                    elif s[0].startswith("x_"):
                        cross(n, s)
                    else:
                        rwkv(n, s)

            def residual(i, y, x, g, last_block):
                dve.wait_ge(evac_done, last_block)
                link(V.tensor_reduce(stat[:, 2 + i], ssq[:], AX.X, ALU.add))
                give(V.tensor_scalar(stat[:, 2 + i], stat[:, 2 + i], 1.0 / D, RMS_EPS, ALU.mult, ALU.add), f"post{i}_ms")
                dve.wait_ge(S_(f"post{i}_rt"), 1)
                link(V.reciprocal(stat[:, 2 + i], stat[:, 2 + i]))
                dve.wait_ge(S_("gpost_loaded"), 16 * (i + 1))
                dve.wait_ge(S_("x2_loaded" if i == 2 else "xres_loaded"), 16)
                for j in range(TT):
                    link(V.scalar_tensor_tensor(y[:, j], y[:, j], stat[:, 2 + i, j:j + 1], g[:], ALU.mult, ALU.mult))
                    give(V.tensor_tensor(x[:, j], x[:, j], y[:, j], ALU.add), "result" if i == 2 else "xres_ready")
                if i < 2:
                    dve.wait_ge(S_(f"pre{i}_ssq"), TT)
                    mean_square(5, 0, f"pre{i}")
                    for j in range(TT):
                        give(V.tensor_scalar(y[:, j], x[:, j], stat[:, 5, j:j + 1], None, ALU.mult), f"pre{i}_rows")

            def loop_rows(g0):
                with dve.Fori(0, 2) as b2:
                    for m in range(2 * HU):
                        w_low(b2 * (2 * HU) + (g0 * HU + m + 3), (m + 3) % HU)

            dve.wait_ge(S_("x_ssq"), TT)
            mean_square(0, 0, "x")
            for j in range(TT):
                give(V.tensor_scalar(rows0[:, j], rows0[:, j], stat[:, 0, j:j + 1], None, ALU.mult), "x_rows")
            dve.wait_ge(S_("pos_loaded"), 16)
            dve.wait_ge(S_("pack_zero"), 1)
            give(V.tensor_copy(pack[96:98, 1], pos_i[96:98]), "pos_float")
            dve.wait_ge(S_("masks"), 1)
            dve.wait_ge(S_("sink_loaded"), 16)
            for k in range(3):
                w_low(k, k)
            walk(mix_steps)
            loop_rows(B_OUT)
            residual(0, y_rows, x_res, g_post, B_WQ)
            walk(cross_steps)
            loop_rows(B_WO)
            residual(1, y_rows, x_res, g_post, B_UP)
            walk(ffn_steps)
            dve.wait_ge(xh_ready, 4 * 5 + 4)
            dve.wait_ge(S_("x2_stored"), 16)
            V.memset(gate[:, :, :, 0:2], 0.0).then_inc(S_("gate_zero"), 1)

            def conv_block(i, r, w=None):
                dve.wait_ge(S_("gate_ready"), i + 1)
                for f in range(2):
                    last = V.tensor_scalar(conv[:, r, f], gate[:, r, f, 0:SEQ], colC[:, bass.ds(i * 2 + f, 1)],
                                           colB[:, bass.ds(i * 2 + (CB_CB + f), 1)], ALU.mult, ALU.add)
                last.then_inc(S_("conv_part"), 1)
                dve.wait_ge(S_("conv_part"), i * 2 + 1)
                for f in range(2):
                    last = V.scalar_tensor_tensor(conv[:, r, f], gate[:, r, f, 1:SEQ + 1], colC[:, bass.ds(i * 2 + (FT_FF + f), 1)],
                                                  conv[:, r, f], ALU.mult, ALU.add)
                last.then_inc(S_("conv_part"), 1)
                dve.wait_ge(S_("conv_part"), i * 2 + 2)
                for f in range(2):
                    last = V.scalar_tensor_tensor(conv[:, r, f], gate[:, r, f, 2:SEQ + 2], colC[:, bass.ds(i * 2 + (2 * FT_FF + f), 1)],
                                                  conv[:, r, f], ALU.mult, ALU.add)
                last.then_inc(S_("conv_ready"), 1)

            def mult_block(i, r):
                dve.wait_ge(S_("gelu_ready"), i + 1)
                V.tensor_tensor(act32[:, r], gelu[:, r], acc[(B_UP + r) % 2][:, 512:1024].rearrange("p (f t) -> p f t", f=2),
                                ALU.mult).then_inc(evac_done, 1)

            def low_block(i, r):
                dve.wait_ge(S_("acth_ready"), i + 1)
                V.tensor_tensor(act_lo[:, bass.ds(i * 2, 2)], act32[:, r], act_hi[:, bass.ds(i * 2, 2)].bitcast(F32),
                                ALU.subtract).then_inc(S_("actl_ready"), 1)

            def up_step(i, r, first, last):
                for k in range(HU):
                    if not first and k == 0:
                        conv_block(i - 1, 1 - r)
                    if not first and k == 3:
                        mult_block(i - 1, 1 - r)
                    if not first and k == 6:
                        low_block(i - 1, 1 - r)
                    if not (last and k + 3 >= HU):
                        w_low(i * HU + (B_UP * HU + k + 3), (k + 3) % HU)

            up_step(0, 0, True, False)
            up_step(1, 1, False, False)
            with dve.Fori(1, (N_UP - 1) // 2) as i2:
                up_step(i2 * 2, 0, False, False)
                up_step(i2 * 2 + 1, 1, False, False)
            up_step(N_UP - 1, 0, False, True)
            conv_block(N_UP - 1, 0)
            mult_block(N_UP - 1, 0)
            low_block(N_UP - 1, 0)
            with dve.Fori(0, N_DOWN // 2) as b2:
                for m in range(2 * HD_DOWN):
                    w_low_down(b2 * 2 + m // HD_DOWN, m % HD_DOWN)
            residual(2, y_fin, x_fin, g_fin, B_DOWN + N_DOWN)

        @block.tensor
        def _(pe):
            T = nc.tensor

            def products(g, par, k, kind, f, n=512):
                q = g * HU + k
                if k == 0 and not (isinstance(g, int) and g < 2):
                    pe.wait_ge(evac_done, g - 1)
                if f is not None and k % 2 == 0:
                    pe.wait_ge(xl_ready, 4 * f + k // 2 + 1)
                pe.wait_ge(lo_ready, q + 1)
                sl_ = k % SLOTS
                for kt in range(2):
                    x = 2 * k + kt
                    first, final = x == 0, x == KT - 1
                    if kind == ROWS:
                        for t in range(TT):
                            o = acc[par][:, 512 * t:512 * t + 512]
                            xs_ = slice(P * t, P * t + P)
                            T.matmul(o, x_hi[:, x, xs_], w_hi[:, sl_, kt], start=first, stop=False)
                            T.matmul(o, x_hi[:, x, xs_], w_lo[:, sl_, kt], start=False, stop=False)
                            last = T.matmul(o, x_lo[:, x, xs_], w_hi[:, sl_, kt], start=False, stop=final)
                    else:
                        for c in range(n // P + (n % P > 0)):
                            o = acc[par][:, SEQ * c:SEQ * c + SEQ]
                            cs = slice(P * c, P * c + P)
                            T.matmul(o, w_hi[:, sl_, kt, cs], x_hi[:, x], start=first and c % 2 == 0, stop=False, skip_group_check=True)
                            T.matmul(o, w_hi[:, sl_, kt, cs], x_lo[:, x], start=False, stop=False, skip_group_check=True)
                            last = T.matmul(o, w_lo[:, sl_, kt, cs], x_hi[:, x], start=False, stop=final, skip_group_check=True)
                last.then_inc(used, 1)

            def begin(n):
                if n >= 2:
                    pe.wait_ge(job_free[n % 2], n // 2)
                return js[n % 2]

            def end(ins, n):
                ins.then_inc(job_full[n % 2], 1)

            def mm(o, l, r, start=True, stop=True):
                return T.matmul(o, l, r, start=start, stop=stop, skip_group_check=True)

            ROWS_OF = {0: (rows0, "x_rows"), 1: (rows0, "mem_rows"), 3: (y_rows, "pre0_rows"), 5: (y_rows, "pre1_rows")}

            def fill(n, f, i):
                p = begin(n)
                rows, ready = ROWS_OF[f]
                pe.wait_ge(S_(ready), TT)
                for c in range(4):
                    for t in range(TT):
                        last = T.transpose(p[:, SEQ * c + P * t:SEQ * c + P * t + P],
                                           rows[:, t, P * (4 * i + c):P * (4 * i + c) + P], ident[:])
                end(last, n)

            def swa(n, s):
                p = begin(n)
                if s[0] == "swa_kT":
                    pe.wait_ge(S_("kdup_ready"), 1)
                    for g in range(4):
                        for t in range(TT):
                            last = T.transpose(p[:, SEQ * g + P * t:SEQ * g + P * t + P],
                                               k_dup[:, t, g].rearrange("p a d -> p (a d)"), ident[:])
                elif s[0] == "swa_qT":
                    g = s[1]
                    for f in range(2):
                        for t in range(TT):
                            last = T.transpose(p[:, SEQ * f + P * t:SEQ * f + P * t + P],
                                               zq[:, t, 4 * g + 2 * f:4 * g + 2 * f + 2].rearrange("p a d -> p (a d)"), ident[:])
                elif s[0] == "swa_scores":
                    g, j = s[1:]
                    consumed(pe, "swa_qT", g)
                    consumed(pe, "swa_kT")
                    for f in range(2):
                        for par in range(2):
                            c = 2 * j + par
                            for hh in range(2):
                                h = slice(64 * hh, 64 * hh + 64)
                                for piece in range(2):
                                    own = piece == par
                                    kc = c if own else max(c - 1, 0)
                                    last = mm(p[64 * par:64 * par + 64, 512 * hh + P * f + CH * piece:512 * hh + P * f + CH * piece + CH],
                                              q_T[h, g % 2, f, CH * c:CH * c + CH], k_T[h, g, CH * kc:CH * kc + CH])
                elif s[0] == "swa_pT":
                    g, j = s[1:]
                    pe.wait_ge(S_("s_norm"), 2 * g + j + 1)
                    for i in range(4):
                        last = T.transpose(p[:, P * i:P * i + P], prob[:, j, i], ident[:])
                else:
                    g, j = s[1:]
                    consumed(pe, "swa_pT", g, j)
                    for f in range(2):
                        for par in range(2):
                            for hh in range(2):
                                last = mm(p[64 * hh:64 * hh + 64, P * f + CH * par:P * f + CH * par + CH],
                                          v_win[:, 2 * j + par, g], prob_T[:, j, 2 * hh + f, CH * par:CH * par + CH])
                end(last, n)

            def rwkv(n, s):
                what, G = s[0], s[1]
                p = begin(n)
                hs = [slice(0, 64), slice(64, 128)]
                if what == "lora_wa":
                    pe.wait_ge(S_("lora_act"), 3)
                    pe.wait_ge(S_("lora_loaded"), 64 * (G + 1))
                    for f in range(2):
                        for i in range(2):
                            last = mm(p[:, 512 * i + SEQ * f:512 * i + SEQ * f + SEQ], lora_w[hs[i], 0, P * f:P * f + P], lora[hs[i], 0])
                elif what == "lora_g":
                    for f in range(2):
                        o = p[:, SEQ * f:SEQ * f + SEQ]
                        mm(o, lora_w[:, 1, P * f:P * f + P], lora[:, 1], True, False)
                        last = mm(o, lora_w[0:32, 2, P * f:P * f + P], lora[0:32, 2], False, True)
                elif what == "kk_norm":
                    pe.wait_ge(S_("kk_sq"), G + 1)
                    last = mm(p[:, 0:512], hones[:], sl[6][:].rearrange("p f t -> p (f t)"))
                elif what == "v_rows":
                    for t in range(TT):
                        for f in range(2):
                            last = T.transpose(p[:, SEQ * t + P * f:SEQ * t + P * f + P], rkv[:, 16 + 2 * G + f, P * t:P * t + P], ident[:])
                elif what == "bk_rows":
                    pe.wait_ge(S_("kr_ready"), G + 1)
                    for f in range(2):
                        for c in range(NCH):
                            last = T.transpose(p[:, 512 * f + P * c:512 * f + P * c + P], bk[:, f, c].rearrange("p a s -> p (a s)"), ident[:])
                elif what == "scores":
                    for f in range(2):
                        for cc in range(2):
                            c = 2 * s[2] + cc
                            for hh in range(2):
                                at_ = 512 * hh + 256 * f + P * cc
                                last = mm(p[:, at_:at_ + P], bk[hs[hh], f, c].rearrange("p a s -> p (a s)"),
                                          kr[hs[hh], f, c].rearrange("p a s -> p (a s)"))
                elif what == "lower":
                    for c in range(NCH):
                        for f in range(2):
                            for hh in range(2):
                                at_ = 512 * hh + P * (c // 2) + CH * f
                                last = mm(p[half(c), at_:at_ + CH], kr[hs[hh], f, c, 0], bk[hs[hh], f, c, b_part(c)])
                elif what in ("inv_p", "inv_x", "inv_t"):
                    b = s[2]
                    if what == "inv_p":
                        if b == LEVELS[0]:
                            pe.wait_ge(S_("inv_ready"), G + 1)
                        else:
                            consumed(pe, "inv_x", G, b // 2)
                        left, right = low, inv_x
                    elif what == "inv_x":
                        consumed(pe, "inv_p", G, b)
                        if b != LEVELS[0]:
                            consumed(pe, "inv_t", G, b // 2)
                        left, right = inv_t, inv_p
                    else:
                        left, right = inv_p, inv_t
                    for i in range(8):
                        ix = (i // 4, i // 2 % 2, i % 2)
                        for q in range(2):
                            at_ = 512 * q + CH * i
                            last = mm(p[hs[q], at_:at_ + CH], left[hs[q], ix[0], ix[1], ix[2]], right[hs[q], ix[0], ix[1], ix[2]])
                elif what in ("scan_x", "scan_u", "scan_ys"):
                    c = s[2]
                    h = half(c)
                    if what == "scan_x":
                        if c:
                            pe.wait_ge(S_("state_ready"), 3 * G + c)
                        else:
                            consumed(pe, "v_rows", G)
                            consumed(pe, "bk_rows", G)
                            consumed(pe, "scores", G, 1)
                            pe.wait_ge(S_("uv_zero"), G + 1)
                        consumed(pe, "inv_x", G, LEVELS[-1])
                    elif what == "scan_u":
                        consumed(pe, "scan_x", G, c)
                    else:
                        consumed(pe, "scan_u", G, c)
                    for f in range(2):
                        for hh in range(2):
                            i = 2 * f + hh
                            m = mx[:, c // 2, hh, f, c % 2]
                            if what == "scan_x":
                                o = p[h, 512 * hh + CH * f:512 * hh + CH * f + CH]
                                last = mm(o, m[:, 0:CH], uv[:, c, i], True, c == 0)
                                if c:
                                    last = mm(o, kr[hs[hh], f, c, 0], state[hs[hh], f], False, True)
                            elif what == "scan_u":
                                last = mm(p[h, CH * i:CH * i + CH], inv_x[h, c // 2, hh, f], xs[h, i])
                            else:
                                o = p[hs[hh], CH * f:CH * f + CH]
                                mm(o, uv[:, c, i], m[:, CH:2 * CH], True, c == 0)
                                if c:
                                    mm(o, state[hs[hh], f], kr[hs[hh], f, c, 1], False, True)
                                last = mm(p[hs[hh], 512 + CH * f:512 + CH * f + CH], bk_rows[:, f, c, 64 * hh:64 * hh + 64], uv[:, c, i])
                elif what == "gn_mean":
                    consumed(pe, "scan_ys", G, NCH - 1)
                    pe.wait_ge(S_("bonus_ready"), G + 1)
                    mm(p[:, 0:512], hones[:], sl[7][:].rearrange("p f t -> p (f t)"))
                    last = mm(p[:, 512:1024], hones[:], sl[6][:].rearrange("p f t -> p (f t)"))
                else:
                    pe.wait_ge(S_("gn_sq"), G + 1)
                    last = mm(p[:, 0:512], hones[:], sl[5][:].rearrange("p f t -> p (f t)"))
                end(last, n)

            def cross(n, s):
                p = begin(n)
                h = s[1]
                if s[0] == "x_scores":
                    pe.wait_ge(evac_done, B_WQ + h + 1)
                    pe.wait_ge(S_("kv_loaded"), 16 * 8)
                    for j in range(TT):
                        for c in range(4):
                            last = mm(p[:, MEM * j:MEM * j + MEM], y_T[:, 4 * h + c, P * j:P * j + P], kx[:, 4 * h + c], c == 0, c == 3)
                elif s[0] == "x_pT":
                    pe.wait_ge(S_("x_norm"), h + 1)
                    for m in range(2):
                        for j in range(TT):
                            last = T.transpose(p[:, SEQ * m + P * j:SEQ * m + P * j + P], xp[:, h % 2, j, P * m:P * m + P], ident[:])
                else:
                    consumed(pe, "x_pT", h)
                    for c in range(4):
                        for m in range(2):
                            last = mm(p[:, SEQ * c:SEQ * c + SEQ], vx[:, m, h, P * c:P * c + P], xp_T[:, h % 2, m], m == 0, m == 1)
                end(last, n)

            def walk(steps):
                for n, *s in steps:
                    if s[0] == "params":
                        p = begin(n)
                        pe.wait_ge(S_("pos_float"), 1)
                        pe.wait_ge(S_("pack_loaded"), 15 * 16)
                        pe.wait_ge(S_("masks"), 1)
                        for i in range(3):
                            last = T.transpose(p[:, P * i:P * i + P], pack[:, i], ident[:])
                        end(last, n)
                    elif s[0] == "hu":
                        g, k = s[1:]
                        products(g, g % 2, k, kind_of(g), FIRST_OF_FILL.get(g), 288 if g == B_LORA else 512)
                    elif s[0] == "fill":
                        fill(n, *s[1:])
                    elif s[0].startswith("swa"):
                        swa(n, s)
                    elif s[0].startswith("x_"):
                        cross(n, s)
                    elif s[0] not in ("mem_norm", "fill_T"):
                        rwkv(n, s)

            def loop_rows(g0, f):
                with pe.Fori(0, 2) as b2:
                    for r in range(2):
                        for k in range(HU):
                            products(b2 * 2 + (g0 + r), (g0 + r) % 2, k, ROWS, f)

            walk(mix_steps)
            loop_rows(B_OUT, 2)
            walk(cross_steps)
            loop_rows(B_WO, 4)
            walk(ffn_steps)
            for k in range(HU):
                products(B_UP, B_UP % 2, k, COLS, 5)
            with pe.Fori(0, (N_UP - 1) // 2) as i2:
                for r in range(2):
                    for k in range(HU):
                        products(i2 * 2 + (B_UP + 1 + r), (B_UP + 1 + r) % 2, k, COLS, None)
            with pe.Fori(0, N_DOWN // 2) as b2:
                for r in range(2):
                    par = (B_DOWN + r) % 2
                    pe.wait_ge(evac_done, b2 * 2 + (B_DOWN + r - 1))
                    for m in range(HD_DOWN):
                        pe.wait_ge(S_("actl_ready"), m + 1)
                        pe.wait_ge(lo_ready, b2 * (2 * HD_DOWN) + (Q_DOWN + r * HD_DOWN + m + 1))
                        for kt in range(2):
                            x = 2 * m + kt
                            for t in range(TT):
                                o = acc[par][:, 512 * t:512 * t + 512]
                                ts_ = slice(P * t, P * t + P)
                                T.matmul(o, act_hi[:, x, ts_], w_hi[:, m % SLOTS_D, kt], start=x == 0, stop=False)
                                T.matmul(o, act_hi[:, x, ts_], w_lo[:, m % SLOTS_D, kt], start=False, stop=False)
                                last = T.matmul(o, act_lo[:, x, ts_], w_hi[:, m % SLOTS_D, kt], start=False, stop=x == FT_FF - 1)
                        last.then_inc(used, 1)


_INS = ["x", "mem", "positions", "norm_mix_pre", "norm_mix_post", "w_in", "shift_mu", "w0", "w_lora_up", "a0",
        "a_lora_up", "g_lora_up", "k_k", "k_a", "r_k", "ln_x_w", "ln_x_b", "attn_sinks", "w_out", "norm_cross_pre",
        "norm_cross_post", "mem_norm", "wq_x", "wk_x", "wv_x", "wo_x", "norm_ffn_pre", "norm_ffn_post", "w_up",
        "conv_w", "conv_b", "w_down"]


def kernel(**inputs):
    import numpy as _np
    import concourse.bacc as _bacc
    from concourse import mybir as _mybir
    from concourse.bass_utils import run_bass_kernel_spmd as _run

    nc = _bacc.Bacc("TRN2", target_bir_lowering=False, num_devices=1)
    arrays, args = {}, {}
    for name in _INS:
        v = _np.ascontiguousarray(inputs[name])
        arrays[f"in_{name}_dram"] = v
        args[name] = nc.dram_tensor(f"in_{name}_dram", v.shape, _mybir.dt.from_np(v.dtype), kind="ExternalInput").ap()
    out = nc.dram_tensor("out_0_dram", (1, SEQ, D), _mybir.dt.float32, kind="ExternalOutput").ap()
    build(nc, args, out)
    r = _run(nc, [arrays], core_ids=[0])
    return r.results[0]["out_0_dram"]
```

```python
import math
import concourse.bass as bass
from concourse import mybir
from contextlib import ExitStack

F32, F32R, I32 = mybir.dt.float32, mybir.dt.float32r, mybir.dt.int32
ALU, ACT, AX = mybir.AluOpType, mybir.ActivationFunctionType, mybir.AxisListType

D, SEQ, MEM, P = 2048, 256, 256, 128
KT = D // P
TT = SEQ // P
CH = 64
NCH = SEQ // CH
RW, HD = 1024, 64
NLORA_W, NLORA_A, NLORA_G = 64, 64, 160
N_RWKV = 3 * RW + NLORA_W + NLORA_A + NLORA_G
N_IN = N_RWKV + 24 * HD
DFF = 5376
FT_FF = DFF // P
XHEADS, XHD = 4, 512
DECAY_SCALE = math.exp(-0.5)
GN_EPS, RMS_EPS = 64e-5, 1e-6
NEG_INF = -1e30
ROT = 16
INV_FREQ = [500000.0 ** (-i / ROT) for i in range(0, ROT, 2)]

B_SWA, B_LORA, B_RKV, B_WK, B_WV, B_OUT, B_WQ, B_WO, B_UP, B_DOWN = 0, 3, 4, 10, 14, 18, 22, 26, 30, 51
N_UP, N_DOWN = 21, 4
HU = 8
Q_DOWN = B_DOWN * HU
HD_DOWN = FT_FF // 2
AHEAD = 6
SLOTS, SLOTS_D, RAW_D = 4, 3, 7
COLS, ROWS = "cols", "rows"


def kind_of(g):
    return COLS if B_LORA <= g < B_WV or B_WQ <= g < B_WO or B_UP <= g < B_DOWN else ROWS


FIRST_OF_FILL = {B_SWA: 0, B_WK: 1, B_OUT: 2, B_WQ: 3, B_WO: 4, B_UP: 5}

LEVELS = (2, 4, 8, 16, 32)


HERE = ("hu",)
NO_JOB = ("hu", "mem_sq", "mem_scale", "angles", "fill_T", "rope", "uv_zero", "prep_kk", "prep_decay", "prep_k", "prep_bonus",
          "prep_kr", "prep_bk", "gn_out")


def swa_steps():
    H = HERE
    yield from [("rope",), H, H, H, ("swa_kT",), ("swa_qT", 0), H, H]
    for g in range(4):
        yield from [("swa_scores", g, 0), H, H, ("swa_scores", g, 1), H, H, ("swa_pT", g, 0), H, H,
                    ("swa_out", g, 0), H]
        if g < 3:
            yield from [("swa_qT", g + 1), H]
        yield from [("swa_pT", g, 1), H, H, ("swa_out", g, 1), H]


def rwkv_steps():
    H = HERE
    yield from [("uv_zero", 0)]
    for G in range(4):
        nxt = G + 1 < 4

        def prep(*steps):
            return [(s, G + 1) for s in steps] if nxt else []

        if G == 0:
            yield from [("v_rows", 0), ("bk_rows", 0), ("lower", 0), ("scores", 0, 0), H, ("scores", 0, 1), H]
        yield ("inv_p", G, 2)
        yield H
        yield ("inv_x", G, 2)
        yield ("inv_t", G, 2)
        yield from prep("prep_kk")
        yield from [("inv_p", G, 4), H, ("inv_x", G, 4), ("inv_t", G, 4)]
        yield from prep("lora_wa", "kk_norm")
        yield from [("inv_p", G, 8), H, ("inv_x", G, 8), ("inv_t", G, 8)]
        yield from prep("prep_decay")
        yield from [("inv_p", G, 16), H, ("inv_x", G, 16), ("inv_t", G, 16)]
        yield from prep("prep_k")
        yield from [("inv_p", G, 32), H, ("inv_x", G, 32), H]
        for c in range(NCH):
            yield ("scan_x", G, c)
            if c < NCH - 1:
                yield H
            else:
                yield ("lora_g", G)
            yield ("scan_u", G, c)
            if c < NCH - 1:
                yield from prep(("prep_bonus", "prep_kr", "prep_bk")[c])
            if c < 1:
                yield H
            yield ("scan_ys", G, c)
            if c < NCH - 1:
                yield H
        if nxt:
            yield from [("bk_rows", G + 1), ("gn_mean", G), ("uv_zero", G + 1), ("scores", G + 1, 0), ("gn_var", G),
                        ("lower", G + 1), ("v_rows", G + 1), ("scores", G + 1, 1), ("gn_out", G), H]
        else:
            yield from [("gn_mean", G), H, ("gn_var", G), ("gn_out", G)]


def cross_jobs(h):
    yield ("x_scores", h)
    yield ("x_pT", h)
    yield ("x_out", h)


def weave(steps, hus):
    hus = list(hus)
    out = [hus.pop(0) if s == HERE else s for s in steps]
    return out, hus


def spread(jobs, hus):
    jobs, hus = list(jobs), list(hus)
    out, done = [], 0
    for i, job in enumerate(jobs):
        out.append(job)
        upto = (i + 1) * len(hus) // len(jobs)
        out += hus[done:upto]
        done = upto
    return out + hus[done:]


def half_units(g0, g1):
    return [("hu", g, k) for g in range(g0, g1) for k in range(HU)]


def schedule():
    H = HERE
    mix, left = weave([("gain",), ("fill", 0, 0), ("fill", 0, 1), H, ("fill", 0, 2), H, ("fill", 0, 3), H, H, H,
                       ("mem_sq",), H, H, ("params",), H, ("mem_scale",), H, H, ("angles",)],
                      half_units(B_SWA, B_LORA))
    mix += left
    steps, left = weave(swa_steps(), half_units(B_LORA, B_WK))
    mix += steps + left[:-2] + [("prep_kk", 0)] + left[-2:] + [("lora_wa", 0), ("kk_norm", 0)]
    steps, left = weave([("fill", 1, 0), ("fill", 1, 1), ("prep_decay", 0), H, ("fill", 1, 2), ("prep_k", 0), H,
                         ("fill", 1, 3), ("prep_bonus", 0), H, ("prep_kr", 0), ("prep_bk", 0), H]
                        + list(rwkv_steps()), half_units(B_WK, B_OUT))
    mix += steps + left
    mix += [("fill_T", 2, i) for i in range(4)]
    cross, left = weave([("fill", 3, 0), ("fill", 3, 1), H, ("fill", 3, 2), H, ("fill", 3, 3)], half_units(B_WQ, B_WQ + 1))
    cross += left
    for h in range(XHEADS):
        jobs = list(cross_jobs(h))
        if h < XHEADS - 1:
            cross += spread(jobs, half_units(B_WQ + h + 1, B_WQ + h + 2))
        else:
            cross += jobs
    cross += [("fill_T", 4, i) for i in range(4)]
    ffn, left = weave([("fill", 5, 0), ("fill", 5, 1), H, ("fill", 5, 2), H, ("fill", 5, 3)], half_units(B_UP, B_UP + 1))
    ffn += left
    n, out = 0, []
    for part in (mix, cross, ffn):
        steps = []
        for s in part:
            if s[0] in NO_JOB:
                steps.append((None,) + s)
            else:
                steps.append((n,) + s)
                n += 1
        out.append(steps)
    return out


def build(nc, a, out):
    mix_steps, cross_steps, ffn_steps = schedule()
    ctx = ExitStack()
    with ctx:
        base = 16640

        def sb(name, shape, dt, at):
            return nc.alloc_sbuf_tensor_at(name, [P] + list(shape), dt, offset=base + at)

        raw = sb("raw", [4, 4, 512], F32, 0)
        raw_d = sb("raw_d", [RAW_D, 2, 512], F32, 0)
        w_hi = sb("w_hi", [SLOTS, 2, 512], F32R, 32768)
        w_lo = sb("w_lo", [SLOTS, 2, 512], F32R, 49152)
        x_hi = sb("x_hi", [KT, SEQ], F32R, 65536)
        x_lo = sb("x_lo", [KT, SEQ], F32R, 81920)
        at = [98304]

        def const(name, shape, dt=F32):
            n = 4
            for s in shape:
                n *= s
            t = sb(name, shape, dt, at[0])
            at[0] += (n + 31) // 32 * 32
            return t

        colA, colB, colC = const("colA", [P]), const("colB", [P]), const("colC", [P])
        ident, hones = const("ident", [P]), const("hones", [P])
        mask_sc, mask_low = const("mask_sc", [2, CH]), const("mask_low", [CH])
        lvl_x, lvl_t = const("lvl_x", [6, CH]), const("lvl_t", [5, CH])
        eye = const("eye", [CH])
        reset = const("reset", [SEQ])
        trig = const("trig", [2, TT, 8])
        sink = const("sink", [16])
        ssq = const("ssq", [TT, 4])
        stat = const("stat", [8, TT])
        soft = const("soft", [6, 4])
        assert at[0] <= 106496, at
        R = 106496

        feat = sb("feat", [32, SEQ], F32, R)
        y_T = feat[:, 0:KT]
        junk = sb("junk", [D], F32, R + 16384)
        slot_at = [R + 32768 + 2048 * i for i in range(4)]
        lora = sb("lora", [3, SEQ], F32, R + 40960)
        lora_w = sb("lora_w", [3, 2 * P], F32, R + 44032)
        stage = sb("stage", [2, 4, SEQ + 1], F32, R + 47104)
        fill_tmp = sb("fill_tmp", [2, 4, SEQ], F32, R + 47104)
        pack = sb("pack", [3, P], F32, R + 40960)
        pos_i = sb("pos_i", [P], I32, R + 40960 + 1536)
        ang = sb("ang", [6, TT, 8], F32, R + 47104 + 2048)
        S = R + 55360
        rows0 = sb("rows0", [TT, D], F32, S)
        zq = sb("zq", [TT, 24, HD], F32, S + 16384)
        q_T = sb("q_T", [2, 2, SEQ], F32, S + 28672)
        k_T = sb("k_T", [4, SEQ], F32, S + 32768)
        v_win = sb("v_win", [NCH, 4, HD], F32, S + 36864)
        prob = sb("prob", [2, 4, P], F32, S + 40960)
        rope = sb("rope", [4, 20, 8], F32, S + 40960)
        prob_T = sb("prob_T", [2, 4, P], F32, S + 45056)
        k_dup = sb("k_dup", [TT, 4, 2, HD], F32, S + 45056)
        bk = sb("bk", [2, NCH, 2, CH], F32, S)
        kr = [sb(f"kr{i}", [2, NCH, 2, CH], F32, S + o) for i, o in enumerate((4096, 28672))]
        bk_rows = sb("bk_rows", [2, NCH, P], F32, S + 8192)
        uv = sb("uv", [NCH, 4, HD], F32, S + 12288)
        slot_at += [S + 16384 + 2048 * i for i in range(6)]
        decay, rate, kk, inv_norm, cum, exp_neg, k_new, y_grp, bonus0, bonus1 = (
            sb(name, [2, SEQ], F32, o) for name, o in zip(
                ("decay", "rate", "kk", "inv_norm", "cum", "exp_neg", "k_new", "y_grp", "bonus0", "bonus1"), slot_at))
        bonus = [bonus0, bonus1]
        y_sq, rstd, bonus_v, gate_g = decay, rate, kk, exp_neg
        mx = sb("mx", [2, 2, 2, 2, 2 * CH], F32, S + 32768)
        low = sb("low", [2, 2, 2, CH], F32, S + 40960)
        inv_t = sb("inv_t", [2, 2, 2, CH], F32, S + 43008)
        inv_x = sb("inv_x", [2, 2, 2, CH], F32, S + 45056)
        inv_p = sb("inv_p", [2, 2, 2, CH], F32, S + 47104)
        state = sb("state", [2, HD], F32, S + 49152)
        xs = sb("xs", [4, HD], F32, S + 49664)
        chunk_decay = sb("chunk_decay", [2, 2, NCH], F32, S + 50688)
        y_rows = sb("y_rows", [TT, D], F32, R + 16384)
        x_res = sb("x_res", [TT, D], F32, R + 32768)
        kx = sb("kx", [KT, MEM], F32, R + 49152)
        vx = sb("vx", [TT, 4, 512], F32, R + 65536)
        g_post = sb("g_post", [D], F32, R + 81920)
        xp = sb("xp", [2, TT, MEM], F32, R + 90112)
        xp_T = sb("xp_T", [2, TT, SEQ], F32, R + 94208)
        xfill = sb("xfill", [2, 4, SEQ], F32, R)
        act_hi = sb("act_hi", [FT_FF, SEQ], F32R, R)
        act_lo = sb("act_lo", [FT_FF, SEQ], F32R, R + 43008)
        F = R + 86016
        gate = sb("gate", [2, 2, SEQ + 2], F32, F)
        conv = sb("conv", [2, 2, SEQ], F32, F + 4128)
        gelu = sb("gelu", [2, 2, SEQ], F32, F + 8224)
        act32 = sb("act32", [2, 2, SEQ], F32, F + 12320)
        ffill = sb("ffill", [2, 4, SEQ], F32, F)
        y_fin = sb("y_fin", [TT, D], F32, 65536)
        x_fin = sb("x_fin", [TT, D], F32, 81920)
        g_fin = sb("g_fin", [D], F32, F)

        acc = [ctx.enter_context(nc.psum_tensor(f"acc{i}", [P, 1024], F32)) for i in range(2)]
        js = [ctx.enter_context(nc.psum_tensor(f"job{i}", [P, 1024], F32)) for i in range(2)]
        kx_d = nc.dram_tensor("kx_scratch", (4, P, 1024), F32, kind="Internal").ap()
        vx_d = nc.dram_tensor("vx_scratch", (4, P, 1024), F32, kind="Internal").ap()

        sems = {}

        def S_(name):
            if name not in sems:
                sems[name] = ctx.enter_context(nc.semaphore(name))
            return sems[name]

        raw_loaded = [S_(f"raw_loaded{j}") for j in range(4)]
        rawd_loaded = [S_(f"rawd_loaded{j}") for j in range(RAW_D)]
        hi_ready, lo_ready, used = S_("hi_ready"), S_("lo_ready"), S_("used")
        evac_done = S_("evac_done")
        job_full, job_free = [S_("job_full0"), S_("job_full1")], [S_("job_free0"), S_("job_free1")]
        xh_ready, xl_ready = S_("xh_ready"), S_("xl_ready")
        kv_stored = [S_("kv_stored0"), S_("kv_stored1")]
        JOB = {tuple(s): n for steps in (mix_steps, cross_steps, ffn_steps) for n, *s in steps if n is not None}
        FREE_AT = {0: 0, 1: B_WK, 2: B_OUT, 3: B_WQ, 4: B_WO, 5: B_UP}

        def fill_buf(f, i):
            return (fill_tmp if f < 2 else xfill if f == 3 else ffill)[:, i % 2]

        def produced(eng, *step):
            n = JOB[step]
            eng.wait_ge(job_full[n % 2], n // 2 + 1)

        def consumed(eng, *step):
            n = JOB[step]
            eng.wait_ge(job_free[n % 2], n // 2 + 1)

        G_COL = {0: 0, 1: 16, 3: 32, 5: 48}
        C_W0, C_A0, C_KK, C_KA, C_RK, C_LNW, C_LNB = (64 + 8 * i for i in range(7))
        CB_MU, CB_CB, CB_POS = 0, 27, 96
        N_PACK = 14
        block = ctx.enter_context(nc.Block())

        def job_wait_full(eng, n):
            eng.wait_ge(job_full[n % 2], n // 2 + 1)
            return js[n % 2]

        def half(c):
            return slice(64, 128) if c % 2 == 0 else slice(0, 64)

        def b_part(c):
            return 1 if c % 2 == 0 else 0

        @block.sync
        def _(sp):
            xv = a["x"].rearrange("b (t p) d -> p (b t) d", p=P)
            sp.dma_start(rows0[:, 0], xv[:, 0]).then_inc(S_("x_loaded0"), 16)
            sp.wait_ge(S_("pack_zero"), 1)
            sp.dma_start(pack[0:KT, 0, :], a["norm_mix_pre"].rearrange("l (f p) -> (l f) p", p=P)).then_inc(S_("gain_loaded"), 16)
            sp.dma_start(rows0[:, 1], xv[:, 1]).then_inc(S_("x_loaded1"), 16)

            w_in = a["w_in"]
            src = {}
            for i in range(3):
                src[B_SWA + i] = (w_in, N_RWKV + 512 * i, 512)
            src[B_LORA] = (w_in, 3 * RW, NLORA_W + NLORA_A + NLORA_G)
            for i in range(6):
                src[B_RKV + i] = (w_in, 512 * i, 512)
            for i in range(4):
                src[B_WK + i] = (a["wk_x"], 512 * i, 512)
                src[B_WV + i] = (a["wv_x"], 512 * i, 512)
                src[B_WQ + i] = (a["wq_x"], 512 * i, 512)

            def load(g, j, w, c0, n):
                if not (isinstance(g, int) and g == 0):
                    sp.wait_ge(lo_ready, g * HU + (2 * j + 2 - HU))
                sp.dma_start(raw[:, j, :, 0:n],
                             w[0, j * 512:(j + 1) * 512, bass.ds(c0, n)].rearrange("(k p) n -> p k n", p=P)
                             ).then_inc(raw_loaded[j], 16)

            for g in range(B_OUT):
                for j in range(4):
                    load(g, j, *src[g])
            for g0, w in ((B_OUT, a["w_out"]), (B_WQ, a["wq_x"]), (B_WO, a["wo_x"])):
                with sp.Fori(0, 4) as b:
                    for j in range(4):
                        load(b + g0, j, w, b * 512, 512)
            with sp.Fori(0, N_UP) as b:
                for j in range(4):
                    sp.wait_ge(lo_ready, (b + B_UP) * HU + (2 * j + 2 - HU))
                    for part in range(2):
                        sp.dma_start(raw[:, j, :, part * 256:part * 256 + 256],
                                     a["w_up"][0, j * 512:(j + 1) * 512, bass.ds(b * 256 + part * DFF, 256)]
                                     .rearrange("(k p) n -> p k n", p=P)).then_inc(raw_loaded[j], 16)

            def load_down(b, k, first):
                if first:
                    sp.wait_ge(lo_ready, Q_DOWN - HU + 2 * (k // 2) + 2)
                else:
                    sp.wait_ge(lo_ready, b * HD_DOWN + (Q_DOWN + k - RAW_D + 1))
                sp.dma_start(raw_d[:, k % RAW_D],
                             a["w_down"][0, k * 256:(k + 1) * 256, bass.ds(b * 512, 512)]
                             .rearrange("(k p) n -> p k n", p=P)).then_inc(rawd_loaded[k % RAW_D], 16)

            for k in range(HD_DOWN):
                load_down(0, k, k < RAW_D)
            with sp.Fori(1, N_DOWN) as b:
                for k in range(HD_DOWN):
                    load_down(b, k, False)
            ov = out.rearrange("b (t p) d -> p (b t) d", p=P)
            for c in range(4):
                sp.wait_ge(S_("result"), TT * (c + 1))
                cs = slice(512 * c, 512 * c + 512)
                sp.dma_start(ov[:, :, cs], x_fin[:, :, cs]).then_inc(S_("result_stored"), 16)
            sp.wait_ge(S_("result_stored"), 16 * 4)

        @block.gpsimd
        def _(pool):
            nc.gpsimd.memset(pack[:], 0.0).then_inc(S_("pack_zero"), 1)
            pool.wait_ge(S_("pack_zero"), 1)
            nc.gpsimd.memset(ident[:], 0.0).then_inc(S_("ident_zero"), 1)
            pool.wait_ge(S_("ident_zero"), 1)
            nc.gpsimd.affine_select(out=ident[:], in_=ident[:], compare_op=ALU.not_equal, fill=1.0, base=0,
                                    pattern=[[-1, P]], channel_multiplier=1).then_inc(S_("ident_ready"), 1)

            def vec(name, rows, t, row):
                pool.dma_start(pack[row:row + rows, t, :],
                               a[name].rearrange("l (f p) -> (l f) p", p=P)).then_inc(S_("pack_loaded"), 16)

            n = 1
            for f, name in ((3, "norm_cross_pre"), (5, "norm_ffn_pre")):
                vec(name, 16, 0, G_COL[f])
                n += 1
            pool.dma_start(pack[16:32, 0, :], a["mem_norm"].rearrange("(f p) -> f p", p=P)).then_inc(S_("pack_loaded"), 16)
            for name, c in (("w0", C_W0), ("a0", C_A0), ("k_k", C_KK), ("k_a", C_KA), ("ln_x_w", C_LNW), ("ln_x_b", C_LNB)):
                vec(name, 8, 0, c)
                n += 1
            pool.dma_start(pack[C_RK:C_RK + 8, 0, :], a["r_k"].rearrange("l (f h) d -> (l f) (h d)", h=2)).then_inc(S_("pack_loaded"), 16)
            pool.dma_start(pack[0:26, 1, :], a["shift_mu"][:, 0:26 * P].rearrange("l (f p) -> (l f) p", p=P)).then_inc(S_("pack_loaded"), 16)
            pool.dma_start(pack[26:27, 1, 0:32], a["shift_mu"][:, 26 * P:26 * P + 32]).then_inc(S_("pack_loaded"), 16)
            vec("conv_b", FT_FF, 1, CB_CB)
            pool.dma_start(pack[0:3 * FT_FF, 2, :], a["conv_w"].rearrange("l w (f p) -> (l w f) p", p=P)).then_inc(S_("pack_loaded"), 16)
            pool.dma_start(pos_i[96:98, :], a["positions"].rearrange("b (t p) -> (b t) p", p=P)).then_inc(S_("pos_loaded"), 16)
            pool.dma_start(sink[:], a["attn_sinks"].partition_broadcast(P).rearrange("q l n -> q (l n)")).then_inc(S_("sink_loaded"), 16)
            n += 5
            assert n == N_PACK
            marks = S_("mask_step")
            cnt = [0]

            def mark(ins):
                cnt[0] += 1
                ins.then_inc(marks, 1)
                pool.wait_ge(marks, cnt[0])

            def pick(ap, pattern, op, base_, cm, fill):
                mark(nc.gpsimd.affine_select(out=ap, in_=ap, compare_op=op, fill=fill, base=base_,
                                             pattern=pattern, channel_multiplier=cm))

            mark(nc.gpsimd.memset(hones[:], 0.0))
            mark(nc.gpsimd.memset(mask_sc[:], 1.0))
            mark(nc.gpsimd.memset(mask_low[:], -1.0))
            mark(nc.gpsimd.memset(lvl_x[:], 0.0))
            mark(nc.gpsimd.memset(lvl_t[:], 0.0))
            mark(nc.gpsimd.memset(eye[:], 0.0))
            for hh in range(2):
                h = slice(64 * hh, 64 * hh + 64)
                mark(nc.gpsimd.memset(hones[h, 64 * hh:64 * hh + 64], 1.0))
                pick(eye[h], [[-1, CH]], ALU.not_equal, 0, 1, 1.0)
                pick(mask_sc[h, 0], [[1, CH]], ALU.is_gt, 0, -1, 0.0)
                pick(mask_sc[h, 1], [[1, CH]], ALU.is_ge, 0, -1, 0.0)
                pick(mask_low[h], [[-1, CH]], ALU.is_gt, 0, 1, 0.0)
                for i in range(6):
                    b = 1 << i
                    n2 = CH // (2 * b)
                    v = lvl_x[h, i].rearrange("p (n h b) -> p n h b", h=2, b=b)[:, :, 1]
                    sgn = -1.0 if i == 0 else 1.0
                    mark(nc.gpsimd.memset(v, sgn))
                    pick(v, [[-2 * b, n2], [0, b]], ALU.is_ge, 0, 1, 0.0)
                    pick(v, [[2 * b, n2], [0, b]], ALU.is_ge, b - 1, -1, 0.0)
                    if i < 5:
                        v = lvl_t[h, i].rearrange("p (n h b) -> p n h b", h=2, b=b)[:, :, 0]
                        mark(nc.gpsimd.memset(v, 1.0))
                        pick(v, [[-2 * b, n2], [0, b]], ALU.is_ge, -b, 1, 0.0)
                        pick(v, [[2 * b, n2], [0, b]], ALU.is_ge, 2 * b - 1, -1, 0.0)
            mark(nc.gpsimd.memset(reset[:], 1.0))
            nc.gpsimd.memset(reset[:].rearrange("p (c t) -> p c t", t=CH)[:, :, 0:1], 0.0).then_inc(S_("masks"), 1)

            produced(pool, "fill", 0, 2)
            produced(pool, "fill", 0, 3)
            mv = a["mem"].rearrange("b (t p) d -> p (b t) d", p=P)
            for j in range(TT):
                pool.dma_start(rows0[:, j], mv[:, j]).then_inc(S_(f"mem_loaded{j}"), 16)
            for G in range(4):
                c = slice(256 * G, 256 * G + 256)
                if G:
                    produced(pool, "lora_wa", G - 1)
                pool.dma_start(lora_w[0:64, 0], a["w_lora_up"][0, :, c]).then_inc(S_("wa_loaded"), 16)
                pool.dma_start(lora_w[64:128, 0], a["a_lora_up"][0, :, c]).then_inc(S_("wa_loaded"), 16)
                if G:
                    produced(pool, "lora_g", G - 1)
                pool.dma_start(lora_w[:, 1], a["g_lora_up"][0, 0:128, c]).then_inc(S_("g_loaded"), 16)
                pool.dma_start(lora_w[0:32, 2], a["g_lora_up"][0, 128:160, c]).then_inc(S_("g_loaded"), 16)
            pool.wait_ge(S_("yt_ready"), 4)
            for i in range(2):
                pool.wait_ge(kv_stored[i], 16 * 4)
            xv = a["x"].rearrange("b (t p) d -> p (b t) d", p=P)
            pool.dma_start(x_res[:], xv).then_inc(S_("xres_loaded"), 16)
            pool.dma_start(g_post[:], a["norm_mix_post"][0].partition_broadcast(P)).then_inc(S_("gpost_loaded"), 16)
            for b in range(4):
                pool.dma_start(kx[:, 4 * b:4 * b + 4, :], kx_d[b].rearrange("p (f m) -> p f m", f=4)).then_inc(S_("kv_loaded"), 16)
                pool.dma_start(vx[:, :, b, :], vx_d[b].rearrange("p (t n) -> p t n", t=2)).then_inc(S_("kv_loaded"), 16)
            pool.wait_ge(evac_done, B_WQ)
            pool.dma_start(g_post[:], a["norm_cross_post"][0].partition_broadcast(P)).then_inc(S_("gpost_loaded"), 16)
            pool.wait_ge(S_("xres_ready"), 16)
            pool.dma_start(out.rearrange("b (t p) d -> p (b t) d", p=P), x_res[:]).then_inc(S_("x2_stored"), 16)
            pool.wait_ge(S_("x2_stored"), 16)
            pool.wait_ge(used, Q_DOWN)
            pool.dma_start(x_fin[:], out.rearrange("b (t p) d -> p (b t) d", p=P)).then_inc(S_("x2_loaded"), 16)
            pool.wait_ge(S_("actl_ready"), N_UP)
            pool.dma_start(g_fin[:], a["norm_ffn_post"][0].partition_broadcast(P)).then_inc(S_("gpost_loaded"), 16)

        @block.scalar
        def _(act):
            A = nc.scalar.activation

            def w_high(q, g, k, n=512, up=False):
                j = k // 2
                if up:
                    act.wait_ge(raw_loaded[j], g * 32 + (32 - 16 * B_UP))
                else:
                    act.wait_ge(raw_loaded[j], g * 16 + 16)
                if not (isinstance(q, int) and q < SLOTS):
                    act.wait_ge(used, q + (1 - SLOTS))
                A(w_hi[:, k % SLOTS, :, 0:n], raw[:, j, 2 * (k % 2):2 * (k % 2) + 2, 0:n], ACT.Copy).then_inc(hi_ready, 1)

            def w_high_down(b, m):
                act.wait_ge(rawd_loaded[m % RAW_D], b * 48 + 16 * (m // RAW_D + 1))
                act.wait_ge(used, b * HD_DOWN + (Q_DOWN - 2 + m))
                A(w_hi[:, m % SLOTS_D], raw_d[:, m % RAW_D], ACT.Copy).then_inc(hi_ready, 1)

            def width(g):
                return 288 if g == B_LORA else 512

            def lead(g, k):
                g2, k2 = (g, k + 3) if k + 3 < HU else (g + 1, k + 3 - HU)
                w_high(g2 * HU + k2, g2, k2, width(g2), g2 >= B_UP)

            def rows_squares(dst, b, par):
                for j in range(TT):
                    A(dst[:, j, bass.ds(b * 512, 512)], acc[par][:, j * 512:j * 512 + 512], ACT.Square,
                      accum_out=ssq[:, j, bass.ds(b, 1)]).then_inc(S_("squared"), 1)

            def evac(g):
                p = acc[g % 2]
                act.wait_ge(used, HU * (g + 1))
                if g < B_SWA + 2:
                    A(zq[:, :, 8 * g:8 * g + 8, :].rearrange("p t h d -> p t (h d)"),
                      p[:].rearrange("p (t n) -> p t n", t=TT), ACT.Copy).then_inc(evac_done, 1)
                elif g == B_SWA + 2:
                    pv = p[:].rearrange("p (t n) -> p t n", t=TT)
                    A(zq[:, :, 16:20, :].rearrange("p t h d -> p t (h d)"), pv[:, :, 0:256], ACT.Copy)
                    act.wait_ge(S_("vwin_zero"), 1)
                    for c, rows, t in ((1, slice(0, 128), 0), (3, slice(0, 128), 1), (0, slice(0, 64), 0),
                                       (2, slice(0, 64), 1), (2, slice(64, 128), 0)):
                        last = A(v_win[rows, c].rearrange("p g d -> p (g d)"), pv[rows, t, 256:512], ACT.Copy)
                    last.then_inc(evac_done, 1)
                elif g < B_WK:
                    if g == B_LORA:
                        act.wait_ge(S_("stage_zero"), 1)
                    if g >= B_LORA + 2:
                        act.wait_ge(S_("shifted"), g - B_LORA - 1)
                    A(stage[:, g % 2, 0:nf(g), 1:SEQ + 1],
                      p[:, 0:nf(g) * SEQ].rearrange("p (f t) -> p f t", t=SEQ), ACT.Copy).then_inc(evac_done, 1)
                elif g < B_OUT:
                    i = g - B_WK
                    if i >= 2:
                        act.wait_ge(kv_stored[i % 2], 16 * (i // 2))
                    st = fill_tmp[:, g % 2]
                    A(st.rearrange("p f t -> p (f t)"), p[:], ACT.Copy).then_inc(evac_done, 1)
                    act.wait_ge(evac_done, g + 1)
                    act.dma_start(kx_d[i] if i < 4 else vx_d[i - 4],
                                  st.rearrange("p f t -> p (f t)")).then_inc(kv_stored[i % 2], 16)
                elif B_WQ <= g < B_WO:
                    i = g - B_WQ
                    A(y_T[:, 4 * i:4 * i + 4].rearrange("p f t -> p (f t)"), p[:], ACT.Copy).then_inc(evac_done, 1)

            def nf(g):
                return 3 if g == B_LORA else 4

            def preload(name):
                nc.scalar.preload_act_table_set(name)

            logs = [0]

            def log_exp(t, name):
                logs[0] += 1
                A(t, t, ACT.Ln).then_inc(S_("log_ready"), 1)
                act.wait_ge(S_("log_ready"), logs[0])
                A(t, t, ACT.Exp, scale=-0.5).then_inc(S_(name), 1)

            def stat_root(i, name):
                act.wait_ge(S_(name + "_ms"), 1)
                log_exp(stat[:, i], name + "_inv")

            def row_squares(rows, k, name):
                for j in range(TT):
                    act.wait_ge(S_(f"{name}_loaded{j}"), 16)
                    A(junk[:], rows[:, j], ACT.Square, accum_out=ssq[:, j, k:k + 1]).then_inc(S_(name + "_ssq"), 1)
                    act.wait_ge(S_(name + "_ssq"), j + 1)

            def scale_rows(dst, src, i, name):
                act.wait_ge(S_(name + "_inv"), 1)
                for c in range(4):
                    A(dst[:, 1, 512 * c:512 * c + 512], src[:, 1, 512 * c:512 * c + 512], ACT.Copy,
                      scale=stat[:, i, 1:2]).then_inc(S_(name + "_rows1"), 1)

            preload("natural_log_exp_and_others")
            row_squares(rows0, 0, "x")
            stat_root(0, "x")
            scale_rows(rows0, rows0, 0, "x")
            w_high(0, 0, 0)
            w_high(1, 0, 1)

            def fill_high(f, i, src):
                if i == 0 and f:
                    act.wait_ge(used, HU * FREE_AT[f])
                consumed(act, "fill", f, i)
                A(x_hi[:, 4 * i:4 * i + 4].rearrange("p f t -> p (f t)"), src.rearrange("p f t -> p (f t)"), ACT.Copy).then_inc(xh_ready, 1)

            def swa(n, s):
                if s[0] == "swa_scores":
                    p = job_wait_full(act, n)
                    g, j = s[1:]
                    m = 2 * g + j
                    if g:
                        produced(act, "swa_pT", g - 1, j)
                    else:
                        consumed(act, "swa_kT")
                    A(prob[:, j].rearrange("p (h f) k -> p h (f k)", h=2),
                      p[:].rearrange("p (h n) -> p h n", h=2)[:, :, 0:256], ACT.Copy, scale=HD ** -0.5).then_inc(job_free[n % 2], 1)
                    act.wait_ge(S_("s_shift"), m + 1)
                    A(prob[:, j], prob[:, j], ACT.Exp).then_inc(S_("s_exp"), 1)
                    A(soft[:, 2], soft[:, 1], ACT.Exp).then_inc(S_("s_exp"), 1)
                elif s[0] == "swa_pT":
                    p = job_wait_full(act, n)
                    g, j = s[1:]
                    if g:
                        produced(act, "swa_out", g - 1, j)
                    A(prob_T[:, j].rearrange("p h t -> p (h t)"), p[:, 0:512], ACT.Copy).then_inc(job_free[n % 2], 1)

            def rwkv(n, s):
                what, G = s[0], s[1]
                if what == "lora_wa":
                    preload("sigmoid_and_others")
                    p = job_wait_full(act, n)
                    if G >= 2:
                        act.wait_ge(S_("yt_ready"), G - 1)
                    for f in range(2):
                        A(decay[:, f], p[:, f * 256:f * 256 + 256], ACT.Sigmoid, bias=colA[:, C_W0 + 2 * G + f:C_W0 + 2 * G + f + 1])
                        last = A(rate[:, f], p[:, 512 + f * 256:768 + f * 256], ACT.Sigmoid, bias=colA[:, C_A0 + 2 * G + f:C_A0 + 2 * G + f + 1])
                    last.then_inc(job_free[n % 2], 1)
                elif what == "lora_g":
                    p = job_wait_full(act, n)
                    act.wait_ge(S_("kr_ready"), min(G + 2, 4))
                    A(gate_g[:].rearrange("p f t -> p (f t)"), p[:, 0:512], ACT.Copy).then_inc(job_free[n % 2], 1)
                elif what == "kk_norm":
                    preload("natural_log_exp_and_others")
                    consumed(act, *s)
                    log_exp(inv_norm[:], "kk_rt")
                elif what == "prep_k":
                    if G == 0:
                        produced(act, "swa_qT", 3)
                    act.wait_ge(S_("cum_ready"), G + 1)
                    A(decay[:], decay[:], ACT.Exp).then_inc(S_("exp_ready"), 1)
                    A(exp_neg[:], cum[:], ACT.Exp, scale=-1.0).then_inc(S_("exp_ready"), 1)
                    act.wait_ge(S_("exp_ready"), 3 * G + 2)
                    A(cum[:], cum[:], ACT.Exp).then_inc(S_("exp_ready"), 1)
                elif what == "bk_rows":
                    p = job_wait_full(act, n)
                    A(bk_rows[:].rearrange("p f c n -> p (f c n)"), p[:], ACT.Copy).then_inc(job_free[n % 2], 1)
                elif what == "inv_p":
                    p = job_wait_full(act, n)
                    for i in range(2):
                        h = slice(64 * i, 64 * i + 64)
                        last = A(inv_p[h].rearrange("p a b c d -> p (a b c d)"), p[h, 512 * i:512 * i + 512], ACT.Copy)
                    last.then_inc(job_free[n % 2], 1)
                elif what == "scan_x":
                    p = job_wait_full(act, n)
                    h = half(s[2])
                    A(xs[h].rearrange("p (f i) d -> p i f d", i=2),
                      p[h].rearrange("p (i n) -> p i n", i=2)[:, :, 0:P].rearrange("p i (f d) -> p i f d", f=2),
                      ACT.Copy, scale=-1.0).then_inc(job_free[n % 2], 1)
                elif what == "scan_u":
                    p = job_wait_full(act, n)
                    h = half(s[2])
                    A(uv[h, s[2]].rearrange("p i d -> p (i d)"), p[h, 0:256], ACT.Copy).then_inc(job_free[n % 2], 1)
                elif what == "gn_var":
                    consumed(act, *s)
                    log_exp(rstd[:], "gn_rt")

            def cross(n, s):
                h = s[1]
                if s[0] == "x_scores":
                    act.wait_ge(S_("x_max"), h + 1)
                    if h >= 2:
                        produced(act, "x_pT", h - 2)
                    p = js[n % 2]
                    for j in range(TT):
                        last = A(xp[:, h % 2, j], p[:, j * 256:j * 256 + 256], ACT.Exp, bias=stat[:, 6, j:j + 1],
                                 scale=XHD ** -0.5, accum_out=stat[:, 7, j:j + 1])
                    last.then_inc(job_free[n % 2], 1)
                elif s[0] == "x_pT":
                    p = job_wait_full(act, n)
                    if h >= 2:
                        produced(act, "x_out", h - 2)
                    A(xp_T[:, h % 2].rearrange("p m t -> p (m t)"), p[:, 0:512], ACT.Copy).then_inc(job_free[n % 2], 1)
                elif s[0] == "x_out":
                    p = job_wait_full(act, n)
                    A(y_T[:, 4 * h:4 * h + 4].rearrange("p f t -> p (f t)"), p[:], ACT.Copy).then_inc(job_free[n % 2], 1)

            def walk(steps):
                for n, *s in steps:
                    if s[0] == "hu":
                        g, k = s[1:]
                        lead(g, k)
                        if k == HU - 1:
                            evac(g)
                            if g == B_LORA:
                                preload("sigmoid_and_others")
                                act.wait_ge(S_("shifted"), 1)
                                A(lora[0:64, 0], lora[0:64, 0], ACT.Tanh).then_inc(S_("lora_act"), 1)
                                A(lora[:, 1], lora[:, 1], ACT.Sigmoid).then_inc(S_("lora_act"), 1)
                                A(lora[0:32, 2], lora[0:32, 2], ACT.Sigmoid).then_inc(S_("lora_act"), 1)
                    elif s[0] == "mem_sq":
                        row_squares(rows0, 1, "mem")
                    elif s[0] == "mem_scale":
                        stat_root(1, "mem")
                        scale_rows(rows0, rows0, 1, "mem")
                    elif s[0] == "angles":
                        act.wait_ge(S_("ang_ready"), 1)
                        A(trig[:].rearrange("p a t i -> p (a t i)"), ang[:, 1:3].rearrange("p a t i -> p (a t i)"), ACT.Sin).then_inc(S_("trig_ready"), 1)
                        preload("natural_log_exp_and_others")
                    elif s[0] == "fill":
                        f, i = s[1:]
                        fill_high(f, i, fill_buf(f, i))
                        if (f, i) == (0, 0):
                            w_high(2, 0, 2)
                    elif s[0] == "fill_T":
                        f, i = s[1:]
                        if i == 0:
                            act.wait_ge(used, HU * FREE_AT[f])
                            if f == 2:
                                act.wait_ge(S_("yt_ready"), 4)
                            else:
                                consumed(act, "x_out", XHEADS - 1)
                        A(x_hi[:, 4 * i:4 * i + 4].rearrange("p f t -> p (f t)"),
                          y_T[:, 4 * i:4 * i + 4].rearrange("p f t -> p (f t)"), ACT.Copy).then_inc(xh_ready, 1)
                    elif s[0].startswith("swa"):
                        swa(n, s)
                    elif s[0].startswith("x_"):
                        cross(n, s)
                    elif s[0] not in ("gain", "params", "rope"):
                        rwkv(n, s)

            def residual(i):
                stat_root(2 + i, f"post{i}")
                if i < 2:
                    for c in range(4):
                        for j in range(TT):
                            act.wait_ge(S_("xres_ready"), 8 * i + 2 * c + j + 1)
                            last = A(y_rows[:, j, 512 * c:512 * c + 512], x_res[:, j, 512 * c:512 * c + 512], ACT.Square,
                                     accum_out=ssq[:, j, c:c + 1])
                    last.then_inc(S_(f"pre{i}_ssq"), 1)
                    stat_root(5, f"pre{i}")
                    scale_rows(y_rows, x_res, 5, f"pre{i}")

            def loop_rows(g0):
                with act.Fori(0, 2) as b2:
                    for r in range(2):
                        for k in range(HU):
                            g2, k2 = (r, k + 3) if k + 3 < HU else (r + 1, k + 3 - HU)
                            if not (r == 1 and k + 3 >= HU):
                                w_high(b2 * (2 * HU) + ((g0 + g2) * HU + k2), b2 * 2 + (g0 + g2), k2)
                            elif g0 == B_OUT:
                                w_high(b2 * (2 * HU) + ((g0 + g2) * HU + k2), b2 * 2 + (g0 + g2), k2)
                            else:
                                act.wait_ge(raw_loaded[k2 // 2], b2 * (16 * 3) + 16 * (B_WO + 3))
                                act.wait_ge(used, b2 * (2 * HU) + ((g0 + g2) * HU + k2 + 1 - SLOTS))
                                A(w_hi[:, k2 % SLOTS], raw[:, k2 // 2, 2 * (k2 % 2):2 * (k2 % 2) + 2], ACT.Copy).then_inc(hi_ready, 1)
                        act.wait_ge(used, b2 * (2 * HU) + (g0 + r + 1) * HU)
                        rows_squares(y_rows, b2 * 2 + r, (g0 + r) % 2)

            walk(mix_steps)
            loop_rows(B_OUT)
            residual(0)
            walk(cross_steps)
            loop_rows(B_WO)
            residual(1)
            walk(ffn_steps)

            def up_step(i, r, last):
                for k in range(HU):
                    if not (last and k + 3 >= HU):
                        g2, k2 = (0, k + 3) if k + 3 < HU else (1, k + 3 - HU)
                        w_high(i * HU + ((B_UP + g2) * HU + k2), i + (B_UP + g2), k2, 512, True)
                    if k == 2:
                        act.wait_ge(S_("conv_ready"), i)
                        A(gelu[:, 1 - r], conv[:, 1 - r], ACT.Gelu).then_inc(S_("gelu_ready"), 1)
                    if k == 5:
                        act.wait_ge(evac_done, i + B_UP)
                        A(act_hi[:, bass.ds(i * 2 - 2, 2)], act32[:, 1 - r], ACT.Copy).then_inc(S_("acth_ready"), 1)
                if last:
                    w_high_down(0, 0)
                    w_high_down(0, 1)
                gate_out(i, r)

            def gate_out(i, r):
                act.wait_ge(used, i * HU + (B_UP + 1) * HU)
                A(gate[:, r, :, 2:SEQ + 2], acc[(B_UP + r) % 2][:, 0:512].rearrange("p (f t) -> p f t", f=2), ACT.Copy).then_inc(S_("gate_ready"), 1)

            preload("gelu_and_others")
            act.wait_ge(S_("gate_zero"), 1)
            act.wait_ge(S_("x2_stored"), 16)
            gate_out(0, 0)
            up_step(1, 1, False)
            with act.Fori(1, (N_UP - 1) // 2) as i2:
                up_step(i2 * 2, 0, False)
                up_step(i2 * 2 + 1, 1, False)
            up_step(N_UP - 1, 0, True)
            w_high_down(0, 2)
            w_high_down(0, 3)
            act.wait_ge(S_("conv_ready"), N_UP)
            A(gelu[:, 0], conv[:, 0], ACT.Gelu).then_inc(S_("gelu_ready"), 1)
            w_high_down(0, 4)
            act.wait_ge(evac_done, B_DOWN)
            A(act_hi[:, FT_FF - 2:FT_FF], act32[:, 0], ACT.Copy).then_inc(S_("acth_ready"), 1)
            w_high_down(0, 5)

            preload("natural_log_exp_and_others")

            def down_pair(b, last):
                for r in range(2):
                    for m in range(2 if r else AHEAD, HD_DOWN):
                        w_high_down(b + r, m)
                    if not (last and r):
                        w_high_down(b + (r + 1), 0)
                        w_high_down(b + (r + 1), 1)
                    act.wait_ge(used, b * HD_DOWN + (Q_DOWN + (r + 1) * HD_DOWN))
                    rows_squares(y_fin, b + r, (B_DOWN + r) % 2)
                if not last:
                    for m in range(2, AHEAD):
                        w_high_down(b + 2, m)

            with act.Fori(0, N_DOWN // 2 - 1) as b2:
                down_pair(b2 * 2, False)
            down_pair(N_DOWN - 2, True)
            residual(2)

        @block.vector
        def _(dve):
            V = nc.vector
            chain, counts = [0], {}

            def link(ins):
                chain[0] += 1
                ins.then_inc(S_("dve_chain"), 1)
                dve.wait_ge(S_("dve_chain"), chain[0])

            def give(ins, name):
                counts[name] = counts.get(name, 0) + 1
                ins.then_inc(S_(name), 1)
                dve.wait_ge(S_(name), counts[name])

            def free_job(ins, n):
                ins.then_inc(job_free[n % 2], 1)
                dve.wait_ge(job_free[n % 2], n // 2 + 1)

            def w_low(q, k, n=512):
                dve.wait_ge(hi_ready, q + 1)
                V.tensor_tensor(w_lo[:, k % SLOTS, :, 0:n], raw[:, k // 2, 2 * (k % 2):2 * (k % 2) + 2, 0:n],
                                w_hi[:, k % SLOTS, :, 0:n].bitcast(F32), ALU.subtract).then_inc(lo_ready, 1)

            def w_low_down(b, m):
                dve.wait_ge(hi_ready, b * HD_DOWN + (Q_DOWN + m + 1))
                V.tensor_tensor(w_lo[:, m % SLOTS_D], raw_d[:, m % RAW_D],
                                w_hi[:, m % SLOTS_D].bitcast(F32), ALU.subtract).then_inc(lo_ready, 1)

            def bc(t, shape):
                return t.broadcast_to(shape)

            def mean_square(i, sums, name):
                give(V.tensor_scalar(stat[:, i], sums, 1.0 / D, RMS_EPS, ALU.mult, ALU.add), name + "_ms")

            def scale_rows(dst, src, i, name):
                dve.wait_ge(S_(name + "_inv"), 1)
                for c in range(4):
                    V.tensor_scalar(dst[:, 0, 512 * c:512 * c + 512], src[:, 0, 512 * c:512 * c + 512],
                                    stat[:, i, 0:1], None, ALU.mult).then_inc(S_(name + "_rows0"), 1)

            def fill(n, f, i):
                p = job_wait_full(dve, n)
                if i >= 2:
                    dve.wait_ge(xh_ready, 4 * f + i - 1)
                gain = colA[:, G_COL[f] + 4 * i:G_COL[f] + 4 * i + 4].unsqueeze(2)
                free_job(V.tensor_tensor(fill_buf(f, i), p[:].rearrange("p (f t) -> p f t", f=4),
                                         bc(gain, [P, 4, SEQ]), ALU.mult), n)
                low_fill(f, i, fill_buf(f, i))

            def low_fill(f, i, src):
                dve.wait_ge(xh_ready, 4 * f + i + 1)
                V.tensor_tensor(x_lo[:, 4 * i:4 * i + 4], src, x_hi[:, 4 * i:4 * i + 4].bitcast(F32),
                                ALU.subtract).then_inc(xl_ready, 1)

            def angles():
                c1, rest = 6.28125, 2 * math.pi - 6.28125
                c2 = math.floor(rest * 2.0 ** 17) / 2.0 ** 17
                c3 = math.floor((rest - c2) * 2.0 ** 26) / 2.0 ** 26
                c4 = rest - c2 - c3
                for i in range(8):
                    last = V.memset(ang[:, 5, 0, i:i + 1], INV_FREQ[i])
                link(last)
                for t in range(TT):
                    last = V.tensor_scalar(ang[:, 0, t], ang[:, 5, 0], colB[:, CB_POS + t:CB_POS + t + 1], None, ALU.mult)
                link(last)
                for m, turn, off in ((1, 0.25, math.pi / 2), (2, 0.0, 0.0)):
                    r, q = ang[:, m], ang[:, 2 + m]
                    link(V.tensor_scalar(q, ang[:, 0], 1 / (2 * math.pi), turn, ALU.mult, ALU.add))
                    link(V.tensor_scalar(q, q, 12582912.0, 12582912.0, ALU.add, ALU.subtract))
                    link(V.scalar_tensor_tensor(r, q, -c1, ang[:, 0], ALU.mult, ALU.add))
                    for c in (c2, c3, c4):
                        link(V.scalar_tensor_tensor(r, q, -c, r, ALU.mult, ALU.add))
                    link(V.tensor_scalar(r, r, off, 3.1415925, ALU.add, ALU.min))
                    ins = V.tensor_scalar(r, r, -3.1415925, None, ALU.max)
                    if m == 1:
                        link(ins)
                give(ins, "ang_ready")

            def rope_q_k():
                dve.wait_ge(evac_done, B_LORA)
                dve.wait_ge(S_("trig_ready"), 1)
                for j in range(TT):
                    t1, t2 = zq[:, j, 0:20, 0:8], zq[:, j, 0:20, 8:16]
                    cos, sin = (bc(trig[:, m, j].unsqueeze(1), [P, 20, 8]) for m in range(2))
                    for i, (x, y) in enumerate(((t1, cos), (t2, sin), (t2, cos), (t1, sin))):
                        last = V.tensor_tensor(rope[:, i], x, y, ALU.mult)
                    link(last)
                    V.tensor_tensor(t1, rope[:, 0], rope[:, 1], ALU.subtract)
                    link(V.tensor_tensor(t2, rope[:, 2], rope[:, 3], ALU.add))
                for j in range(TT):
                    last = V.tensor_copy(k_dup[:, j], bc(zq[:, j, 16:20].unsqueeze(2), [P, 4, 2, HD]))
                give(last, "kdup_ready")

            def swa(n, s):
                if s[0] == "swa_kT":
                    p = job_wait_full(dve, n)
                    free_job(V.tensor_copy(k_T[:].rearrange("p g t -> p (g t)"), p[:]), n)
                elif s[0] == "swa_qT":
                    p = job_wait_full(dve, n)
                    free_job(V.tensor_copy(q_T[:, s[1] % 2].rearrange("p f t -> p (f t)"), p[:, 0:512]), n)
                elif s[0] == "swa_scores":
                    g, j = s[1:]
                    consumed(dve, *s)
                    pr = prob[:, j]
                    if j == 0:
                        link(V.memset(prob[0:64, 0, :, 64:128], NEG_INF))
                    dve.wait_ge(S_("sink_loaded"), 16)
                    sk = sink[:, 4 * g:4 * g + 4].rearrange("p (f h) -> p h f", h=2)
                    s4 = [soft[:, i] for i in range(5)]
                    link(V.tensor_reduce(s4[0], pr, AX.X, ALU.max))
                    link(V.tensor_tensor(s4[0].rearrange("p (h f) -> p h f", h=2), s4[0].rearrange("p (h f) -> p h f", h=2), sk, ALU.max))
                    V.tensor_tensor(s4[1].rearrange("p (h f) -> p h f", h=2), sk, s4[0].rearrange("p (h f) -> p h f", h=2), ALU.subtract)
                    give(V.tensor_tensor(pr, pr, bc(s4[0].unsqueeze(2), [P, 4, P]), ALU.subtract), "s_shift")
                    dve.wait_ge(S_("s_exp"), 2 * (2 * g + j) + 2)
                    link(V.tensor_reduce(s4[3], pr, AX.X, ALU.add))
                    link(V.tensor_tensor(s4[3], s4[3], s4[2], ALU.add))
                    link(V.reciprocal(s4[3], s4[3]))
                    give(V.tensor_tensor(pr, pr, bc(s4[3].unsqueeze(2), [P, 4, P]), ALU.mult), "s_norm")
                elif s[0] == "swa_out":
                    g, j = s[1:]
                    p = job_wait_full(dve, n)
                    free_job(V.tensor_copy(y_T[:, 8 + 2 * g:10 + 2 * g, j * P:j * P + P],
                                           p[:, 0:256].rearrange("p (f t) -> p f t", f=2)), n)

            def shift(g):
                nf = 3 if g == B_LORA else 4
                f0 = 24 if g == B_LORA else 4 * (g - B_RKV)
                to = f0 if f0 < 8 else f0 + 8
                dst = lora[:] if g == B_LORA else feat[:, to:to + 4]
                dve.wait_ge(evac_done, g + 1)
                now, before = stage[:, g % 2, 0:nf, 1:SEQ + 1], stage[:, g % 2, 0:nf, 0:SEQ]
                link(V.tensor_tensor(dst, before, now, ALU.subtract))
                mu = bc(colB[:, CB_MU + f0:CB_MU + f0 + nf].unsqueeze(2), [P, nf, SEQ])
                link(V.tensor_tensor(dst, dst, mu, ALU.mult))
                give(V.tensor_tensor(dst, dst, now, ALU.add), "shifted")

            def heads(t):
                return t.rearrange("p f (c t) -> p f c t", c=NCH)

            def flat(t):
                return t.rearrange("p f t -> p (f t)")

            def rwkv(n, s):
                what, G = s[0], s[1]
                r, k, v = (feat[:, i + 2 * G:i + 2 * G + 2] for i in (0, 16, 24))
                col = lambda c, f: colA[:, c + 2 * G + f:c + 2 * G + f + 1]
                if what == "prep_kk":
                    if G == 0:
                        dve.wait_ge(S_("masks"), 1)
                    for f in range(2):
                        last = V.tensor_scalar(kk[:, f], k[:, f], col(C_KK, f), None, ALU.mult)
                    link(last)
                    give(V.tensor_tensor(inv_norm[:], kk[:], kk[:], ALU.mult), "kk_sq")
                elif what == "uv_zero":
                    V.memset(uv[64:128, 0:NCH:2], 0.0)
                    give(V.memset(uv[0:64, 1:NCH:2], 0.0), "uv_zero")
                elif what == "kk_norm":
                    p = job_wait_full(dve, n)
                    free_job(V.tensor_scalar(flat(inv_norm[:]), p[:, 0:512], 1e-24, None, ALU.max), n)
                elif what == "prep_decay":
                    if G == 0:
                        produced(dve, "swa_qT", 3)
                    consumed(dve, "lora_wa", G)
                    link(V.tensor_scalar(decay[:], decay[:], -DECAY_SCALE, None, ALU.mult))
                    for f in range(2):
                        last = V.tensor_tensor_scan(cum[:, f], reset[:], decay[:, f], 0.0, ALU.mult, ALU.add)
                    link(last)
                    give(V.tensor_tensor(decay[:], cum[:], decay[:], ALU.subtract), "cum_ready")
                elif what == "prep_k":
                    for f in range(2):
                        last = V.tensor_scalar(k_new[:, f], rate[:, f], -1.0, col(C_KA, f), ALU.add, ALU.mult)
                    link(last)
                    link(V.scalar_tensor_tensor(k_new[:], k_new[:], 1.0, k, ALU.add, ALU.mult))
                elif what == "prep_bonus":
                    for f in range(2):
                        last = V.scalar_tensor_tensor(bonus[G % 2][:, f], r[:, f], col(C_RK, f), k_new[:, f], ALU.mult, ALU.mult)
                    give(last, "bonus_ready")
                    dve.wait_ge(S_("kk_rt"), G + 1)
                    link(V.tensor_tensor(kk[:], kk[:], inv_norm[:], ALU.mult))
                    link(V.tensor_tensor(rate[:], rate[:], kk[:], ALU.mult))
                elif what == "prep_kr":
                    dve.wait_ge(S_("exp_ready"), 3 * G + 3)
                    V.tensor_tensor(kr[G % 2][:, :, :, 0], heads(kk[:]), heads(decay[:]), ALU.mult)
                    V.tensor_tensor(kr[G % 2][:, :, :, 1], heads(r), heads(cum[:]), ALU.mult)
                    link(V.tensor_copy(chunk_decay[:, G % 2], heads(cum[:])[:, :, :, CH - 1]))
                elif what == "prep_bk":
                    if G:
                        produced(dve, "bk_rows", G - 1)
                        produced(dve, "scores", G - 1, 1)
                        produced(dve, "lower", G - 1)
                    for c in range(2):
                        cs = slice(c, NCH, 2)
                        V.tensor_tensor(bk[:, :, cs, b_part(c)], heads(rate[:])[:, :, cs], heads(exp_neg[:])[:, :, cs], ALU.mult)
                        last = V.tensor_tensor(bk[:, :, cs, 1 - b_part(c)], heads(k_new[:])[:, :, cs], heads(exp_neg[:])[:, :, cs], ALU.mult)
                    give(last, "kr_ready")
                elif what == "v_rows":
                    p = job_wait_full(dve, n)
                    pv = p[:, 0:512].rearrange("p (t n) -> p t n", t=TT)
                    V.tensor_copy(uv[0:64, 0:NCH:2].rearrange("p c i d -> p c (i d)"), pv[0:64])
                    free_job(V.tensor_copy(uv[64:128, 1:NCH:2].rearrange("p c i d -> p c (i d)"), pv[64:128]), n)
                elif what == "scores":
                    p = job_wait_full(dve, n)
                    mask = bc(mask_sc[:].rearrange("p m t -> p (m t)").unsqueeze(1), [P, 8, P])
                    free_job(V.tensor_tensor(mx[:, s[2]].rearrange("p h f c n -> p (h f c) n"),
                                             p[:].rearrange("p (i n) -> p i n", i=8), mask, ALU.mult), n)
                elif what == "lower":
                    p = job_wait_full(dve, n)
                    mask = bc(mask_low[:].unsqueeze(1).unsqueeze(1), [P, 2, 2, CH])
                    for hh in range(2):
                        last = V.tensor_tensor(low[:, :, hh], p[:, 512 * hh:512 * hh + 256].rearrange("p (c f s) -> p c f s", c=2, f=2), mask, ALU.mult)
                    free_job(last, n)
                    link(V.tensor_tensor(inv_t[:].rearrange("p a b c d -> p (a b c) d"), low[:].rearrange("p a b c d -> p (a b c) d"),
                                         bc(lvl_t[:, 0].unsqueeze(1), [P, 8, CH]), ALU.mult))
                    tv = inv_t[:].rearrange("p a b c d -> p (a b c) d")
                    link(V.tensor_tensor(tv, tv, bc(eye[:].unsqueeze(1), [P, 8, CH]), ALU.add))
                if what == "scores" and s[2] == 1:
                    for c in range(2):
                        h = half(c)
                        last = V.tensor_tensor(inv_x[h].rearrange("p a b c d -> p (a b c) d"),
                                        mx[h].rearrange("p a b f c n -> p (a b f) c n")[:, :, c, 0:CH],
                                        bc(lvl_x[h, 0].unsqueeze(1), [64, 8, CH]), ALU.mult)
                    link(last)
                    tv = inv_x[:].rearrange("p a b c d -> p (a b c) d")
                    give(V.tensor_tensor(tv, tv, bc(eye[:].unsqueeze(1), [P, 8, CH]), ALU.add), "inv_ready")
                elif what in ("inv_x", "inv_t"):
                    p = job_wait_full(dve, n)
                    i = s[2].bit_length() - 1
                    dst, m = (inv_x, lvl_x) if what == "inv_x" else (inv_t, lvl_t)
                    for q in range(2):
                        h = slice(64 * q, 64 * q + 64)
                        last = V.copy_predicated(dst[h].rearrange("p a b c d -> p (a b c) d"),
                                                 bc(m[h, i].bitcast(I32).unsqueeze(1), [64, 8, CH]),
                                                 p[h, 512 * q:512 * q + 512].rearrange("p (i n) -> p i n", i=8))
                    free_job(last, n)
                elif what == "scan_ys":
                    p = job_wait_full(dve, n)
                    c = s[2]
                    if c < NCH - 1:
                        ps = p[:, 512:640].rearrange("p (f d) -> p f d", f=2)
                        fade = bc(chunk_decay[:, G % 2, :, c:c + 1], [P, 2, HD])
                        if c:
                            link(V.tensor_tensor(state[:], ps, state[:], ALU.add))
                            give(V.tensor_tensor(state[:], state[:], fade, ALU.mult), "state_ready")
                        else:
                            give(V.tensor_tensor(state[:], ps, fade, ALU.mult), "state_ready")
                    free_job(V.tensor_copy(y_grp[:, :, CH * c:CH * c + CH], p[:, 0:128].rearrange("p (f t) -> p f t", f=2)), n)
                elif what == "gn_mean":
                    p = job_wait_full(dve, n)
                    V.scalar_tensor_tensor(flat(y_grp[:]), p[:, 0:512], -1.0 / HD, flat(y_grp[:]), ALU.mult, ALU.add)
                    free_job(V.tensor_tensor(flat(bonus_v[:]), p[:, 512:1024], flat(v), ALU.mult), n)
                    give(V.tensor_tensor(y_sq[:], y_grp[:], y_grp[:], ALU.mult), "gn_sq")
                elif what == "gn_var":
                    p = job_wait_full(dve, n)
                    free_job(V.tensor_scalar(flat(rstd[:]), p[:, 0:512], 1.0 / HD, GN_EPS, ALU.mult, ALU.add), n)
                elif what == "gn_out":
                    dve.wait_ge(S_("gn_rt"), G + 1)
                    link(V.tensor_tensor(y_grp[:], y_grp[:], rstd[:], ALU.mult))
                    for f in range(2):
                        last = V.tensor_scalar(y_grp[:, f], y_grp[:, f], col(C_LNW, f), col(C_LNB, f), ALU.mult, ALU.add)
                    link(last)
                    link(V.tensor_tensor(y_grp[:], y_grp[:], bonus_v[:], ALU.add))
                    consumed(dve, "lora_g", G)
                    give(V.tensor_tensor(y_T[:, 2 * G:2 * G + 2], y_grp[:], gate_g[:], ALU.mult), "yt_ready")

            def cross(n, s):
                h = s[1]
                if s[0] == "x_scores":
                    p = job_wait_full(dve, n)
                    link(V.tensor_reduce(stat[:, 5], p[:, 0:512].rearrange("p (t m) -> p t m", t=TT), AX.X, ALU.max))
                    give(V.tensor_scalar(stat[:, 6], stat[:, 5], -XHD ** -0.5, None, ALU.mult), "x_max")
                    consumed(dve, *s)
                    link(V.reciprocal(stat[:, 7], stat[:, 7]))
                    for j in range(TT):
                        last = V.tensor_scalar(xp[:, h % 2, j], xp[:, h % 2, j], stat[:, 7, j:j + 1], None, ALU.mult)
                    give(last, "x_norm")

            def lead(g, k):
                g2, k2 = (g, k + 3) if k + 3 < HU else (g + 1, k + 3 - HU)
                w_low(g2 * HU + k2, k2, 288 if g2 == B_LORA else 512)

            def walk(steps):
                for n, *s in steps:
                    if s[0] == "gain":
                        p = job_wait_full(dve, n)
                        free_job(V.tensor_copy(colA[:, 0:KT], p[:, 0:KT]), n)
                    elif s[0] == "params":
                        dve.wait_ge(S_("pos_loaded"), 16)
                        give(V.tensor_copy(pack[96:98, 1], pos_i[96:98]), "pos_float")
                        p = job_wait_full(dve, n)
                        V.tensor_copy(colA[:, KT:P], p[:, KT:P])
                        for i, t in ((1, colB), (2, colC)):
                            last = V.tensor_copy(t[:], p[:, P * i:P * i + P])
                        free_job(last, n)
                    elif s[0] == "hu":
                        g, k = s[1:]
                        lead(g, k)
                        if k == HU - 1 and B_LORA <= g < B_WK:
                            shift(g)
                    elif s[0] == "mem_sq":
                        pass
                    elif s[0] == "mem_scale":
                        dve.wait_ge(S_("mem_ssq"), TT)
                        mean_square(1, ssq[:, :, 1], "mem")
                        scale_rows(rows0, rows0, 1, "mem")
                    elif s[0] == "angles":
                        dve.wait_ge(xh_ready, 4)
                        V.memset(v_win[64:128, 0], 0.0).then_inc(S_("vwin_zero"), 1)
                        angles()
                        dve.wait_ge(S_("trig_ready"), 1)
                        V.memset(stage[:, :, :, 0:1], 0.0).then_inc(S_("stage_zero"), 1)
                    elif s[0] == "fill":
                        fill(n, *s[1:])
                        if tuple(s[1:]) == (0, 0):
                            w_low(2, 2)
                    elif s[0] == "fill_T":
                        f, i = s[1:]
                        low_fill(f, i, y_T[:, 4 * i:4 * i + 4])
                    elif s[0] == "rope":
                        rope_q_k()
                    elif s[0].startswith("swa"):
                        swa(n, s)
                    elif s[0].startswith("x_"):
                        cross(n, s)
                    else:
                        rwkv(n, s)

            def rows_out(dst, b, par, i, g):
                dve.wait_ge(S_("gpost_loaded"), 16 * (i + 1))
                for j in range(TT):
                    dve.wait_ge(S_("squared"), b * 2 + (8 * i + j + 1))
                    last = V.tensor_tensor(dst[:, j, bass.ds(b * 512, 512)], acc[par][:, j * 512:j * 512 + 512],
                                           g[:, bass.ds(b * 512, 512)], ALU.mult)
                last.then_inc(evac_done, 1)

            def residual(i, y, x, last_block):
                dve.wait_ge(S_("squared"), 8 * (i + 1))
                dve.wait_ge(evac_done, last_block)
                link(V.tensor_reduce(stat[:, 7], ssq[:], AX.X, ALU.add))
                mean_square(2 + i, stat[:, 7], f"post{i}")
                dve.wait_ge(S_(f"post{i}_inv"), 1)
                dve.wait_ge(S_("x2_loaded" if i == 2 else "xres_loaded"), 16)
                for c in range(4):
                    cs = slice(512 * c, 512 * c + 512)
                    for j in range(TT):
                        V.scalar_tensor_tensor(x[:, j, cs], y[:, j, cs], stat[:, 2 + i, j:j + 1], x[:, j, cs],
                                               ALU.mult, ALU.add).then_inc(S_("result" if i == 2 else "xres_ready"), 1)
                if i < 2:
                    dve.wait_ge(S_(f"pre{i}_ssq"), 1)
                    link(V.tensor_reduce(stat[:, 7], ssq[:], AX.X, ALU.add))
                    mean_square(5, stat[:, 7], f"pre{i}")
                    scale_rows(y, x, 5, f"pre{i}")

            def loop_rows(g0, i):
                with dve.Fori(0, 2) as b2:
                    for r in range(2):
                        for k in range(HU):
                            w_low(b2 * (2 * HU) + ((g0 + r) * HU + k + 3), (k + 3) % HU)
                        rows_out(y_rows, b2 * 2 + r, (g0 + r) % 2, i, g_post)

            dve.wait_ge(S_("x_ssq"), TT)
            mean_square(0, ssq[:, :, 0], "x")
            scale_rows(rows0, rows0, 0, "x")
            w_low(0, 0)
            w_low(1, 1)
            walk(mix_steps)
            loop_rows(B_OUT, 0)
            residual(0, y_rows, x_res, B_WQ)
            walk(cross_steps)
            loop_rows(B_WO, 1)
            residual(1, y_rows, x_res, B_UP)
            walk(ffn_steps)
            dve.wait_ge(xh_ready, 4 * 5 + 4)
            dve.wait_ge(S_("x2_stored"), 16)
            V.memset(gate[:, :, :, 0:2], 0.0).then_inc(S_("gate_zero"), 1)

            def conv_block(i, r, w=None):
                dve.wait_ge(S_("gate_ready"), i + 1)
                for f in range(2):
                    last = V.tensor_scalar(conv[:, r, f], gate[:, r, f, 0:SEQ], colC[:, bass.ds(i * 2 + f, 1)],
                                           colB[:, bass.ds(i * 2 + (CB_CB + f), 1)], ALU.mult, ALU.add)
                last.then_inc(S_("conv_part"), 1)
                dve.wait_ge(S_("conv_part"), i * 2 + 1)
                for f in range(2):
                    last = V.scalar_tensor_tensor(conv[:, r, f], gate[:, r, f, 1:SEQ + 1], colC[:, bass.ds(i * 2 + (FT_FF + f), 1)],
                                                  conv[:, r, f], ALU.mult, ALU.add)
                last.then_inc(S_("conv_part"), 1)
                dve.wait_ge(S_("conv_part"), i * 2 + 2)
                for f in range(2):
                    last = V.scalar_tensor_tensor(conv[:, r, f], gate[:, r, f, 2:SEQ + 2], colC[:, bass.ds(i * 2 + (2 * FT_FF + f), 1)],
                                                  conv[:, r, f], ALU.mult, ALU.add)
                last.then_inc(S_("conv_ready"), 1)

            def mult_block(i, r):
                dve.wait_ge(S_("gelu_ready"), i + 1)
                V.tensor_tensor(act32[:, r], gelu[:, r], acc[(B_UP + r) % 2][:, 512:1024].rearrange("p (f t) -> p f t", f=2),
                                ALU.mult).then_inc(evac_done, 1)

            def low_block(i, r):
                dve.wait_ge(S_("acth_ready"), i + 1)
                V.tensor_tensor(act_lo[:, bass.ds(i * 2, 2)], act32[:, r], act_hi[:, bass.ds(i * 2, 2)].bitcast(F32),
                                ALU.subtract).then_inc(S_("actl_ready"), 1)

            def up_step(i, r, last):
                for k in range(HU):
                    if k == 0:
                        conv_block(i - 1, 1 - r)
                    if k == 3:
                        mult_block(i - 1, 1 - r)
                    if k == 6:
                        low_block(i - 1, 1 - r)
                    if not (last and k + 3 >= HU):
                        w_low(i * HU + (B_UP * HU + k + 3), (k + 3) % HU)

            up_step(1, 1, False)
            with dve.Fori(1, (N_UP - 1) // 2) as i2:
                up_step(i2 * 2, 0, False)
                up_step(i2 * 2 + 1, 1, False)
            up_step(N_UP - 1, 0, True)
            w_low_down(0, 0)
            w_low_down(0, 1)
            conv_block(N_UP - 1, 0)
            w_low_down(0, 2)
            w_low_down(0, 3)
            mult_block(N_UP - 1, 0)
            w_low_down(0, 4)
            low_block(N_UP - 1, 0)
            w_low_down(0, 5)

            def down_pair(b, last):
                for r in range(2):
                    for m in range(2 if r else AHEAD, HD_DOWN):
                        w_low_down(b + r, m)
                    if not (last and r):
                        w_low_down(b + (r + 1), 0)
                        w_low_down(b + (r + 1), 1)
                    rows_out(y_fin, b + r, (B_DOWN + r) % 2, 2, g_fin)
                if not last:
                    for m in range(2, AHEAD):
                        w_low_down(b + 2, m)

            with dve.Fori(0, N_DOWN // 2 - 1) as b2:
                down_pair(b2 * 2, False)
            down_pair(N_DOWN - 2, True)
            residual(2, y_fin, x_fin, B_DOWN + N_DOWN)

        @block.tensor
        def _(pe):
            T = nc.tensor

            def products(g, par, k, kind, f, n=512):
                q = g * HU + k
                if k == 0 and not (isinstance(g, int) and g < 2):
                    pe.wait_ge(evac_done, g - 1)
                if f is not None and k % 2 == 0:
                    pe.wait_ge(xl_ready, 4 * f + k // 2 + 1)
                pe.wait_ge(lo_ready, q + 1)
                sl_ = k % SLOTS
                for kt in range(2):
                    x = 2 * k + kt
                    first, final = x == 0, x == KT - 1
                    if kind == ROWS:
                        for t in range(TT):
                            o = acc[par][:, 512 * t:512 * t + 512]
                            xs_ = slice(P * t, P * t + P)
                            T.matmul(o, x_hi[:, x, xs_], w_hi[:, sl_, kt], start=first, stop=False)
                            T.matmul(o, x_hi[:, x, xs_], w_lo[:, sl_, kt], start=False, stop=False)
                            last = T.matmul(o, x_lo[:, x, xs_], w_hi[:, sl_, kt], start=False, stop=final)
                    else:
                        for c in range(n // P + (n % P > 0)):
                            o = acc[par][:, SEQ * c:SEQ * c + SEQ]
                            cs = slice(P * c, P * c + P)
                            T.matmul(o, w_hi[:, sl_, kt, cs], x_hi[:, x], start=first and c % 2 == 0, stop=False, skip_group_check=True)
                            T.matmul(o, w_hi[:, sl_, kt, cs], x_lo[:, x], start=False, stop=False, skip_group_check=True)
                            last = T.matmul(o, w_lo[:, sl_, kt, cs], x_hi[:, x], start=False, stop=final, skip_group_check=True)
                last.then_inc(used, 1)

            def begin(n):
                if n >= 2:
                    pe.wait_ge(job_free[n % 2], n // 2)
                return js[n % 2]

            def end(ins, n):
                ins.then_inc(job_full[n % 2], 1)

            def mm(o, l, r, start=True, stop=True):
                return T.matmul(o, l, r, start=start, stop=stop, skip_group_check=True)

            ROWS_OF = {0: (rows0, "x"), 1: (rows0, "mem"), 3: (y_rows, "pre0"), 5: (y_rows, "pre1")}

            def fill(n, f, i):
                p = begin(n)
                rows, name = ROWS_OF[f]
                pe.wait_ge(S_(name + "_rows0"), i + 1)
                pe.wait_ge(S_(name + "_rows1"), i + 1)
                for c in range(4):
                    for t in range(TT):
                        last = T.transpose(p[:, SEQ * c + P * t:SEQ * c + P * t + P],
                                           rows[:, t, P * (4 * i + c):P * (4 * i + c) + P], ident[:])
                end(last, n)

            def swa(n, s):
                p = begin(n)
                if s[0] == "swa_kT":
                    pe.wait_ge(S_("kdup_ready"), 1)
                    for g in range(4):
                        for t in range(TT):
                            last = T.transpose(p[:, SEQ * g + P * t:SEQ * g + P * t + P],
                                               k_dup[:, t, g].rearrange("p a d -> p (a d)"), ident[:])
                elif s[0] == "swa_qT":
                    g = s[1]
                    for f in range(2):
                        for t in range(TT):
                            last = T.transpose(p[:, SEQ * f + P * t:SEQ * f + P * t + P],
                                               zq[:, t, 4 * g + 2 * f:4 * g + 2 * f + 2].rearrange("p a d -> p (a d)"), ident[:])
                elif s[0] == "swa_scores":
                    g, j = s[1:]
                    consumed(pe, "swa_qT", g)
                    consumed(pe, "swa_kT")
                    for f in range(2):
                        for par in range(2):
                            c = 2 * j + par
                            for hh in range(2):
                                h = slice(64 * hh, 64 * hh + 64)
                                for piece in range(2):
                                    own = piece == par
                                    kc = c if own else max(c - 1, 0)
                                    last = mm(p[64 * par:64 * par + 64, 512 * hh + P * f + CH * piece:512 * hh + P * f + CH * piece + CH],
                                              q_T[h, g % 2, f, CH * c:CH * c + CH], k_T[h, g, CH * kc:CH * kc + CH])
                elif s[0] == "swa_pT":
                    g, j = s[1:]
                    pe.wait_ge(S_("s_norm"), 2 * g + j + 1)
                    for i in range(4):
                        last = T.transpose(p[:, P * i:P * i + P], prob[:, j, i], ident[:])
                else:
                    g, j = s[1:]
                    consumed(pe, "swa_pT", g, j)
                    for f in range(2):
                        for par in range(2):
                            for hh in range(2):
                                last = mm(p[64 * hh:64 * hh + 64, P * f + CH * par:P * f + CH * par + CH],
                                          v_win[:, 2 * j + par, g], prob_T[:, j, 2 * hh + f, CH * par:CH * par + CH])
                end(last, n)

            def rwkv(n, s):
                what, G = s[0], s[1]
                p = begin(n)
                hs = [slice(0, 64), slice(64, 128)]
                if what == "lora_wa":
                    pe.wait_ge(S_("lora_act"), 3)
                    pe.wait_ge(S_("wa_loaded"), 32 * (G + 1))
                    for f in range(2):
                        for i in range(2):
                            last = mm(p[:, 512 * i + SEQ * f:512 * i + SEQ * f + SEQ], lora_w[hs[i], 0, P * f:P * f + P], lora[hs[i], 0])
                elif what == "lora_g":
                    pe.wait_ge(S_("g_loaded"), 32 * (G + 1))
                    for f in range(2):
                        o = p[:, SEQ * f:SEQ * f + SEQ]
                        mm(o, lora_w[:, 1, P * f:P * f + P], lora[:, 1], True, False)
                        last = mm(o, lora_w[0:32, 2, P * f:P * f + P], lora[0:32, 2], False, True)
                elif what == "kk_norm":
                    pe.wait_ge(S_("kk_sq"), G + 1)
                    last = mm(p[:, 0:512], hones[:], inv_norm[:].rearrange("p f t -> p (f t)"))
                elif what == "v_rows":
                    for t in range(TT):
                        for f in range(2):
                            last = T.transpose(p[:, SEQ * t + P * f:SEQ * t + P * f + P], feat[:, 24 + 2 * G + f, P * t:P * t + P], ident[:])
                elif what == "bk_rows":
                    pe.wait_ge(S_("kr_ready"), G + 1)
                    for f in range(2):
                        for c in range(NCH):
                            last = T.transpose(p[:, 512 * f + P * c:512 * f + P * c + P], bk[:, f, c].rearrange("p a s -> p (a s)"), ident[:])
                elif what == "scores":
                    for f in range(2):
                        for cc in range(2):
                            c = 2 * s[2] + cc
                            for hh in range(2):
                                at_ = 512 * hh + 256 * f + P * cc
                                last = mm(p[:, at_:at_ + P], bk[hs[hh], f, c].rearrange("p a s -> p (a s)"),
                                          kr[G % 2][hs[hh], f, c].rearrange("p a s -> p (a s)"))
                elif what == "lower":
                    for c in range(NCH):
                        for f in range(2):
                            for hh in range(2):
                                at_ = 512 * hh + P * (c // 2) + CH * f
                                last = mm(p[half(c), at_:at_ + CH], kr[G % 2][hs[hh], f, c, 0], bk[hs[hh], f, c, b_part(c)])
                elif what in ("inv_p", "inv_x", "inv_t"):
                    b = s[2]
                    if what == "inv_p":
                        if b == LEVELS[0]:
                            pe.wait_ge(S_("inv_ready"), G + 1)
                        else:
                            consumed(pe, "inv_x", G, b // 2)
                        left, right = low, inv_x
                    elif what == "inv_x":
                        consumed(pe, "inv_p", G, b)
                        if b != LEVELS[0]:
                            consumed(pe, "inv_t", G, b // 2)
                        left, right = inv_t, inv_p
                    else:
                        left, right = inv_p, inv_t
                    for i in range(8):
                        ix = (i // 4, i // 2 % 2, i % 2)
                        for q in range(2):
                            at_ = 512 * q + CH * i
                            last = mm(p[hs[q], at_:at_ + CH], left[hs[q], ix[0], ix[1], ix[2]], right[hs[q], ix[0], ix[1], ix[2]])
                elif what in ("scan_x", "scan_u", "scan_ys"):
                    c = s[2]
                    h = half(c)
                    if what == "scan_x":
                        if c:
                            pe.wait_ge(S_("state_ready"), 3 * G + c)
                        else:
                            consumed(pe, "v_rows", G)
                            consumed(pe, "bk_rows", G)
                            consumed(pe, "scores", G, 1)
                            pe.wait_ge(S_("uv_zero"), G + 1)
                        consumed(pe, "inv_x", G, LEVELS[-1])
                    elif what == "scan_u":
                        consumed(pe, "scan_x", G, c)
                    else:
                        consumed(pe, "scan_u", G, c)
                    for f in range(2):
                        for hh in range(2):
                            i = 2 * f + hh
                            m = mx[:, c // 2, hh, f, c % 2]
                            if what == "scan_x":
                                o = p[h, 512 * hh + CH * f:512 * hh + CH * f + CH]
                                last = mm(o, m[:, 0:CH], uv[:, c, i], True, c == 0)
                                if c:
                                    last = mm(o, kr[G % 2][hs[hh], f, c, 0], state[hs[hh], f], False, True)
                            elif what == "scan_u":
                                last = mm(p[h, CH * i:CH * i + CH], inv_x[h, c // 2, hh, f], xs[h, i])
                            else:
                                o = p[hs[hh], CH * f:CH * f + CH]
                                mm(o, uv[:, c, i], m[:, CH:2 * CH], True, c == 0)
                                if c:
                                    mm(o, state[hs[hh], f], kr[G % 2][hs[hh], f, c, 1], False, True)
                                last = mm(p[hs[hh], 512 + CH * f:512 + CH * f + CH], bk_rows[:, f, c, 64 * hh:64 * hh + 64], uv[:, c, i])
                elif what == "gn_mean":
                    consumed(pe, "scan_ys", G, NCH - 1)
                    pe.wait_ge(S_("bonus_ready"), G + 1)
                    mm(p[:, 0:512], hones[:], y_grp[:].rearrange("p f t -> p (f t)"))
                    last = mm(p[:, 512:1024], hones[:], bonus[G % 2][:].rearrange("p f t -> p (f t)"))
                else:
                    pe.wait_ge(S_("gn_sq"), G + 1)
                    last = mm(p[:, 0:512], hones[:], y_sq[:].rearrange("p f t -> p (f t)"))
                end(last, n)

            def cross(n, s):
                p = begin(n)
                h = s[1]
                if s[0] == "x_scores":
                    pe.wait_ge(evac_done, B_WQ + h + 1)
                    pe.wait_ge(S_("kv_loaded"), 16 * 8)
                    for j in range(TT):
                        for c in range(4):
                            last = mm(p[:, MEM * j:MEM * j + MEM], y_T[:, 4 * h + c, P * j:P * j + P], kx[:, 4 * h + c], c == 0, c == 3)
                elif s[0] == "x_pT":
                    pe.wait_ge(S_("x_norm"), h + 1)
                    for m in range(2):
                        for j in range(TT):
                            last = T.transpose(p[:, SEQ * m + P * j:SEQ * m + P * j + P], xp[:, h % 2, j, P * m:P * m + P], ident[:])
                else:
                    consumed(pe, "x_pT", h)
                    for c in range(4):
                        for m in range(2):
                            last = mm(p[:, SEQ * c:SEQ * c + SEQ], vx[:, m, h, P * c:P * c + P], xp_T[:, h % 2, m], m == 0, m == 1)
                end(last, n)

            def walk(steps):
                for n, *s in steps:
                    if s[0] == "gain":
                        p = begin(n)
                        pe.wait_ge(S_("ident_ready"), 1)
                        pe.wait_ge(S_("gain_loaded"), 16)
                        end(T.transpose(p[:, 0:KT], pack[0:KT, 0], ident[0:KT, 0:KT]), n)
                    elif s[0] == "params":
                        p = begin(n)
                        pe.wait_ge(S_("pos_float"), 1)
                        pe.wait_ge(S_("pack_loaded"), N_PACK * 16)
                        for i in range(3):
                            last = T.transpose(p[:, P * i:P * i + P], pack[:, i], ident[:])
                        end(last, n)
                    elif s[0] == "hu":
                        g, k = s[1:]
                        products(g, g % 2, k, kind_of(g), FIRST_OF_FILL.get(g), 288 if g == B_LORA else 512)
                    elif s[0] == "fill":
                        fill(n, *s[1:])
                    elif s[0].startswith("swa"):
                        swa(n, s)
                    elif s[0].startswith("x_"):
                        cross(n, s)
                    elif s[0] not in NO_JOB:
                        rwkv(n, s)

            def loop_rows(g0, f):
                with pe.Fori(0, 2) as b2:
                    for r in range(2):
                        for k in range(HU):
                            products(b2 * 2 + (g0 + r), (g0 + r) % 2, k, ROWS, f)

            walk(mix_steps)
            loop_rows(B_OUT, 2)
            walk(cross_steps)
            loop_rows(B_WO, 4)
            walk(ffn_steps)
            with pe.Fori(0, (N_UP - 1) // 2) as i2:
                for r in range(2):
                    for k in range(HU):
                        products(i2 * 2 + (B_UP + 1 + r), (B_UP + 1 + r) % 2, k, COLS, None)
            with pe.Fori(0, N_DOWN // 2) as b2:
                for r in range(2):
                    par = (B_DOWN + r) % 2
                    pe.wait_ge(evac_done, b2 * 2 + (B_DOWN + r - 1))
                    for m in range(HD_DOWN):
                        pe.wait_ge(S_("actl_ready"), m + 1)
                        pe.wait_ge(lo_ready, b2 * (2 * HD_DOWN) + (Q_DOWN + r * HD_DOWN + m + 1))
                        for kt in range(2):
                            x = 2 * m + kt
                            for t in range(TT):
                                o = acc[par][:, 512 * t:512 * t + 512]
                                ts_ = slice(P * t, P * t + P)
                                T.matmul(o, act_hi[:, x, ts_], w_hi[:, m % SLOTS_D, kt], start=x == 0, stop=False)
                                T.matmul(o, act_hi[:, x, ts_], w_lo[:, m % SLOTS_D, kt], start=False, stop=False)
                                last = T.matmul(o, act_lo[:, x, ts_], w_hi[:, m % SLOTS_D, kt], start=False, stop=x == FT_FF - 1)
                        last.then_inc(used, 1)


_INS = ["x", "mem", "positions", "norm_mix_pre", "norm_mix_post", "w_in", "shift_mu", "w0", "w_lora_up", "a0",
        "a_lora_up", "g_lora_up", "k_k", "k_a", "r_k", "ln_x_w", "ln_x_b", "attn_sinks", "w_out", "norm_cross_pre",
        "norm_cross_post", "mem_norm", "wq_x", "wk_x", "wv_x", "wo_x", "norm_ffn_pre", "norm_ffn_post", "w_up",
        "conv_w", "conv_b", "w_down"]


def kernel(**inputs):
    import numpy as _np
    import concourse.bacc as _bacc
    from concourse import mybir as _mybir
    from concourse.bass_utils import run_bass_kernel_spmd as _run

    nc = _bacc.Bacc("TRN2", target_bir_lowering=False, num_devices=1)
    arrays, args = {}, {}
    for name in _INS:
        v = _np.ascontiguousarray(inputs[name])
        arrays[f"in_{name}_dram"] = v
        args[name] = nc.dram_tensor(f"in_{name}_dram", v.shape, _mybir.dt.from_np(v.dtype), kind="ExternalInput").ap()
    out = nc.dram_tensor("out_0_dram", (1, SEQ, D), _mybir.dt.float32, kind="ExternalOutput").ap()
    build(nc, args, out)
    r = _run(nc, [arrays], core_ids=[0])
    return r.results[0]["out_0_dram"]
```

```python
import math
import concourse.bass as bass
from concourse import mybir
from contextlib import ExitStack

F32, F32R, I32 = mybir.dt.float32, mybir.dt.float32r, mybir.dt.int32
ALU, ACT, AX = mybir.AluOpType, mybir.ActivationFunctionType, mybir.AxisListType

D, SEQ, MEM, P = 2048, 256, 256, 128
KT = D // P
TT = SEQ // P
CH = 64
NCH = SEQ // CH
RW, HD = 1024, 64
NLORA_W, NLORA_A, NLORA_G = 64, 64, 160
N_RWKV = 3 * RW + NLORA_W + NLORA_A + NLORA_G
N_IN = N_RWKV + 24 * HD
DFF = 5376
FT_FF = DFF // P
XHEADS, XHD = 4, 512
DECAY_SCALE = math.exp(-0.5)
GN_EPS, RMS_EPS = 64e-5, 1e-6
NEG_INF = -1e30
ROT = 16
INV_FREQ = [500000.0 ** (-i / ROT) for i in range(0, ROT, 2)]

B_SWA, B_LORA, B_RKV, B_WK, B_WV, B_OUT, B_WQ, B_WO, B_UP, B_DOWN = 0, 3, 4, 10, 14, 18, 22, 26, 30, 51
N_UP, N_DOWN = 21, 4
HU = 8
Q_DOWN = B_DOWN * HU
HD_DOWN = FT_FF // 2
AHEAD = 6
SLOTS, SLOTS_D, RAW_D = 4, 3, 7
COLS, ROWS = "cols", "rows"


def kind_of(g):
    return COLS if B_LORA <= g < B_WV or B_WQ <= g < B_WO or B_UP <= g < B_DOWN else ROWS


FIRST_OF_FILL = {B_SWA: 0, B_WK: 1, B_OUT: 2, B_WQ: 3, B_WO: 4, B_UP: 5}

LEVELS = (2, 4, 8, 16, 32)
HERE = ("hu",)
NO_JOB = ("hu", "mem_sq", "mem_scale", "angles", "fill_T", "rope", "swa_norm", "prep_kk", "prep_decay", "prep_k",
          "prep_bonus", "prep_kr", "prep_bk", "gn_out", "residual", "res_squares", "pre_stat")


def swa_steps():
    H = HERE
    yield from [("rope",), H, H, H, ("swa_kT",), ("swa_qT", 0), H, H]
    for g in range(4):
        if g < 3:
            yield from [("swa_scores", g, 0), H, ("swa_norm", g, 0), H, ("swa_scores", g, 1), H, ("swa_norm", g, 1), H,
                        ("swa_pT", g, 0), H, H, ("swa_out", g, 0), H, ("swa_qT", g + 1), H, ("swa_pT", g, 1), H, H,
                        ("swa_out", g, 1), H]
        else:
            yield from [("prep_kk", 0), ("swa_scores", g, 0), H, ("swa_norm", g, 0), H, ("swa_scores", g, 1), H,
                        ("swa_norm", g, 1), H, ("swa_pT", g, 0), H, H,
                        ("swa_out", g, 0), H, ("kk_norm", 0), H, ("lora_wa", 0), H, ("swa_pT", g, 1), ("prep_decay", 0), H,
                        ("swa_out", g, 1), ("prep_k", 0), H, H, ("prep_bonus", 0), H, ("prep_kr", 0),
                        H, ("prep_bk", 0)]


def rwkv_steps():
    H = HERE
    for G in range(4):
        nxt = G + 1 < 4

        def prep(*steps):
            return [(s, G + 1) for s in steps] if nxt else []

        if G == 0:
            yield from [("v_rows", 0), ("bk_rows", 0), H, ("lower", 0), ("scores", 0, 0), H, ("scores", 0, 1), H]
        yield from [("inv_p", G, 2), H, ("inv_x", G, 2), ("inv_t", G, 2)]
        yield from prep("prep_kk")
        yield from [("inv_p", G, 4), H, ("inv_x", G, 4), ("inv_t", G, 4)]
        yield from prep("kk_norm", "lora_wa")
        yield from [("inv_p", G, 8), H, ("inv_x", G, 8), ("inv_t", G, 8)]
        yield from prep("prep_decay")
        yield from [("inv_p", G, 16), H, ("inv_x", G, 16), ("inv_t", G, 16)]
        yield from prep("prep_k")
        yield from [("inv_p", G, 32), H, ("inv_x", G, 32)] + ([] if nxt else [H])
        for c in range(NCH):
            yield ("scan_x", G, c)
            if c < NCH - 1:
                yield H
            else:
                yield ("lora_g", G)
            yield ("scan_u", G, c)
            if c < NCH - 1:
                yield from prep(("prep_bonus", "prep_kr", "prep_bk")[c])
            yield ("scan_ys", G, c)
            if c < NCH - 1:
                yield H
        if nxt:
            yield from [("bk_rows", G + 1), ("gn_mean", G), ("scores", G + 1, 0), ("gn_var", G), H,
                        ("lower", G + 1), ("v_rows", G + 1), H, ("scores", G + 1, 1), ("gn_out", G), H]
        else:
            yield from [("fill_T", 2, 0), ("gn_mean", G), H, ("gn_var", G), ("gn_out", G), ("fill_T", 2, 1), H,
                        ("fill_T", 2, 2), H, ("fill_T", 2, 3)]


def residual_steps(i, f):
    H = HERE
    return [("residual", i, 0), ("residual", i, 1), ("fill", f, 0), ("fill", f, 1), ("residual", i, 2), H, H,
            ("fill", f, 2), ("res_squares", i, 0), ("residual", i, 3), H, ("res_squares", i, 1), H, ("fill", f, 3),
            ("res_squares", i, 2), H, ("res_squares", i, 3), ("pre_stat", i), H, H]


def weave(steps, hus):
    hus = list(hus)
    out = [hus.pop(0) if s == HERE else s for s in steps]
    return out, hus


def half_units(g0, g1):
    return [("hu", g, k) for g in range(g0, g1) for k in range(HU)]


def schedule():
    H = HERE
    mix, left = weave([("gain",), ("fill", 0, 0), ("fill", 0, 1), H, ("fill", 0, 2), H, ("fill", 0, 3), H, H, H,
                       ("mem_sq",), H, H, ("params",), H, ("mem_scale",), H, H, ("angles",)],
                      half_units(B_SWA, B_LORA))
    mix += left
    steps, left = weave(swa_steps(), half_units(B_LORA, B_WK))
    mix += steps + left[:-2] + [("fill", 1, 0)] + left[-2:]
    steps, left = weave([("fill", 1, 1), H, ("fill", 1, 2), H, ("fill", 1, 3), H, H]
                        + list(rwkv_steps()), half_units(B_WK, B_OUT))
    assert not left
    mix += steps
    steps = residual_steps(0, 3) + [H]
    for h in range(XHEADS):
        last, split = h == XHEADS - 1, [("fill_T", 4, i) if h == XHEADS - 2 else None for i in range(3)]
        steps += [H, ("x_scores", h), H, split[0], H, ("x_pT", h), H, ("x_out", h), H, split[1], H,
                  ("fill_T", 4, 3) if last else None, H, H, split[2]]
    cross, left = weave([s for s in steps if s], half_units(B_WQ, B_WO + 2))
    cross += left
    ffn, left = weave(residual_steps(1, 5), half_units(B_UP, B_UP + 1))
    ffn += left + [("rstd_T",)]
    n, out = 0, []
    for part in (mix, cross, ffn):
        steps = []
        for s in part:
            if s[0] in NO_JOB:
                steps.append((None,) + s)
            else:
                steps.append((n,) + s)
                n += 1
        out.append(steps)
    return out


def build(nc, a, out):
    mix_steps, cross_steps, ffn_steps = schedule()
    ctx = ExitStack()
    with ctx:
        base = 16640

        def sb(name, shape, dt, at):
            return nc.alloc_sbuf_tensor_at(name, [P] + list(shape), dt, offset=base + at)

        raw = sb("raw", [4, 4, 512], F32, 0)
        raw_d = sb("raw_d", [RAW_D, 2, 512], F32, 0)
        w_hi = sb("w_hi", [SLOTS, 2, 512], F32R, 32768)
        w_lo = sb("w_lo", [SLOTS, 2, 512], F32R, 49152)
        x_hi = sb("x_hi", [KT, SEQ], F32R, 65536)
        x_lo = sb("x_lo", [KT, SEQ], F32R, 81920)
        at = [98304]

        def const(name, shape, dt=F32):
            n = 4
            for s in shape:
                n *= s
            t = sb(name, shape, dt, at[0])
            at[0] += (n + 31) // 32 * 32
            return t

        colA, colB, colC = const("colA", [P]), const("colB", [P]), const("colC", [P])
        ident, hones = const("ident", [P]), const("hones", [P])
        mask_sc, mask_low = const("mask_sc", [2, CH]), const("mask_low", [CH])
        lvl_x, lvl_t = const("lvl_x", [6, CH]), const("lvl_t", [5, CH])
        eye = const("eye", [CH])
        reset = const("reset", [SEQ])
        trig = const("trig", [2, TT, 8])
        sink = const("sink", [16])
        ssq = const("ssq", [TT, 4])
        stat = const("stat", [8, TT])
        soft = const("soft", [6, 4])
        assert at[0] <= 106496, at
        R = 106496

        feat = sb("feat", [32, SEQ], F32, R)
        y_T = feat[:, 0:KT]
        junk = sb("junk", [D], F32, R + 16384)
        slot_at = [R + 32768 + 2048 * i for i in range(4)]
        lora = sb("lora", [3, SEQ], F32, R + 40960)
        lora_w = sb("lora_w", [3, 2 * P], F32, R + 44032)
        stage = sb("stage", [2, 4, SEQ + 1], F32, R + 47104)
        fill_tmp = sb("fill_tmp", [2, 4, SEQ], F32, R + 47104)
        pack = sb("pack", [3, P], F32, R + 40960)
        pos_i = sb("pos_i", [P], I32, R + 40960 + 1536)
        ang = sb("ang", [6, TT, 8], F32, R + 47104 + 2048)
        S = R + 55360
        rows0 = sb("rows0", [TT, D], F32, S)
        zq = sb("zq", [TT, 24, HD], F32, S + 16384)
        q_T = sb("q_T", [2, 2, SEQ], F32, S + 28672)
        k_T = sb("k_T", [4, SEQ], F32, S + 32768)
        v_win = sb("v_win", [NCH, 4, HD], F32, S + 36864)
        prob = sb("prob", [2, 4, P], F32, S + 40960)
        rope = sb("rope", [4, 20, 8], F32, S + 40960)
        prob_T = sb("prob_T", [2, 4, P], F32, S + 45056)
        k_dup = sb("k_dup", [TT, 4, 2, HD], F32, S + 45056)
        bk = sb("bk", [2, NCH, 2, CH], F32, S + 45056)
        kr = [sb(f"kr{i}", [2, NCH, 2, CH], F32, S + o) for i, o in enumerate((28672, 4096))]
        bk_rows = sb("bk_rows", [2, NCH, P], F32, S + 8192)
        uv = sb("uv", [NCH, 4, HD], F32, S + 12288)
        slot_at += [S + 16384 + 2048 * i for i in range(6)]
        decay, rate, kk, inv_norm, cum, exp_neg, k_new, y_grp, bonus0, bonus1 = (
            sb(name, [2, SEQ], F32, o) for name, o in zip(
                ("decay", "rate", "kk", "inv_norm", "cum", "exp_neg", "k_new", "y_grp", "bonus0", "bonus1"), slot_at))
        bonus = [bonus0, bonus1]
        y_sq, rstd, bonus_v, gate_g = decay, rate, kk, exp_neg
        mx = sb("mx", [2, 2, 2, 2, 2 * CH], F32, S + 32768)
        low = sb("low", [2, 2, 2, CH], F32, S + 40960)
        inv_t = sb("inv_t", [2, 2, 2, CH], F32, S + 43008)
        inv_x = sb("inv_x", [2, 2, 2, CH], F32, S)
        inv_p = sb("inv_p", [2, 2, 2, CH], F32, S + 2048)
        state = sb("state", [2, HD], F32, S + 49152)
        xs = sb("xs", [4, HD], F32, S + 49664)
        chunk_decay = sb("chunk_decay", [2, 2, NCH], F32, S + 50688)
        y_rows = sb("y_rows", [TT, D], F32, R + 16384)
        x_res = sb("x_res", [TT, D], F32, R + 32768)
        kx = sb("kx", [KT, MEM], F32, R + 49152)
        vx = sb("vx", [TT, 4, 512], F32, R + 65536)
        g_post = sb("g_post", [D], F32, R + 81920)
        xp = sb("xp", [2, TT, MEM], F32, R + 90112)
        xp_T = sb("xp_T", [2, TT, SEQ], F32, R + 94208)
        xfill = sb("xfill", [2, 4, SEQ], F32, R)
        act_hi = sb("act_hi", [FT_FF, SEQ], F32R, R)
        act_lo = sb("act_lo", [FT_FF, SEQ], F32R, R + 43008)
        F = R + 86016
        gate = sb("gate", [2, 2, SEQ + 2], F32, F)
        conv = sb("conv", [2, 2, SEQ], F32, F + 4128)
        gelu = sb("gelu", [2, 2, SEQ], F32, F + 8224)
        act32 = sb("act32", [2, 2, SEQ], F32, F + 12320)
        rstd_T = sb("rstd_T", [SEQ], F32, F + 16416)
        rstd_diag = sb("rstd_diag", [TT, P], F32, F + 17440)
        ones = sb("ones", [P], F32, F + 18464)
        ffill = sb("ffill", [2, 4, SEQ], F32, F)
        y_fin = sb("y_fin", [TT, D], F32, 65536)
        x_fin = sb("x_fin", [TT, D], F32, 81920)
        g_fin = sb("g_fin", [D], F32, F)

        acc = [ctx.enter_context(nc.psum_tensor(f"acc{i}", [P, 1024], F32)) for i in range(2)]
        js = [ctx.enter_context(nc.psum_tensor(f"job{i}", [P, 1024], F32)) for i in range(2)]
        kx_d = nc.dram_tensor("kx_scratch", (4, P, 1024), F32, kind="Internal").ap()
        vx_d = nc.dram_tensor("vx_scratch", (4, P, 1024), F32, kind="Internal").ap()

        sems = {}

        def S_(name):
            if name not in sems:
                sems[name] = ctx.enter_context(nc.semaphore(name))
            return sems[name]

        raw_loaded = [S_(f"raw_loaded{j}") for j in range(4)]
        rawd_loaded = [S_(f"rawd_loaded{j}") for j in range(RAW_D)]
        hi_ready, lo_ready, used = S_("hi_ready"), S_("lo_ready"), S_("used")
        evac_done = S_("evac_done")
        job_full, job_free = [S_("job_full0"), S_("job_full1")], [S_("job_free0"), S_("job_free1")]
        xh_ready, xl_ready = S_("xh_ready"), S_("xl_ready")
        kv_stored = [S_("kv_stored0"), S_("kv_stored1")]
        JOB = {tuple(s): n for steps in (mix_steps, cross_steps, ffn_steps) for n, *s in steps if n is not None}
        FREE_AT = {0: 0, 1: B_WK, 2: B_OUT, 3: B_WQ, 4: B_WO, 5: B_UP}

        def fill_buf(f, i):
            return (fill_tmp if f < 2 else xfill if f == 3 else ffill)[:, i % 2]

        def halves(i):
            return [slice(0, 2), slice(2, 4)] if i == 0 else [slice(0, 4)]

        def split_count(f, i, m=None):
            return 5 * f + i + (2 if i or m is None or m.start else 1)

        def produced(eng, *step):
            n = JOB[step]
            eng.wait_ge(job_full[n % 2], n // 2 + 1)

        def consumed(eng, *step):
            n = JOB[step]
            eng.wait_ge(job_free[n % 2], n // 2 + 1)

        G_COL = {0: 0, 1: 16, 3: 32, 5: 48}
        C_W0, C_A0, C_KK, C_KA, C_RK, C_LNW, C_LNB = (64 + 8 * i for i in range(7))
        CB_MU, CB_CB, CB_POS = 0, 27, 96
        N_PACK = 14
        block = ctx.enter_context(nc.Block())

        def job_wait_full(eng, n):
            eng.wait_ge(job_full[n % 2], n // 2 + 1)
            return js[n % 2]

        def half(c):
            return slice(64, 128) if c % 2 == 0 else slice(0, 64)

        def b_part(c):
            return 1 if c % 2 == 0 else 0

        def norm_out(eng, E, G):
            n = [4 * G]

            def then(ins):
                n[0] += 1
                ins.then_inc(S_("norm_out"), 1)
                eng.wait_ge(S_("norm_out"), n[0])

            eng.wait_ge(S_("gn_rt"), G + 1)
            then(E.tensor_tensor(y_grp[:], y_grp[:], rstd[:], ALU.mult))
            for f in range(2):
                c = 2 * G + f
                then(E.tensor_scalar(y_grp[:, f], y_grp[:, f], colA[:, C_LNW + c:C_LNW + c + 1],
                                     colA[:, C_LNB + c:C_LNB + c + 1], ALU.mult, ALU.add))
            then(E.tensor_tensor(y_grp[:], y_grp[:], bonus_v[:], ALU.add))
            consumed(eng, "lora_g", G)
            E.tensor_tensor(y_T[:, 2 * G:2 * G + 2], y_grp[:], gate_g[:], ALU.mult).then_inc(S_("yt_ready"), 1)

        @block.sync
        def _(sp):
            xv = a["x"].rearrange("b (t p) d -> p (b t) d", p=P)
            sp.dma_start(rows0[:, 0], xv[:, 0]).then_inc(S_("x_loaded0"), 16)
            sp.wait_ge(S_("pack_zero"), 1)
            sp.dma_start(pack[0:KT, 0, :], a["norm_mix_pre"].rearrange("l (f p) -> (l f) p", p=P)).then_inc(S_("gain_loaded"), 16)
            sp.dma_start(rows0[:, 1], xv[:, 1]).then_inc(S_("x_loaded1"), 16)

            w_in = a["w_in"]
            src = {}
            for i in range(3):
                src[B_SWA + i] = (w_in, N_RWKV + 512 * i, 512)
            src[B_LORA] = (w_in, 3 * RW, NLORA_W + NLORA_A + NLORA_G)
            for i in range(6):
                src[B_RKV + i] = (w_in, 512 * i, 512)
            for i in range(4):
                src[B_WK + i] = (a["wk_x"], 512 * i, 512)
                src[B_WV + i] = (a["wv_x"], 512 * i, 512)
                src[B_WQ + i] = (a["wq_x"], 512 * i, 512)

            def load(g, j, w, c0, n):
                if not (isinstance(g, int) and g == 0):
                    sp.wait_ge(lo_ready, g * HU + (2 * j + 2 - HU))
                sp.dma_start(raw[:, j, :, 0:n],
                             w[0, j * 512:(j + 1) * 512, bass.ds(c0, n)].rearrange("(k p) n -> p k n", p=P)
                             ).then_inc(raw_loaded[j], 16)

            for g in range(B_OUT):
                for j in range(4):
                    load(g, j, *src[g])
            for g0, w in ((B_OUT, a["w_out"]), (B_WQ, a["wq_x"]), (B_WO, a["wo_x"])):
                with sp.Fori(0, 4) as b:
                    for j in range(4):
                        load(b + g0, j, w, b * 512, 512)
            with sp.Fori(0, N_UP) as b:
                for j in range(4):
                    sp.wait_ge(lo_ready, (b + B_UP) * HU + (2 * j + 2 - HU))
                    for part in range(2):
                        sp.dma_start(raw[:, j, :, part * 256:part * 256 + 256],
                                     a["w_up"][0, j * 512:(j + 1) * 512, bass.ds(b * 256 + part * DFF, 256)]
                                     .rearrange("(k p) n -> p k n", p=P)).then_inc(raw_loaded[j], 16)

            def load_down(b, k, first):
                if first:
                    sp.wait_ge(lo_ready, Q_DOWN - HU + 2 * (k // 2) + 2)
                else:
                    sp.wait_ge(lo_ready, b * HD_DOWN + (Q_DOWN + k - RAW_D + 1))
                sp.dma_start(raw_d[:, k % RAW_D],
                             a["w_down"][0, k * 256:(k + 1) * 256, bass.ds(b * 512, 512)]
                             .rearrange("(k p) n -> p k n", p=P)).then_inc(rawd_loaded[k % RAW_D], 16)

            for k in range(HD_DOWN):
                load_down(0, k, k < RAW_D)
            with sp.Fori(1, N_DOWN) as b:
                for k in range(HD_DOWN):
                    load_down(b, k, False)
            ov = out.rearrange("b (t p) d -> p (b t) d", p=P)
            for c in range(4):
                cs = slice(512 * c, 512 * c + 512)
                for js_ in ([slice(0, TT)] if c < 3 else [slice(j, j + 1) for j in range(TT)]):
                    sp.wait_ge(S_("result"), TT * c + js_.stop)
                    sp.dma_start(ov[:, js_, cs], x_fin[:, js_, cs]).then_inc(S_("result_stored"), 16)
            sp.wait_ge(S_("result_stored"), 16 * (3 + TT))

        @block.gpsimd
        def _(pool):
            nc.gpsimd.memset(pack[:], 0.0).then_inc(S_("pack_zero"), 1)
            pool.wait_ge(S_("pack_zero"), 1)
            nc.gpsimd.memset(ident[:], 0.0).then_inc(S_("ident_zero"), 1)
            pool.wait_ge(S_("ident_zero"), 1)
            nc.gpsimd.affine_select(out=ident[:], in_=ident[:], compare_op=ALU.not_equal, fill=1.0, base=0,
                                    pattern=[[-1, P]], channel_multiplier=1).then_inc(S_("ident_ready"), 1)

            def vec(name, rows, t, row):
                pool.dma_start(pack[row:row + rows, t, :],
                               a[name].rearrange("l (f p) -> (l f) p", p=P)).then_inc(S_("pack_loaded"), 16)

            n = 1
            for f, name in ((3, "norm_cross_pre"), (5, "norm_ffn_pre")):
                vec(name, 16, 0, G_COL[f])
                n += 1
            pool.dma_start(pack[16:32, 0, :], a["mem_norm"].rearrange("(f p) -> f p", p=P)).then_inc(S_("pack_loaded"), 16)
            for name, c in (("w0", C_W0), ("a0", C_A0), ("k_k", C_KK), ("k_a", C_KA), ("ln_x_w", C_LNW), ("ln_x_b", C_LNB)):
                vec(name, 8, 0, c)
                n += 1
            pool.dma_start(pack[C_RK:C_RK + 8, 0, :], a["r_k"].rearrange("l (f h) d -> (l f) (h d)", h=2)).then_inc(S_("pack_loaded"), 16)
            pool.dma_start(pack[0:26, 1, :], a["shift_mu"][:, 0:26 * P].rearrange("l (f p) -> (l f) p", p=P)).then_inc(S_("pack_loaded"), 16)
            pool.dma_start(pack[26:27, 1, 0:32], a["shift_mu"][:, 26 * P:26 * P + 32]).then_inc(S_("pack_loaded"), 16)
            vec("conv_b", FT_FF, 1, CB_CB)
            pool.dma_start(pack[0:3 * FT_FF, 2, :], a["conv_w"].rearrange("l w (f p) -> (l w f) p", p=P)).then_inc(S_("pack_loaded"), 16)
            pool.dma_start(pos_i[96:98, :], a["positions"].rearrange("b (t p) -> (b t) p", p=P)).then_inc(S_("pos_loaded"), 16)
            pool.dma_start(sink[:], a["attn_sinks"].partition_broadcast(P).rearrange("q l n -> q (l n)")).then_inc(S_("sink_loaded"), 16)
            n += 5
            assert n == N_PACK
            produced(pool, "fill", 0, 2)
            produced(pool, "fill", 0, 3)
            mv = a["mem"].rearrange("b (t p) d -> p (b t) d", p=P)
            for j in range(TT):
                pool.dma_start(rows0[:, j], mv[:, j]).then_inc(S_(f"mem_loaded{j}"), 16)
            def lora_weights(G):
                c = slice(256 * G, 256 * G + 256)
                if G:
                    produced(pool, "lora_wa", G - 1)
                pool.dma_start(lora_w[0:64, 0], a["w_lora_up"][0, :, c]).then_inc(S_("wa_loaded"), 16)
                pool.dma_start(lora_w[64:128, 0], a["a_lora_up"][0, :, c]).then_inc(S_("wa_loaded"), 16)
                if G:
                    produced(pool, "lora_g", G - 1)
                pool.dma_start(lora_w[:, 1], a["g_lora_up"][0, 0:128, c]).then_inc(S_("g_loaded"), 16)
                pool.dma_start(lora_w[0:32, 2], a["g_lora_up"][0, 128:160, c]).then_inc(S_("g_loaded"), 16)

            lora_weights(0)
            marks = S_("mask_step")
            cnt = [0]

            def mark(ins):
                cnt[0] += 1
                ins.then_inc(marks, 1)
                pool.wait_ge(marks, cnt[0])

            def pick(ap, pattern, op, base_, cm, fill):
                mark(nc.gpsimd.affine_select(out=ap, in_=ap, compare_op=op, fill=fill, base=base_,
                                             pattern=pattern, channel_multiplier=cm))

            mark(nc.gpsimd.memset(hones[:], 0.0))
            mark(nc.gpsimd.memset(mask_sc[:], 1.0))
            mark(nc.gpsimd.memset(mask_low[:], -1.0))
            mark(nc.gpsimd.memset(lvl_x[:], 0.0))
            mark(nc.gpsimd.memset(lvl_t[:], 0.0))
            mark(nc.gpsimd.memset(eye[:], 0.0))
            for hh in range(2):
                h = slice(64 * hh, 64 * hh + 64)
                mark(nc.gpsimd.memset(hones[h, 64 * hh:64 * hh + 64], 1.0))
                pick(eye[h], [[-1, CH]], ALU.not_equal, 0, 1, 1.0)
                pick(mask_sc[h, 0], [[1, CH]], ALU.is_gt, 0, -1, 0.0)
                pick(mask_sc[h, 1], [[1, CH]], ALU.is_ge, 0, -1, 0.0)
                pick(mask_low[h], [[-1, CH]], ALU.is_gt, 0, 1, 0.0)
                for i in range(6):
                    b = 1 << i
                    n2 = CH // (2 * b)
                    v = lvl_x[h, i].rearrange("p (n h b) -> p n h b", h=2, b=b)[:, :, 1]
                    sgn = -1.0 if i == 0 else 1.0
                    mark(nc.gpsimd.memset(v, sgn))
                    pick(v, [[-2 * b, n2], [0, b]], ALU.is_ge, 0, 1, 0.0)
                    pick(v, [[2 * b, n2], [0, b]], ALU.is_ge, b - 1, -1, 0.0)
                    if i < 5:
                        v = lvl_t[h, i].rearrange("p (n h b) -> p n h b", h=2, b=b)[:, :, 0]
                        mark(nc.gpsimd.memset(v, 1.0))
                        pick(v, [[-2 * b, n2], [0, b]], ALU.is_ge, -b, 1, 0.0)
                        pick(v, [[2 * b, n2], [0, b]], ALU.is_ge, 2 * b - 1, -1, 0.0)
            mark(nc.gpsimd.memset(reset[:], 1.0))
            nc.gpsimd.memset(reset[:].rearrange("p (c t) -> p c t", t=CH)[:, :, 0:1], 0.0).then_inc(S_("masks"), 1)

            def inverse_start(G):
                consumed(pool, "lower", G)
                tv = inv_t[:].rearrange("p a b c d -> p (a b c) d")
                nc.gpsimd.tensor_tensor(tv, low[:].rearrange("p a b c d -> p (a b c) d"),
                                        lvl_t[:, 0].unsqueeze(1).broadcast_to([P, 8, CH]), ALU.mult).then_inc(S_("inv_t_part"), 1)
                pool.wait_ge(S_("inv_t_part"), G + 1)
                nc.gpsimd.tensor_tensor(tv, tv, eye[:].unsqueeze(1).broadcast_to([P, 8, CH]), ALU.add).then_inc(S_("inv_t_ready"), 1)
                pool.wait_ge(S_("inv_t_ready"), G + 1)

            for G in range(4):
                if G:
                    lora_weights(G)
                if G:
                    produced(pool, "scan_ys", G - 1, NCH - 1)
                else:
                    produced(pool, "fill", 1, 3)
                if G >= 2:
                    pool.wait_ge(S_("yt_ready"), G - 1)
                nc.gpsimd.memset(uv[64:128, 0:NCH:2], 0.0).then_inc(S_("uv_zero"), 1)
                pool.wait_ge(S_("uv_zero"), 2 * G + 1)
                nc.gpsimd.memset(uv[0:64, 1:NCH:2], 0.0).then_inc(S_("uv_zero"), 1)
                pool.wait_ge(S_("uv_zero"), 2 * G + 2)
                inverse_start(G)
                if G:
                    norm_out(pool, nc.gpsimd, G - 1)
            pool.wait_ge(S_("yt_ready"), 4)
            for i in range(2):
                pool.wait_ge(kv_stored[i], 16 * 4)
            xv = a["x"].rearrange("b (t p) d -> p (b t) d", p=P)
            pool.dma_start(x_res[:], xv).then_inc(S_("xres_loaded"), 16)
            pool.dma_start(g_post[:], a["norm_mix_post"][0].partition_broadcast(P)).then_inc(S_("gpost_loaded"), 16)
            for b in range(4):
                pool.dma_start(kx[:, 4 * b:4 * b + 4, :], kx_d[b].rearrange("p (f m) -> p f m", f=4)).then_inc(S_("kv_loaded"), 16)
                pool.dma_start(vx[:, :, b, :], vx_d[b].rearrange("p (t n) -> p t n", t=2)).then_inc(S_("kv_loaded"), 16)
            pool.wait_ge(evac_done, B_WQ)
            pool.dma_start(g_post[:], a["norm_cross_post"][0].partition_broadcast(P)).then_inc(S_("gpost_loaded"), 16)
            pool.wait_ge(S_("xres_ready"), 16)
            pool.dma_start(out.rearrange("b (t p) d -> p (b t) d", p=P), x_res[:]).then_inc(S_("x2_stored"), 16)
            pool.wait_ge(S_("x2_stored"), 16)
            pool.wait_ge(used, Q_DOWN)
            pool.dma_start(x_fin[:], out.rearrange("b (t p) d -> p (b t) d", p=P)).then_inc(S_("x2_loaded"), 16)
            pool.wait_ge(S_("actl_ready"), N_UP)
            pool.dma_start(g_fin[:], a["norm_ffn_post"][0].partition_broadcast(P)).then_inc(S_("gpost_loaded"), 16)

        @block.scalar
        def _(act):
            A = nc.scalar.activation

            def w_high(q, g, k, n=512, up=False):
                j = k // 2
                if up:
                    act.wait_ge(raw_loaded[j], g * 32 + (32 - 16 * B_UP))
                else:
                    act.wait_ge(raw_loaded[j], g * 16 + 16)
                if not (isinstance(q, int) and q < SLOTS):
                    act.wait_ge(used, q + (1 - SLOTS))
                A(w_hi[:, k % SLOTS, :, 0:n], raw[:, j, 2 * (k % 2):2 * (k % 2) + 2, 0:n], ACT.Copy).then_inc(hi_ready, 1)

            def w_high_down(b, m):
                act.wait_ge(rawd_loaded[m % RAW_D], b * 48 + 16 * (m // RAW_D + 1))
                act.wait_ge(used, b * HD_DOWN + (Q_DOWN - 2 + m))
                A(w_hi[:, m % SLOTS_D], raw_d[:, m % RAW_D], ACT.Copy).then_inc(hi_ready, 1)

            def width(g):
                return 288 if g == B_LORA else 512

            def lead(g, k):
                g2, k2 = (g, k + 3) if k + 3 < HU else (g + 1, k + 3 - HU)
                w_high(g2 * HU + k2, g2, k2, width(g2), g2 >= B_UP)

            def rows_squares(dst, b, par):
                for j in range(TT):
                    A(dst[:, j, bass.ds(b * 512, 512)], acc[par][:, j * 512:j * 512 + 512], ACT.Square,
                      accum_out=ssq[:, j, bass.ds(b, 1)]).then_inc(S_("squared"), 1)

            def evac(g):
                p = acc[g % 2]
                act.wait_ge(used, HU * (g + 1))
                if g < B_SWA + 2:
                    A(zq[:, :, 8 * g:8 * g + 8, :].rearrange("p t h d -> p t (h d)"),
                      p[:].rearrange("p (t n) -> p t n", t=TT), ACT.Copy).then_inc(evac_done, 1)
                elif g == B_SWA + 2:
                    pv = p[:].rearrange("p (t n) -> p t n", t=TT)
                    A(zq[:, :, 16:20, :].rearrange("p t h d -> p t (h d)"), pv[:, :, 0:256], ACT.Copy)
                    act.wait_ge(S_("vwin_zero"), 1)
                    for c, rows, t in ((1, slice(0, 128), 0), (3, slice(0, 128), 1), (0, slice(0, 64), 0),
                                       (2, slice(0, 64), 1), (2, slice(64, 128), 0)):
                        last = A(v_win[rows, c].rearrange("p g d -> p (g d)"), pv[rows, t, 256:512], ACT.Copy)
                    last.then_inc(evac_done, 1)
                elif g < B_WK:
                    if g == B_LORA:
                        act.wait_ge(S_("stage_zero"), 1)
                    if g >= B_LORA + 2:
                        act.wait_ge(S_("shifted"), g - B_LORA - 1)
                    A(stage[:, g % 2, 0:nf(g), 1:SEQ + 1],
                      p[:, 0:nf(g) * SEQ].rearrange("p (f t) -> p f t", t=SEQ), ACT.Copy).then_inc(evac_done, 1)
                elif g < B_OUT:
                    i = g - B_WK
                    if i >= 2:
                        act.wait_ge(kv_stored[i % 2], 16 * (i // 2))
                    st = fill_tmp[:, g % 2]
                    A(st.rearrange("p f t -> p (f t)"), p[:], ACT.Copy).then_inc(evac_done, 1)
                    act.wait_ge(evac_done, g + 1)
                    act.dma_start(kx_d[i] if i < 4 else vx_d[i - 4],
                                  st.rearrange("p f t -> p (f t)")).then_inc(kv_stored[i % 2], 16)
                elif B_WQ <= g < B_WO:
                    i = g - B_WQ
                    A(y_T[:, 4 * i:4 * i + 4].rearrange("p f t -> p (f t)"), p[:], ACT.Copy).then_inc(evac_done, 1)
                elif B_WO <= g < B_UP:
                    rows_squares(y_rows, g - B_WO, g % 2)

            def nf(g):
                return 3 if g == B_LORA else 4

            def preload(name):
                nc.scalar.preload_act_table_set(name)

            logs = [0]

            def log_exp(t, name):
                logs[0] += 1
                A(t, t, ACT.Ln).then_inc(S_("log_ready"), 1)
                act.wait_ge(S_("log_ready"), logs[0])
                A(t, t, ACT.Exp, scale=-0.5).then_inc(S_(name), 1)

            def stat_root(i, name):
                act.wait_ge(S_(name + "_ms"), 1)
                log_exp(stat[:, i], name + "_inv")

            def row_squares(rows, k, name):
                for j in range(TT):
                    act.wait_ge(S_(f"{name}_loaded{j}"), 16)
                    A(junk[:], rows[:, j], ACT.Square, accum_out=ssq[:, j, k:k + 1]).then_inc(S_(name + "_ssq"), 1)
                    act.wait_ge(S_(name + "_ssq"), j + 1)

            def scale_rows(dst, src, i, name):
                act.wait_ge(S_(name + "_inv"), 1)
                for c in range(4):
                    A(dst[:, 1, 512 * c:512 * c + 512], src[:, 1, 512 * c:512 * c + 512], ACT.Copy,
                      scale=stat[:, i, 1:2]).then_inc(S_(name + "_rows1"), 1)

            preload("natural_log_exp_and_others")
            row_squares(rows0, 0, "x")
            stat_root(0, "x")
            scale_rows(rows0, rows0, 0, "x")
            w_high(0, 0, 0)

            def chunk_free(f, i):
                if f:
                    act.wait_ge(used, HU * (FREE_AT[f] - 1) + 2 * i + 2)

            def fill_high(f, i, src):
                chunk_free(f, i)
                for m in halves(i):
                    if i % 2:
                        p = job_wait_full(act, JOB[("fill", f, i)])
                        if i > 2:
                            act.wait_ge(xl_ready, split_count(f, i - 2))
                        elif f == 1:
                            act.wait_ge(S_("shifted"), B_WK - B_LORA)
                        for c in range(4):
                            gain = colA[:, G_COL[f] + 4 * i + c:G_COL[f] + 4 * i + c + 1]
                            last = A(src[:, c], p[:, SEQ * c:SEQ * c + SEQ], ACT.Copy, scale=gain)
                        n = JOB[("fill", f, i)]
                        last.then_inc(job_free[n % 2], 1)
                        consumed(act, "fill", f, i)
                    elif m.stop < 4:
                        act.wait_ge(S_("half_filled"), (0, 1, 3, 5).index(f) + 1)
                    else:
                        consumed(act, "fill", f, i)
                    split_high(i, m, src)

            def split_high(i, m, src):
                A(x_hi[:, 4 * i + m.start:4 * i + m.stop].rearrange("p f t -> p (f t)"),
                  src[:, m].rearrange("p f t -> p (f t)"), ACT.Copy).then_inc(xh_ready, 1)

            def swa(n, s):
                if s[0] == "swa_scores":
                    p = job_wait_full(act, n)
                    g, j = s[1:]
                    if g:
                        produced(act, "swa_pT", g - 1, j)
                    else:
                        consumed(act, "swa_kT")
                    A(prob[:, j].rearrange("p (h f) k -> p h (f k)", h=2),
                      p[:].rearrange("p (h n) -> p h n", h=2)[:, :, 0:256], ACT.Copy, scale=HD ** -0.5).then_inc(job_free[n % 2], 1)
                elif s[0] == "swa_norm":
                    g, j = s[1:]
                    m = 2 * g + j
                    act.wait_ge(S_("s_shift"), m + 1)
                    A(prob[:, j], prob[:, j], ACT.Exp).then_inc(S_("s_exp"), 1)
                    A(soft[:, 2], soft[:, 1], ACT.Exp).then_inc(S_("s_exp"), 1)
                elif s[0] == "swa_pT":
                    p = job_wait_full(act, n)
                    g, j = s[1:]
                    if g:
                        produced(act, "swa_out", g - 1, j)
                    A(prob_T[:, j].rearrange("p h t -> p (h t)"), p[:, 0:512], ACT.Copy).then_inc(job_free[n % 2], 1)

            def rwkv(n, s):
                what, G = s[0], s[1]
                if what == "prep_kk":
                    if G:
                        preload("sigmoid_and_others")
                elif what == "kk_norm":
                    if G == 0:
                        preload("sigmoid_and_others")
                        act.wait_ge(S_("shifted"), 1)
                        A(lora[0:64, 0], lora[0:64, 0], ACT.Tanh).then_inc(S_("lora_act"), 1)
                        A(lora[:, 1], lora[:, 1], ACT.Sigmoid).then_inc(S_("lora_act"), 1)
                        A(lora[0:32, 2], lora[0:32, 2], ACT.Sigmoid).then_inc(S_("lora_act"), 1)
                elif what == "lora_wa":
                    p = job_wait_full(act, n)
                    if G >= 2:
                        act.wait_ge(S_("yt_ready"), G - 1)
                    for f in range(2):
                        A(decay[:, f], p[:, f * 256:f * 256 + 256], ACT.Sigmoid, bias=colA[:, C_W0 + 2 * G + f:C_W0 + 2 * G + f + 1])
                        last = A(rate[:, f], p[:, 512 + f * 256:768 + f * 256], ACT.Sigmoid, bias=colA[:, C_A0 + 2 * G + f:C_A0 + 2 * G + f + 1])
                    last.then_inc(job_free[n % 2], 1)
                elif what == "lora_g":
                    p = job_wait_full(act, n)
                    act.wait_ge(S_("kr_ready"), min(G + 2, 4))
                    if G:
                        act.wait_ge(S_("yt_ready"), G)
                    A(gate_g[:].rearrange("p f t -> p (f t)"), p[:, 0:512], ACT.Copy).then_inc(job_free[n % 2], 1)
                elif what == "prep_decay":
                    preload("natural_log_exp_and_others")
                    consumed(act, "kk_norm", G)
                    log_exp(inv_norm[:], "kk_rt")
                elif what == "prep_k":
                    if G == 0:
                        produced(act, "swa_qT", 3)
                    act.wait_ge(S_("cum_ready"), G + 1)
                    A(decay[:], decay[:], ACT.Exp).then_inc(S_("exp_ready"), 1)
                    A(exp_neg[:], cum[:], ACT.Exp, scale=-1.0).then_inc(S_("exp_ready"), 1)
                    act.wait_ge(S_("exp_ready"), 3 * G + 2)
                    A(cum[:], cum[:], ACT.Exp).then_inc(S_("exp_ready"), 1)
                elif what == "v_rows":
                    p = job_wait_full(act, n)
                    pv = p[:, 0:512].rearrange("p (t n) -> p t n", t=TT)
                    A(uv[0:64, 0:NCH:2].rearrange("p c i d -> p c (i d)"), pv[0:64], ACT.Copy)
                    A(uv[64:128, 1:NCH:2].rearrange("p c i d -> p c (i d)"), pv[64:128], ACT.Copy).then_inc(job_free[n % 2], 1)
                elif what == "bk_rows":
                    p = job_wait_full(act, n)
                    A(bk_rows[:].rearrange("p f c n -> p (f c n)"), p[:], ACT.Copy).then_inc(job_free[n % 2], 1)
                elif what == "inv_p":
                    p = job_wait_full(act, n)
                    A(inv_p[:].rearrange("p a b c d -> p (a b c d)"), p[:, 0:512], ACT.Copy).then_inc(job_free[n % 2], 1)
                elif what == "scan_x":
                    p = job_wait_full(act, n)
                    h = half(s[2])
                    A(xs[h].rearrange("p (f i) d -> p i f d", i=2),
                      p[h].rearrange("p (i n) -> p i n", i=2)[:, :, 0:P].rearrange("p i (f d) -> p i f d", f=2),
                      ACT.Copy, scale=-1.0).then_inc(job_free[n % 2], 1)
                elif what == "scan_u":
                    p = job_wait_full(act, n)
                    h = half(s[2])
                    A(uv[h, s[2]].rearrange("p i d -> p (i d)"), p[h, 0:256], ACT.Copy).then_inc(job_free[n % 2], 1)
                elif what == "gn_var":
                    consumed(act, *s)
                    log_exp(rstd[:], "gn_rt")

            def cross(n, s):
                h = s[1]
                if s[0] == "x_scores":
                    act.wait_ge(S_("x_max"), h + 1)
                    if h >= 2:
                        produced(act, "x_pT", h - 2)
                    p = js[n % 2]
                    for j in range(TT):
                        last = A(xp[:, h % 2, j], p[:, j * 256:j * 256 + 256], ACT.Exp, bias=stat[:, 6, j:j + 1],
                                 scale=stat[:, 0, j:j + 1], accum_out=stat[:, 7, j:j + 1])
                    last.then_inc(job_free[n % 2], 1)
                elif s[0] == "x_pT":
                    p = job_wait_full(act, n)
                    if h >= 2:
                        produced(act, "x_out", h - 2)
                    A(xp_T[:, h % 2].rearrange("p m t -> p (m t)"), p[:, 0:512], ACT.Copy).then_inc(job_free[n % 2], 1)
                elif s[0] == "x_out":
                    p = job_wait_full(act, n)
                    A(y_T[:, 4 * h:4 * h + 4].rearrange("p f t -> p (f t)"), p[:], ACT.Copy).then_inc(job_free[n % 2], 1)

            def walk(steps):
                for n, *s in steps:
                    if s[0] == "hu":
                        g, k = s[1:]
                        lead(g, k)
                        if k == HU - 1:
                            evac(g)
                    elif s[0] == "mem_sq":
                        row_squares(rows0, 1, "mem")
                    elif s[0] == "mem_scale":
                        stat_root(1, "mem")
                        scale_rows(rows0, rows0, 1, "mem")
                    elif s[0] == "angles":
                        preload("trig_and_small")
                        act.wait_ge(S_("ang_ready"), 1)
                        A(trig[:].rearrange("p a t i -> p (a t i)"), ang[:, 1:3].rearrange("p a t i -> p (a t i)"), ACT.Sin).then_inc(S_("trig_ready"), 1)
                    elif s[0] == "rope":
                        preload("natural_log_exp_and_others")
                    elif s[0] == "res_squares":
                        i, c = s[1:]
                        act.wait_ge(S_("xres_ready"), 8 * i + 2 * c + 2)
                        for j in range(TT):
                            A(y_rows[:, j, 512 * c:512 * c + 512], x_res[:, j, 512 * c:512 * c + 512], ACT.Square,
                              accum_out=ssq[:, j, c:c + 1]).then_inc(S_("res_squared"), 1)
                    elif s[0] == "pre_stat":
                        stat_root(5, f"pre{s[1]}")
                    elif s[0] == "rstd_T":
                        p = job_wait_full(act, n)
                        A(rstd_T[:], p[:, 0:SEQ], ACT.Copy).then_inc(job_free[n % 2], 1)
                        preload("gelu_and_others")
                    elif s[0] == "residual":
                        pass
                    elif s[0] == "fill":
                        f, i = s[1:]
                        fill_high(f, i, fill_buf(f, i))
                        if f == 0 and i < 2:
                            w_high(i + 1, 0, i + 1)
                    elif s[0] == "fill_T":
                        f, i = s[1:]
                        chunk_free(f, i)
                        if f == 4:
                            consumed(act, "x_out", i)
                        elif i < 2:
                            act.wait_ge(S_("yt_ready"), 2 * i + 2)
                        for m in halves(i):
                            split_high(i, m, y_T[:, 4 * i:4 * i + 4])
                    elif s[0].startswith("swa"):
                        swa(n, s)
                    elif s[0].startswith("x_"):
                        cross(n, s)
                    elif s[0] not in ("gain", "params"):
                        rwkv(n, s)

            def loop_rows(g0, first):
                with act.Fori(first, 2) as b2:
                    for r in range(2):
                        for k in range(HU):
                            g2, k2 = (r, k + 3) if k + 3 < HU else (r + 1, k + 3 - HU)
                            if not (r == 1 and k + 3 >= HU):
                                w_high(b2 * (2 * HU) + ((g0 + g2) * HU + k2), b2 * 2 + (g0 + g2), k2)
                            elif g0 == B_OUT:
                                w_high(b2 * (2 * HU) + ((g0 + g2) * HU + k2), b2 * 2 + (g0 + g2), k2)
                            else:
                                act.wait_ge(raw_loaded[k2 // 2], b2 * (16 * 3) + 16 * (B_WO + 3))
                                act.wait_ge(used, b2 * (2 * HU) + ((g0 + g2) * HU + k2 + 1 - SLOTS))
                                A(w_hi[:, k2 % SLOTS], raw[:, k2 // 2, 2 * (k2 % 2):2 * (k2 % 2) + 2], ACT.Copy).then_inc(hi_ready, 1)
                        act.wait_ge(used, b2 * (2 * HU) + (g0 + r + 1) * HU)
                        rows_squares(y_rows, b2 * 2 + r, (g0 + r) % 2)

            walk(mix_steps)
            loop_rows(B_OUT, 0)
            stat_root(2, "post0")
            walk(cross_steps)
            loop_rows(B_WO, 1)
            stat_root(3, "post1")
            walk(ffn_steps)

            def up_step(i, r, last):
                for k in range(HU):
                    if not (last and k + 3 >= HU):
                        g2, k2 = (0, k + 3) if k + 3 < HU else (1, k + 3 - HU)
                        w_high(i * HU + ((B_UP + g2) * HU + k2), i + (B_UP + g2), k2, 512, True)
                    if k == 2:
                        act.wait_ge(S_("conv_ready"), i)
                        A(gelu[:, 1 - r], conv[:, 1 - r], ACT.Gelu).then_inc(S_("gelu_ready"), 1)
                    if k == 5:
                        act.wait_ge(S_("act_ready"), i)
                        A(act_hi[:, bass.ds(i * 2 - 2, 2)], act32[:, 1 - r], ACT.Copy).then_inc(S_("acth_ready"), 1)
                if last:
                    w_high_down(0, 0)
                    w_high_down(0, 1)

            act.wait_ge(S_("x2_stored"), 16)
            up_step(1, 1, False)
            with act.Fori(1, (N_UP - 1) // 2) as i2:
                up_step(i2 * 2, 0, False)
                up_step(i2 * 2 + 1, 1, False)
            up_step(N_UP - 1, 0, True)
            w_high_down(0, 2)
            w_high_down(0, 3)
            act.wait_ge(S_("conv_ready"), N_UP)
            A(gelu[:, 0], conv[:, 0], ACT.Gelu).then_inc(S_("gelu_ready"), 1)
            w_high_down(0, 4)
            act.wait_ge(S_("act_ready"), N_UP)
            A(act_hi[:, FT_FF - 2:FT_FF], act32[:, 0], ACT.Copy).then_inc(S_("acth_ready"), 1)
            w_high_down(0, 5)

            preload("natural_log_exp_and_others")

            def down_pair(b, last):
                for r in range(2):
                    for m in range(2 if r else AHEAD, HD_DOWN):
                        w_high_down(b + r, m)
                    if not (last and r):
                        w_high_down(b + (r + 1), 0)
                        w_high_down(b + (r + 1), 1)
                    act.wait_ge(used, b * HD_DOWN + (Q_DOWN + (r + 1) * HD_DOWN))
                    rows_squares(y_fin, b + r, (B_DOWN + r) % 2)
                if not last:
                    for m in range(2, AHEAD):
                        w_high_down(b + 2, m)

            with act.Fori(0, N_DOWN // 2 - 1) as b2:
                down_pair(b2 * 2, False)
            down_pair(N_DOWN - 2, True)
            stat_root(4, "post2")

        @block.vector
        def _(dve):
            V = nc.vector
            chain, counts = [0], {}

            def link(ins):
                chain[0] += 1
                ins.then_inc(S_("dve_chain"), 1)
                dve.wait_ge(S_("dve_chain"), chain[0])

            def give(ins, name):
                counts[name] = counts.get(name, 0) + 1
                ins.then_inc(S_(name), 1)
                dve.wait_ge(S_(name), counts[name])

            def free_job(ins, n):
                ins.then_inc(job_free[n % 2], 1)
                dve.wait_ge(job_free[n % 2], n // 2 + 1)

            def w_low(q, k, n=512):
                dve.wait_ge(hi_ready, q + 1)
                V.tensor_tensor(w_lo[:, k % SLOTS, :, 0:n], raw[:, k // 2, 2 * (k % 2):2 * (k % 2) + 2, 0:n],
                                w_hi[:, k % SLOTS, :, 0:n].bitcast(F32), ALU.subtract).then_inc(lo_ready, 1)

            def w_low_down(b, m):
                dve.wait_ge(hi_ready, b * HD_DOWN + (Q_DOWN + m + 1))
                V.tensor_tensor(w_lo[:, m % SLOTS_D], raw_d[:, m % RAW_D],
                                w_hi[:, m % SLOTS_D].bitcast(F32), ALU.subtract).then_inc(lo_ready, 1)

            def bc(t, shape):
                return t.broadcast_to(shape)

            def mean_square(i, sums, name):
                give(V.tensor_scalar(stat[:, i], sums, 1.0 / D, RMS_EPS, ALU.mult, ALU.add), name + "_ms")

            def scale_rows(dst, src, i, name):
                dve.wait_ge(S_(name + "_inv"), 1)
                for c in range(4):
                    V.tensor_scalar(dst[:, 0, 512 * c:512 * c + 512], src[:, 0, 512 * c:512 * c + 512],
                                    stat[:, i, 0:1], None, ALU.mult).then_inc(S_(name + "_rows0"), 1)

            def fill(n, f, i):
                if i % 2:
                    if f == 0 and i == 1:
                        w_low(1, 1)
                    low_fill(f, i, fill_buf(f, i))
                    return
                p = job_wait_full(dve, n)
                if i >= 2:
                    dve.wait_ge(xl_ready, split_count(f, i - 2))
                for m in halves(i):
                    gain = colA[:, G_COL[f] + 4 * i + m.start:G_COL[f] + 4 * i + m.stop].unsqueeze(2)
                    last = V.tensor_tensor(fill_buf(f, i)[:, m], p[:].rearrange("p (f t) -> p f t", f=4)[:, m],
                                           bc(gain, [P, m.stop - m.start, SEQ]), ALU.mult)
                    if m.stop < 4:
                        last.then_inc(S_("half_filled"), 1)
                free_job(last, n)
                if f == 0 and i == 0:
                    w_low(0, 0)
                low_fill(f, i, fill_buf(f, i))

            def low_fill(f, i, src):
                for m in halves(i):
                    ks = slice(4 * i + m.start, 4 * i + m.stop)
                    dve.wait_ge(xh_ready, split_count(f, i, m))
                    V.tensor_tensor(x_lo[:, ks], src[:, m], x_hi[:, ks].bitcast(F32), ALU.subtract).then_inc(xl_ready, 1)

            def angles():
                c1, rest = 6.28125, 2 * math.pi - 6.28125
                c2 = math.floor(rest * 2.0 ** 17) / 2.0 ** 17
                c3 = math.floor((rest - c2) * 2.0 ** 26) / 2.0 ** 26
                c4 = rest - c2 - c3
                for i in range(8):
                    last = V.memset(ang[:, 5, 0, i:i + 1], INV_FREQ[i])
                link(last)
                for t in range(TT):
                    last = V.tensor_scalar(ang[:, 0, t], ang[:, 5, 0], colB[:, CB_POS + t:CB_POS + t + 1], None, ALU.mult)
                link(last)
                for m, turn, off in ((1, 0.25, math.pi / 2), (2, 0.0, 0.0)):
                    r, q = ang[:, m], ang[:, 2 + m]
                    link(V.tensor_scalar(q, ang[:, 0], 1 / (2 * math.pi), turn, ALU.mult, ALU.add))
                    link(V.tensor_scalar(q, q, 12582912.0, 12582912.0, ALU.add, ALU.subtract))
                    link(V.scalar_tensor_tensor(r, q, -c1, ang[:, 0], ALU.mult, ALU.add))
                    for c in (c2, c3, c4):
                        link(V.scalar_tensor_tensor(r, q, -c, r, ALU.mult, ALU.add))
                    link(V.tensor_scalar(r, r, off, 3.1415925, ALU.add, ALU.min))
                    ins = V.tensor_scalar(r, r, -3.1415925, None, ALU.max)
                    if m == 1:
                        link(ins)
                give(ins, "ang_ready")

            def rope_q_k():
                dve.wait_ge(evac_done, B_LORA)
                dve.wait_ge(S_("trig_ready"), 1)
                for j in range(TT):
                    t1, t2 = zq[:, j, 0:20, 0:8], zq[:, j, 0:20, 8:16]
                    cos, sin = (bc(trig[:, m, j].unsqueeze(1), [P, 20, 8]) for m in range(2))
                    for i, (x, y) in enumerate(((t1, cos), (t2, sin), (t2, cos), (t1, sin))):
                        last = V.tensor_tensor(rope[:, i], x, y, ALU.mult)
                    link(last)
                    V.tensor_tensor(t1, rope[:, 0], rope[:, 1], ALU.subtract)
                    link(V.tensor_tensor(t2, rope[:, 2], rope[:, 3], ALU.add))
                for j in range(TT):
                    last = V.tensor_copy(k_dup[:, j], bc(zq[:, j, 16:20].unsqueeze(2), [P, 4, 2, HD]))
                give(last, "kdup_ready")

            def swa(n, s):
                if s[0] == "swa_kT":
                    p = job_wait_full(dve, n)
                    free_job(V.tensor_copy(k_T[:].rearrange("p g t -> p (g t)"), p[:]), n)
                elif s[0] == "swa_qT":
                    p = job_wait_full(dve, n)
                    free_job(V.tensor_copy(q_T[:, s[1] % 2].rearrange("p f t -> p (f t)"), p[:, 0:512]), n)
                elif s[0] == "swa_scores":
                    g, j = s[1:]
                    consumed(dve, *s)
                    pr = prob[:, j]
                    if j == 0:
                        link(V.memset(prob[0:64, 0, :, 64:128], NEG_INF))
                    dve.wait_ge(S_("sink_loaded"), 16)
                    sk = sink[:, 4 * g:4 * g + 4].rearrange("p (f h) -> p h f", h=2)
                    s4 = [soft[:, i] for i in range(5)]
                    link(V.tensor_reduce(s4[0], pr, AX.X, ALU.max))
                    link(V.tensor_tensor(s4[0].rearrange("p (h f) -> p h f", h=2), s4[0].rearrange("p (h f) -> p h f", h=2), sk, ALU.max))
                    V.tensor_tensor(s4[1].rearrange("p (h f) -> p h f", h=2), sk, s4[0].rearrange("p (h f) -> p h f", h=2), ALU.subtract)
                    give(V.tensor_tensor(pr, pr, bc(s4[0].unsqueeze(2), [P, 4, P]), ALU.subtract), "s_shift")
                elif s[0] == "swa_norm":
                    g, j = s[1:]
                    pr = prob[:, j]
                    s4 = [soft[:, i] for i in range(5)]
                    dve.wait_ge(S_("s_exp"), 2 * (2 * g + j) + 2)
                    link(V.tensor_reduce(s4[3], pr, AX.X, ALU.add))
                    link(V.tensor_tensor(s4[3], s4[3], s4[2], ALU.add))
                    link(V.reciprocal(s4[3], s4[3]))
                    give(V.tensor_tensor(pr, pr, bc(s4[3].unsqueeze(2), [P, 4, P]), ALU.mult), "s_norm")
                elif s[0] == "swa_out":
                    g, j = s[1:]
                    p = job_wait_full(dve, n)
                    free_job(V.tensor_copy(y_T[:, 8 + 2 * g:10 + 2 * g, j * P:j * P + P],
                                           p[:, 0:256].rearrange("p (f t) -> p f t", f=2)), n)

            def shift(g):
                nf = 3 if g == B_LORA else 4
                f0 = 24 if g == B_LORA else 4 * (g - B_RKV)
                to = f0 if f0 < 8 else f0 + 8
                dst = lora[:] if g == B_LORA else feat[:, to:to + 4]
                dve.wait_ge(evac_done, g + 1)
                now, before = stage[:, g % 2, 0:nf, 1:SEQ + 1], stage[:, g % 2, 0:nf, 0:SEQ]
                link(V.tensor_tensor(dst, before, now, ALU.subtract))
                mu = bc(colB[:, CB_MU + f0:CB_MU + f0 + nf].unsqueeze(2), [P, nf, SEQ])
                link(V.tensor_tensor(dst, dst, mu, ALU.mult))
                give(V.tensor_tensor(dst, dst, now, ALU.add), "shifted")

            def heads(t):
                return t.rearrange("p f (c t) -> p f c t", c=NCH)

            def flat(t):
                return t.rearrange("p f t -> p (f t)")

            def rwkv(n, s):
                what, G = s[0], s[1]
                r, k, v = (feat[:, i + 2 * G:i + 2 * G + 2] for i in (0, 16, 24))
                col = lambda c, f: colA[:, c + 2 * G + f:c + 2 * G + f + 1]
                if what == "prep_kk":
                    if G == 0:
                        dve.wait_ge(S_("masks"), 1)
                    elif G >= 2:
                        dve.wait_ge(S_("yt_ready"), G - 1)
                    for f in range(2):
                        last = V.tensor_scalar(kk[:, f], k[:, f], col(C_KK, f), None, ALU.mult)
                    link(last)
                    give(V.tensor_tensor(inv_norm[:], kk[:], kk[:], ALU.mult), "kk_sq")
                elif what == "kk_norm":
                    p = job_wait_full(dve, n)
                    free_job(V.tensor_scalar(flat(inv_norm[:]), p[:, 0:512], 1e-24, None, ALU.max), n)
                elif what == "prep_decay":
                    if G == 0:
                        produced(dve, "swa_qT", 3)
                    consumed(dve, "lora_wa", G)
                    link(V.tensor_scalar(decay[:], decay[:], -DECAY_SCALE, None, ALU.mult))
                    for f in range(2):
                        last = V.tensor_tensor_scan(cum[:, f], reset[:], decay[:, f], 0.0, ALU.mult, ALU.add)
                    link(last)
                    give(V.tensor_tensor(decay[:], cum[:], decay[:], ALU.subtract), "cum_ready")
                elif what == "prep_k":
                    for f in range(2):
                        last = V.tensor_scalar(k_new[:, f], rate[:, f], -1.0, col(C_KA, f), ALU.add, ALU.mult)
                    link(last)
                    link(V.scalar_tensor_tensor(k_new[:], k_new[:], 1.0, k, ALU.add, ALU.mult))
                elif what == "prep_bonus":
                    for f in range(2):
                        last = V.scalar_tensor_tensor(bonus[G % 2][:, f], r[:, f], col(C_RK, f), k_new[:, f], ALU.mult, ALU.mult)
                    give(last, "bonus_ready")
                    dve.wait_ge(S_("kk_rt"), G + 1)
                    link(V.tensor_tensor(kk[:], kk[:], inv_norm[:], ALU.mult))
                    link(V.tensor_tensor(rate[:], rate[:], kk[:], ALU.mult))
                elif what == "prep_kr":
                    if G == 0:
                        consumed(dve, "swa_scores", 3, 1)
                    dve.wait_ge(S_("exp_ready"), 3 * G + 3)
                    V.tensor_tensor(kr[G % 2][:, :, :, 0], heads(kk[:]), heads(decay[:]), ALU.mult)
                    V.tensor_tensor(kr[G % 2][:, :, :, 1], heads(r), heads(cum[:]), ALU.mult)
                    link(V.tensor_copy(chunk_decay[:, G % 2], heads(cum[:])[:, :, :, CH - 1]))
                elif what == "prep_bk":
                    if G:
                        produced(dve, "bk_rows", G - 1)
                        produced(dve, "scores", G - 1, 1)
                        produced(dve, "lower", G - 1)
                    else:
                        consumed(dve, "swa_out", 3, 1)
                    for c in range(2):
                        cs = slice(c, NCH, 2)
                        V.tensor_tensor(bk[:, :, cs, b_part(c)], heads(rate[:])[:, :, cs], heads(exp_neg[:])[:, :, cs], ALU.mult)
                        last = V.tensor_tensor(bk[:, :, cs, 1 - b_part(c)], heads(k_new[:])[:, :, cs], heads(exp_neg[:])[:, :, cs], ALU.mult)
                    give(last, "kr_ready")
                elif what == "scores":
                    p = job_wait_full(dve, n)
                    mask = bc(mask_sc[:].rearrange("p m t -> p (m t)").unsqueeze(1), [P, 8, P])
                    free_job(V.tensor_tensor(mx[:, s[2]].rearrange("p h f c n -> p (h f c) n"),
                                             p[:].rearrange("p (i n) -> p i n", i=8), mask, ALU.mult), n)
                elif what == "lower":
                    p = job_wait_full(dve, n)
                    mask = bc(mask_low[:].unsqueeze(1).unsqueeze(1), [P, 2, 2, CH])
                    for hh in range(2):
                        last = V.tensor_tensor(low[:, :, hh], p[:, 512 * hh:512 * hh + 256].rearrange("p (c f s) -> p c f s", c=2, f=2), mask, ALU.mult)
                    free_job(last, n)
                if what == "scores" and s[2] == 1:
                    for c in range(2):
                        h = half(c)
                        last = V.tensor_tensor(inv_x[h].rearrange("p a b c d -> p (a b c) d"),
                                        mx[h].rearrange("p a b f c n -> p (a b f) c n")[:, :, c, 0:CH],
                                        bc(lvl_x[h, 0].unsqueeze(1), [64, 8, CH]), ALU.mult)
                    link(last)
                    tv = inv_x[:].rearrange("p a b c d -> p (a b c) d")
                    give(V.tensor_tensor(tv, tv, bc(eye[:].unsqueeze(1), [P, 8, CH]), ALU.add), "inv_ready")
                elif what in ("inv_x", "inv_t"):
                    p = job_wait_full(dve, n)
                    i = s[2].bit_length() - 1
                    dst, m = (inv_x, lvl_x) if what == "inv_x" else (inv_t, lvl_t)
                    free_job(V.copy_predicated(dst[:].rearrange("p a b c d -> p (a b c) d"),
                                               bc(m[:, i].bitcast(I32).unsqueeze(1), [P, 8, CH]),
                                               p[:, 0:512].rearrange("p (i n) -> p i n", i=8)), n)
                elif what == "scan_ys":
                    p = job_wait_full(dve, n)
                    c = s[2]
                    if c < NCH - 1:
                        ps = p[:, 512:640].rearrange("p (f d) -> p f d", f=2)
                        fade = bc(chunk_decay[:, G % 2, :, c:c + 1], [P, 2, HD])
                        if c:
                            link(V.tensor_tensor(state[:], ps, state[:], ALU.add))
                            give(V.tensor_tensor(state[:], state[:], fade, ALU.mult), "state_ready")
                        else:
                            give(V.tensor_tensor(state[:], ps, fade, ALU.mult), "state_ready")
                    if c == 0 and G:
                        dve.wait_ge(S_("yt_ready"), G)
                    free_job(V.tensor_copy(y_grp[:, :, CH * c:CH * c + CH], p[:, 0:128].rearrange("p (f t) -> p f t", f=2)), n)
                elif what == "gn_mean":
                    p = job_wait_full(dve, n)
                    V.scalar_tensor_tensor(flat(y_grp[:]), p[:, 0:512], -1.0 / HD, flat(y_grp[:]), ALU.mult, ALU.add)
                    free_job(V.tensor_tensor(flat(bonus_v[:]), p[:, 512:1024], flat(v), ALU.mult), n)
                    give(V.tensor_tensor(y_sq[:], y_grp[:], y_grp[:], ALU.mult), "gn_sq")
                elif what == "gn_var":
                    p = job_wait_full(dve, n)
                    free_job(V.tensor_scalar(flat(rstd[:]), p[:, 0:512], 1.0 / HD, GN_EPS, ALU.mult, ALU.add), n)
                elif what == "gn_out":
                    if G == 3:
                        norm_out(dve, V, G)

            def cross(n, s):
                h = s[1]
                if s[0] == "x_scores":
                    p = job_wait_full(dve, n)
                    link(V.tensor_reduce(stat[:, 5], p[:, 0:512].rearrange("p (t m) -> p t m", t=TT), AX.X, ALU.max))
                    give(V.tensor_tensor(stat[:, 6], stat[:, 5], stat[:, 1], ALU.mult), "x_max")
                    consumed(dve, *s)
                    link(V.reciprocal(stat[:, 7], stat[:, 7]))
                    for j in range(TT):
                        last = V.tensor_scalar(xp[:, h % 2, j], xp[:, h % 2, j], stat[:, 7, j:j + 1], None, ALU.mult)
                    give(last, "x_norm")

            def lead(g, k):
                g2, k2 = (g, k + 3) if k + 3 < HU else (g + 1, k + 3 - HU)
                w_low(g2 * HU + k2, k2, 288 if g2 == B_LORA else 512)

            def walk(steps):
                for n, *s in steps:
                    if s[0] == "gain":
                        p = job_wait_full(dve, n)
                        free_job(V.tensor_copy(colA[:, 0:KT], p[:, 0:KT]), n)
                    elif s[0] == "params":
                        dve.wait_ge(S_("pos_loaded"), 16)
                        give(V.tensor_copy(pack[96:98, 1], pos_i[96:98]), "pos_float")
                        p = job_wait_full(dve, n)
                        V.tensor_copy(colA[:, KT:P], p[:, KT:P])
                        for i, t in ((1, colB), (2, colC)):
                            last = V.tensor_copy(t[:], p[:, P * i:P * i + P])
                        free_job(last, n)
                    elif s[0] == "hu":
                        g, k = s[1:]
                        lead(g, k)
                        if k == HU - 1 and B_LORA <= g < B_WK:
                            shift(g)
                        if k == HU - 1 and B_WO <= g < B_UP:
                            rows_out(y_rows, g - B_WO, g % 2, 1, g_post)
                    elif s[0] == "mem_sq":
                        pass
                    elif s[0] == "mem_scale":
                        dve.wait_ge(S_("mem_ssq"), TT)
                        mean_square(1, ssq[:, :, 1], "mem")
                        scale_rows(rows0, rows0, 1, "mem")
                    elif s[0] == "angles":
                        dve.wait_ge(xh_ready, split_count(0, 3))
                        V.memset(v_win[64:128, 0], 0.0).then_inc(S_("vwin_zero"), 1)
                        angles()
                        dve.wait_ge(S_("trig_ready"), 1)
                        V.memset(stage[:, :, :, 0:1], 0.0).then_inc(S_("stage_zero"), 1)
                    elif s[0] == "fill":
                        fill(n, *s[1:])
                        if tuple(s[1:]) == (0, 1):
                            w_low(2, 2)
                    elif s[0] == "fill_T":
                        f, i = s[1:]
                        low_fill(f, i, y_T[:, 4 * i:4 * i + 4])
                    elif s[0] == "rope":
                        rope_q_k()
                    elif s[0] == "residual":
                        residual(s[1], s[2], y_rows, x_res)
                    elif s[0] == "pre_stat":
                        pre_stat(s[1])
                    elif s[0] in ("res_squares", "rstd_T"):
                        pass
                    elif s[0].startswith("swa"):
                        swa(n, s)
                    elif s[0].startswith("x_"):
                        cross(n, s)
                    else:
                        rwkv(n, s)

            def rows_out(dst, b, par, i, g):
                dve.wait_ge(S_("gpost_loaded"), 16 * (i + 1))
                for j in range(TT):
                    dve.wait_ge(S_("squared"), b * 2 + (8 * i + j + 1))
                    last = V.tensor_tensor(dst[:, j, bass.ds(b * 512, 512)], acc[par][:, j * 512:j * 512 + 512],
                                           g[:, bass.ds(b * 512, 512)], ALU.mult)
                last.then_inc(evac_done, 1)

            def post_stat(i, last_block):
                dve.wait_ge(S_("squared"), 8 * (i + 1))
                link(V.tensor_reduce(stat[:, 7], ssq[:], AX.X, ALU.add))
                mean_square(2 + i, stat[:, 7], f"post{i}")
                if i == 2:
                    rows_out(y_fin, N_DOWN - 1, (B_DOWN + N_DOWN - 1) % 2, 2, g_fin)
                dve.wait_ge(evac_done, last_block)
                dve.wait_ge(S_(f"post{i}_inv"), 1)
                dve.wait_ge(S_("x2_loaded" if i == 2 else "xres_loaded"), 16)

            def residual(i, c, y, x):
                cs = slice(512 * c, 512 * c + 512)
                for j in range(TT):
                    V.scalar_tensor_tensor(x[:, j, cs], y[:, j, cs], stat[:, 2 + i, j:j + 1], x[:, j, cs],
                                           ALU.mult, ALU.add).then_inc(S_("result" if i == 2 else "xres_ready"), 1)

            def pre_stat(i):
                dve.wait_ge(S_("res_squared"), 8 * (i + 1))
                link(V.tensor_reduce(stat[:, 7], ssq[:], AX.X, ALU.add))
                mean_square(5, stat[:, 7], f"pre{i}")
                dve.wait_ge(S_(f"pre{i}_inv"), 1)
                if i == 0:
                    V.tensor_scalar(stat[:, 0], stat[:, 5], XHD ** -0.5, None, ALU.mult)
                    link(V.tensor_scalar(stat[:, 1], stat[:, 5], -XHD ** -0.5, None, ALU.mult))
                else:
                    V.memset(ones[:], 1.0)
                    for j in range(TT):
                        last = V.tensor_scalar(rstd_diag[:, j], ident[:], stat[:, 5, j:j + 1], None, ALU.mult)
                    give(last, "diag_ready")

            def loop_rows(g0, i, first):
                with dve.Fori(first, 2) as b2:
                    for r in range(2):
                        for k in range(HU):
                            w_low(b2 * (2 * HU) + ((g0 + r) * HU + k + 3), (k + 3) % HU)
                        rows_out(y_rows, b2 * 2 + r, (g0 + r) % 2, i, g_post)

            dve.wait_ge(S_("x_ssq"), TT)
            mean_square(0, ssq[:, :, 0], "x")
            scale_rows(rows0, rows0, 0, "x")
            walk(mix_steps)
            loop_rows(B_OUT, 0, 0)
            post_stat(0, B_WQ)
            walk(cross_steps)
            loop_rows(B_WO, 1, 1)
            post_stat(1, B_UP)
            walk(ffn_steps)
            dve.wait_ge(xh_ready, split_count(5, 3))
            give(V.memset(gate[:, :, :, 0:2], 0.0), "gate_zero")
            consumed(dve, "rstd_T")
            rstd2 = bc(rstd_T[:].unsqueeze(1), [P, 2, SEQ])

            def conv_block(i, r):
                dve.wait_ge(used, i * HU + (B_UP + 1) * HU)
                V.tensor_tensor(gate[:, r, :, 2:SEQ + 2], acc[(B_UP + r) % 2][:, 0:512].rearrange("p (f t) -> p f t", f=2),
                                rstd2, ALU.mult).then_inc(S_("gate_ready"), 1)
                dve.wait_ge(S_("gate_ready"), i + 1)
                for f in range(2):
                    last = V.tensor_scalar(conv[:, r, f], gate[:, r, f, 0:SEQ], colC[:, bass.ds(i * 2 + f, 1)],
                                           colB[:, bass.ds(i * 2 + (CB_CB + f), 1)], ALU.mult, ALU.add)
                last.then_inc(S_("conv_part"), 1)
                dve.wait_ge(S_("conv_part"), i * 2 + 1)
                for f in range(2):
                    last = V.scalar_tensor_tensor(conv[:, r, f], gate[:, r, f, 1:SEQ + 1], colC[:, bass.ds(i * 2 + (FT_FF + f), 1)],
                                                  conv[:, r, f], ALU.mult, ALU.add)
                last.then_inc(S_("conv_part"), 1)
                dve.wait_ge(S_("conv_part"), i * 2 + 2)
                for f in range(2):
                    last = V.scalar_tensor_tensor(conv[:, r, f], gate[:, r, f, 2:SEQ + 2], colC[:, bass.ds(i * 2 + (2 * FT_FF + f), 1)],
                                                  conv[:, r, f], ALU.mult, ALU.add)
                last.then_inc(S_("conv_ready"), 1)

            def mult_block(i, r):
                dve.wait_ge(S_("gelu_ready"), i + 1)
                V.tensor_tensor(act32[:, r], gelu[:, r], acc[(B_UP + r) % 2][:, 512:1024].rearrange("p (f t) -> p f t", f=2),
                                ALU.mult).then_inc(evac_done, 1)
                dve.wait_ge(evac_done, i + (B_UP + 1))
                V.tensor_tensor(act32[:, r], act32[:, r], rstd2, ALU.mult).then_inc(S_("act_ready"), 1)

            def low_block(i, r):
                dve.wait_ge(S_("acth_ready"), i + 1)
                V.tensor_tensor(act_lo[:, bass.ds(i * 2, 2)], act32[:, r], act_hi[:, bass.ds(i * 2, 2)].bitcast(F32),
                                ALU.subtract).then_inc(S_("actl_ready"), 1)

            def up_step(i, r, last):
                for k in range(HU):
                    if k == 0:
                        conv_block(i - 1, 1 - r)
                    if k == 3:
                        mult_block(i - 1, 1 - r)
                    if k == 6:
                        low_block(i - 1, 1 - r)
                    if not (last and k + 3 >= HU):
                        w_low(i * HU + (B_UP * HU + k + 3), (k + 3) % HU)

            up_step(1, 1, False)
            with dve.Fori(1, (N_UP - 1) // 2) as i2:
                up_step(i2 * 2, 0, False)
                up_step(i2 * 2 + 1, 1, False)
            up_step(N_UP - 1, 0, True)
            w_low_down(0, 0)
            w_low_down(0, 1)
            conv_block(N_UP - 1, 0)
            w_low_down(0, 2)
            w_low_down(0, 3)
            mult_block(N_UP - 1, 0)
            w_low_down(0, 4)
            low_block(N_UP - 1, 0)
            w_low_down(0, 5)

            def down_pair(b, last):
                for r in range(2):
                    for m in range(2 if r else AHEAD, HD_DOWN):
                        w_low_down(b + r, m)
                    if not (last and r):
                        w_low_down(b + (r + 1), 0)
                        w_low_down(b + (r + 1), 1)
                    if not (last and r):
                        rows_out(y_fin, b + r, (B_DOWN + r) % 2, 2, g_fin)
                if not last:
                    for m in range(2, AHEAD):
                        w_low_down(b + 2, m)

            with dve.Fori(0, N_DOWN // 2 - 1) as b2:
                down_pair(b2 * 2, False)
            down_pair(N_DOWN - 2, True)
            post_stat(2, B_DOWN + N_DOWN)
            for c in range(4):
                residual(2, c, y_fin, x_fin)

        @block.tensor
        def _(pe):
            T = nc.tensor

            def products(g, par, k, kind, f, n=512):
                q = g * HU + k
                if k == 0 and not (isinstance(g, int) and g < 2):
                    pe.wait_ge(evac_done, g - 1)
                if f is not None and (k < 2 or k % 2 == 0):
                    pe.wait_ge(xl_ready, split_count(f, k // 2, slice(0, 2) if k == 0 else None))
                pe.wait_ge(lo_ready, q + 1)
                sl_ = k % SLOTS
                for kt in range(2):
                    x = 2 * k + kt
                    first, final = x == 0, x == KT - 1
                    if kind == ROWS:
                        for t in range(TT):
                            o = acc[par][:, 512 * t:512 * t + 512]
                            xs_ = slice(P * t, P * t + P)
                            T.matmul(o, x_hi[:, x, xs_], w_hi[:, sl_, kt], start=first, stop=False)
                            T.matmul(o, x_hi[:, x, xs_], w_lo[:, sl_, kt], start=False, stop=False)
                            last = T.matmul(o, x_lo[:, x, xs_], w_hi[:, sl_, kt], start=False, stop=final)
                    else:
                        for c in range(n // P + (n % P > 0)):
                            o = acc[par][:, SEQ * c:SEQ * c + SEQ]
                            cs = slice(P * c, P * c + P)
                            T.matmul(o, w_hi[:, sl_, kt, cs], x_hi[:, x], start=first and c % 2 == 0, stop=False, skip_group_check=True)
                            T.matmul(o, w_hi[:, sl_, kt, cs], x_lo[:, x], start=False, stop=False, skip_group_check=True)
                            last = T.matmul(o, w_lo[:, sl_, kt, cs], x_hi[:, x], start=False, stop=final, skip_group_check=True)
                last.then_inc(used, 1)

            def begin(n):
                if n >= 2:
                    pe.wait_ge(job_free[n % 2], n // 2)
                return js[n % 2]

            def end(ins, n):
                ins.then_inc(job_full[n % 2], 1)

            def mm(o, l, r, start=True, stop=True):
                return T.matmul(o, l, r, start=start, stop=stop, skip_group_check=True)

            ROWS_OF = {0: (rows0, "x"), 1: (rows0, "mem"), 3: (x_res, None), 5: (x_res, None)}

            def fill(n, f, i):
                p = begin(n)
                rows, name = ROWS_OF[f]
                if name:
                    pe.wait_ge(S_(name + "_rows0"), i + 1)
                    pe.wait_ge(S_(name + "_rows1"), i + 1)
                else:
                    pe.wait_ge(S_("xres_ready"), 4 * (f - 3) + 2 * i + 2)
                for c in range(4):
                    for t in range(TT):
                        last = T.transpose(p[:, SEQ * c + P * t:SEQ * c + P * t + P],
                                           rows[:, t, P * (4 * i + c):P * (4 * i + c) + P], ident[:])
                end(last, n)

            def swa(n, s):
                p = begin(n)
                if s[0] == "swa_kT":
                    pe.wait_ge(S_("kdup_ready"), 1)
                    for g in range(4):
                        for t in range(TT):
                            last = T.transpose(p[:, SEQ * g + P * t:SEQ * g + P * t + P],
                                               k_dup[:, t, g].rearrange("p a d -> p (a d)"), ident[:])
                elif s[0] == "swa_qT":
                    g = s[1]
                    for f in range(2):
                        for t in range(TT):
                            last = T.transpose(p[:, SEQ * f + P * t:SEQ * f + P * t + P],
                                               zq[:, t, 4 * g + 2 * f:4 * g + 2 * f + 2].rearrange("p a d -> p (a d)"), ident[:])
                elif s[0] == "swa_scores":
                    g, j = s[1:]
                    consumed(pe, "swa_qT", g)
                    consumed(pe, "swa_kT")
                    for f in range(2):
                        for par in range(2):
                            c = 2 * j + par
                            for hh in range(2):
                                h = slice(64 * hh, 64 * hh + 64)
                                for piece in range(2):
                                    own = piece == par
                                    kc = c if own else max(c - 1, 0)
                                    last = mm(p[64 * par:64 * par + 64, 512 * hh + P * f + CH * piece:512 * hh + P * f + CH * piece + CH],
                                              q_T[h, g % 2, f, CH * c:CH * c + CH], k_T[h, g, CH * kc:CH * kc + CH])
                elif s[0] == "swa_pT":
                    g, j = s[1:]
                    pe.wait_ge(S_("s_norm"), 2 * g + j + 1)
                    for i in range(4):
                        last = T.transpose(p[:, P * i:P * i + P], prob[:, j, i], ident[:])
                else:
                    g, j = s[1:]
                    consumed(pe, "swa_pT", g, j)
                    for f in range(2):
                        for par in range(2):
                            for hh in range(2):
                                last = mm(p[64 * hh:64 * hh + 64, P * f + CH * par:P * f + CH * par + CH],
                                          v_win[:, 2 * j + par, g], prob_T[:, j, 2 * hh + f, CH * par:CH * par + CH])
                end(last, n)

            def rwkv(n, s):
                what, G = s[0], s[1]
                p = begin(n)
                hs = [slice(0, 64), slice(64, 128)]
                if what == "lora_wa":
                    pe.wait_ge(S_("lora_act"), 3)
                    pe.wait_ge(S_("wa_loaded"), 32 * (G + 1))
                    for f in range(2):
                        for i in range(2):
                            last = mm(p[:, 512 * i + SEQ * f:512 * i + SEQ * f + SEQ], lora_w[hs[i], 0, P * f:P * f + P], lora[hs[i], 0])
                elif what == "lora_g":
                    pe.wait_ge(S_("g_loaded"), 32 * (G + 1))
                    for f in range(2):
                        o = p[:, SEQ * f:SEQ * f + SEQ]
                        mm(o, lora_w[:, 1, P * f:P * f + P], lora[:, 1], True, False)
                        last = mm(o, lora_w[0:32, 2, P * f:P * f + P], lora[0:32, 2], False, True)
                elif what == "kk_norm":
                    pe.wait_ge(S_("kk_sq"), G + 1)
                    last = mm(p[:, 0:512], hones[:], inv_norm[:].rearrange("p f t -> p (f t)"))
                elif what == "v_rows":
                    for t in range(TT):
                        for f in range(2):
                            last = T.transpose(p[:, SEQ * t + P * f:SEQ * t + P * f + P], feat[:, 24 + 2 * G + f, P * t:P * t + P], ident[:])
                elif what == "bk_rows":
                    pe.wait_ge(S_("kr_ready"), G + 1)
                    for f in range(2):
                        for c in range(NCH):
                            last = T.transpose(p[:, 512 * f + P * c:512 * f + P * c + P], bk[:, f, c].rearrange("p a s -> p (a s)"), ident[:])
                elif what == "scores":
                    for f in range(2):
                        for cc in range(2):
                            c = 2 * s[2] + cc
                            for hh in range(2):
                                at_ = 512 * hh + 256 * f + P * cc
                                last = mm(p[:, at_:at_ + P], bk[hs[hh], f, c].rearrange("p a s -> p (a s)"),
                                          kr[G % 2][hs[hh], f, c].rearrange("p a s -> p (a s)"))
                elif what == "lower":
                    for c in range(NCH):
                        for f in range(2):
                            for hh in range(2):
                                at_ = 512 * hh + P * (c // 2) + CH * f
                                last = mm(p[half(c), at_:at_ + CH], kr[G % 2][hs[hh], f, c, 0], bk[hs[hh], f, c, b_part(c)])
                elif what in ("inv_p", "inv_x", "inv_t"):
                    b = s[2]
                    if what == "inv_p":
                        if b == LEVELS[0]:
                            pe.wait_ge(S_("inv_ready"), G + 1)
                        else:
                            consumed(pe, "inv_x", G, b // 2)
                        left, right = low, inv_x
                    elif what == "inv_x":
                        consumed(pe, "inv_p", G, b)
                        if b != LEVELS[0]:
                            consumed(pe, "inv_t", G, b // 2)
                        else:
                            pe.wait_ge(S_("inv_t_ready"), G + 1)
                        left, right = inv_t, inv_p
                    else:
                        left, right = inv_p, inv_t
                    for i in range(8):
                        ix = (i // 4, i // 2 % 2, i % 2)
                        for q in range(2):
                            at_ = CH * i
                            last = mm(p[hs[q], at_:at_ + CH], left[hs[q], ix[0], ix[1], ix[2]], right[hs[q], ix[0], ix[1], ix[2]])
                elif what in ("scan_x", "scan_u", "scan_ys"):
                    c = s[2]
                    h = half(c)
                    if what == "scan_x":
                        if c:
                            pe.wait_ge(S_("state_ready"), 3 * G + c)
                        else:
                            consumed(pe, "v_rows", G)
                            consumed(pe, "bk_rows", G)
                            consumed(pe, "scores", G, 1)
                            pe.wait_ge(S_("uv_zero"), 2 * (G + 1))
                        consumed(pe, "inv_x", G, LEVELS[-1])
                    elif what == "scan_u":
                        consumed(pe, "scan_x", G, c)
                    elif c:
                        for i in range(4):
                            f, hh = i // 2, i % 2
                            mm(p[hs[hh], CH * f:CH * f + CH], state[hs[hh], f], kr[G % 2][hs[hh], f, c, 1], f == 0, False)
                    if what == "scan_ys":
                        consumed(pe, "scan_u", G, c)
                    for f in range(2):
                        for hh in range(2):
                            i = 2 * f + hh
                            m = mx[:, c // 2, hh, f, c % 2]
                            if what == "scan_x":
                                o = p[h, 512 * hh + CH * f:512 * hh + CH * f + CH]
                                last = mm(o, m[:, 0:CH], uv[:, c, i], True, c == 0)
                                if c:
                                    last = mm(o, kr[G % 2][hs[hh], f, c, 0], state[hs[hh], f], False, True)
                            elif what == "scan_u":
                                last = mm(p[h, CH * i:CH * i + CH], inv_x[h, c // 2, hh, f], xs[h, i])
                            else:
                                o = p[hs[hh], CH * f:CH * f + CH]
                                mm(o, uv[:, c, i], m[:, CH:2 * CH], c == 0, True)
                                last = mm(p[hs[hh], 512 + CH * f:512 + CH * f + CH], bk_rows[:, f, c, 64 * hh:64 * hh + 64], uv[:, c, i])
                elif what == "gn_mean":
                    consumed(pe, "scan_ys", G, NCH - 1)
                    pe.wait_ge(S_("bonus_ready"), G + 1)
                    mm(p[:, 0:512], hones[:], y_grp[:].rearrange("p f t -> p (f t)"))
                    last = mm(p[:, 512:1024], hones[:], bonus[G % 2][:].rearrange("p f t -> p (f t)"))
                else:
                    pe.wait_ge(S_("gn_sq"), G + 1)
                    last = mm(p[:, 0:512], hones[:], y_sq[:].rearrange("p f t -> p (f t)"))
                end(last, n)

            def cross(n, s):
                p = begin(n)
                h = s[1]
                if s[0] == "x_scores":
                    pe.wait_ge(evac_done, B_WQ + h + 1)
                    pe.wait_ge(S_("kv_loaded"), 16 * 8)
                    for j in range(TT):
                        for c in range(4):
                            last = mm(p[:, MEM * j:MEM * j + MEM], y_T[:, 4 * h + c, P * j:P * j + P], kx[:, 4 * h + c], c == 0, c == 3)
                elif s[0] == "x_pT":
                    pe.wait_ge(S_("x_norm"), h + 1)
                    for m in range(2):
                        for j in range(TT):
                            last = T.transpose(p[:, SEQ * m + P * j:SEQ * m + P * j + P], xp[:, h % 2, j, P * m:P * m + P], ident[:])
                else:
                    consumed(pe, "x_pT", h)
                    for c in range(4):
                        for m in range(2):
                            last = mm(p[:, SEQ * c:SEQ * c + SEQ], vx[:, m, h, P * c:P * c + P], xp_T[:, h % 2, m], m == 0, m == 1)
                end(last, n)

            def walk(steps):
                for n, *s in steps:
                    if s[0] == "gain":
                        p = begin(n)
                        pe.wait_ge(S_("ident_ready"), 1)
                        pe.wait_ge(S_("gain_loaded"), 16)
                        end(T.transpose(p[:, 0:KT], pack[0:KT, 0], ident[0:KT, 0:KT]), n)
                    elif s[0] == "params":
                        p = begin(n)
                        pe.wait_ge(S_("pos_float"), 1)
                        pe.wait_ge(S_("pack_loaded"), N_PACK * 16)
                        for i in range(3):
                            last = T.transpose(p[:, P * i:P * i + P], pack[:, i], ident[:])
                        end(last, n)
                    elif s[0] == "hu":
                        g, k = s[1:]
                        products(g, g % 2, k, kind_of(g), FIRST_OF_FILL.get(g), 288 if g == B_LORA else 512)
                    elif s[0] == "fill":
                        fill(n, *s[1:])
                    elif n is None:
                        pass
                    elif s[0] == "rstd_T":
                        p = begin(n)
                        pe.wait_ge(S_("diag_ready"), 1)
                        for j in range(TT):
                            last = mm(p[:, P * j:P * j + P], ones[:], rstd_diag[:, j])
                        end(last, n)
                    elif s[0].startswith("swa"):
                        swa(n, s)
                    elif s[0].startswith("x_"):
                        cross(n, s)
                    else:
                        rwkv(n, s)

            def loop_rows(g0, f, first):
                with pe.Fori(first, 2) as b2:
                    for r in range(2):
                        for k in range(HU):
                            products(b2 * 2 + (g0 + r), (g0 + r) % 2, k, ROWS, f)

            walk(mix_steps)
            loop_rows(B_OUT, 2, 0)
            walk(cross_steps)
            loop_rows(B_WO, None, 1)
            walk(ffn_steps)
            with pe.Fori(0, (N_UP - 1) // 2) as i2:
                for r in range(2):
                    for k in range(HU):
                        products(i2 * 2 + (B_UP + 1 + r), (B_UP + 1 + r) % 2, k, COLS, None)
            with pe.Fori(0, N_DOWN // 2) as b2:
                for r in range(2):
                    par = (B_DOWN + r) % 2
                    pe.wait_ge(evac_done, b2 * 2 + (B_DOWN + r - 1))
                    for m in range(HD_DOWN):
                        pe.wait_ge(S_("actl_ready"), m + 1)
                        pe.wait_ge(lo_ready, b2 * (2 * HD_DOWN) + (Q_DOWN + r * HD_DOWN + m + 1))
                        for kt in range(2):
                            x = 2 * m + kt
                            for t in range(TT):
                                o = acc[par][:, 512 * t:512 * t + 512]
                                ts_ = slice(P * t, P * t + P)
                                T.matmul(o, act_hi[:, x, ts_], w_hi[:, m % SLOTS_D, kt], start=x == 0, stop=False)
                                T.matmul(o, act_hi[:, x, ts_], w_lo[:, m % SLOTS_D, kt], start=False, stop=False)
                                last = T.matmul(o, act_lo[:, x, ts_], w_hi[:, m % SLOTS_D, kt], start=False, stop=x == FT_FF - 1)
                        last.then_inc(used, 1)


_INS = ["x", "mem", "positions", "norm_mix_pre", "norm_mix_post", "w_in", "shift_mu", "w0", "w_lora_up", "a0",
        "a_lora_up", "g_lora_up", "k_k", "k_a", "r_k", "ln_x_w", "ln_x_b", "attn_sinks", "w_out", "norm_cross_pre",
        "norm_cross_post", "mem_norm", "wq_x", "wk_x", "wv_x", "wo_x", "norm_ffn_pre", "norm_ffn_post", "w_up",
        "conv_w", "conv_b", "w_down"]


def kernel(**inputs):
    import numpy as _np
    import concourse.bacc as _bacc
    from concourse import mybir as _mybir
    from concourse.bass_utils import run_bass_kernel_spmd as _run

    nc = _bacc.Bacc("TRN2", target_bir_lowering=False, num_devices=1)
    arrays, args = {}, {}
    for name in _INS:
        v = _np.ascontiguousarray(inputs[name])
        arrays[f"in_{name}_dram"] = v
        args[name] = nc.dram_tensor(f"in_{name}_dram", v.shape, _mybir.dt.from_np(v.dtype), kind="ExternalInput").ap()
    out = nc.dram_tensor("out_0_dram", (1, SEQ, D), _mybir.dt.float32, kind="ExternalOutput").ap()
    build(nc, args, out)
    r = _run(nc, [arrays], core_ids=[0])
    return r.results[0]["out_0_dram"]
```
